# Optimizing a Trainium2 kernel written in Bass

```python
import math
import jax
import jax.numpy as jnp
from jax import lax
import numpy as np

D_MODEL = 1024
BATCH = 1
SEQ = 256
DEPTH = 2
DEC_BATCH = 8
DEC_SEQ = 1
PAST_LEN = 2048
PAGE_SIZE = 128

RWKV_HEADS = 8
RWKV_HEAD_DIM = 64
RWKV_WIDTH = RWKV_HEADS * RWKV_HEAD_DIM
DECAY_LORA = 64
ICLR_LORA = 64
GATE_LORA = 128
GN_EPS = 64e-5
MLA_HEADS = 8
QK_NOPE_DIM = 64
QK_ROPE_DIM = 32
V_HEAD_DIM = 64
MLA_WIDTH = MLA_HEADS * V_HEAD_DIM
Q_LORA = 256
KV_LORA = 128
ROPE_THETA = 10000.0
MLA_SCALE = (QK_NOPE_DIM + QK_ROPE_DIM) ** -0.5
Q_BLOCK = 128
RWKV_PROJ = 3 * RWKV_WIDTH + DECAY_LORA + ICLR_LORA + GATE_LORA
MLA_PROJ = Q_LORA + KV_LORA + QK_ROPE_DIM
IN_PROJ = RWKV_PROJ + MLA_PROJ
MIX_WIDTH = RWKV_WIDTH + MLA_WIDTH
N_MEM = 256
MEM_HEADS = 4
MEM_HEAD_DIM = D_MODEL // MEM_HEADS
D_FF = 2816
RMS_EPS = 1e-6

kernel_name = 'hymba_rwkv7_mla_macaron_step'

def rmsnorm(x, g):
    xf = x.astype(jnp.float32)
    y = xf * lax.rsqrt(jnp.mean(xf * xf, axis=-1, keepdims=True) + RMS_EPS)
    return (y * g.astype(jnp.float32)).astype(x.dtype)

def swiglu_ffn(h, w_gate, w_up, w_down):
    return (jax.nn.silu(h @ w_gate) * (h @ w_up)) @ w_down

def rope(x, pos):
    half = QK_ROPE_DIM // 2
    inv_freq = ROPE_THETA ** (-jnp.arange(half, dtype=jnp.float32) / half)
    ang = pos.astype(jnp.float32)[:, None] * inv_freq[None, :]
    ang = ang.reshape((ang.shape[0],) + (1,) * (x.ndim - 3) + (half,))
    cos, sin = jnp.cos(ang), jnp.sin(ang)
    xf = x.astype(jnp.float32)
    x1, x2 = xf[..., :half], xf[..., half:]
    return jnp.concatenate([x1 * cos - x2 * sin, x1 * sin + x2 * cos], axis=-1).astype(x.dtype)

def token_shift(p, prev, mu):
    p_prev = jnp.concatenate([prev[:, None, :].astype(p.dtype), p[:, :-1]], axis=1)
    return p + (p_prev - p) * mu, p[:, -1]

def rwkv7_mix(p, s0, w0, w_up, a0, a_up, g_up, k_k, k_a, r_k, gn_w, gn_b):
    B, T, _ = p.shape
    H, N, W = RWKV_HEADS, RWKV_HEAD_DIM, RWKV_WIDTH
    o1 = 3 * W
    r = p[..., :W]
    k = p[..., W:2 * W]
    v = p[..., 2 * W:o1]
    wd = p[..., o1:o1 + DECAY_LORA]
    ad = p[..., o1 + DECAY_LORA:o1 + DECAY_LORA + ICLR_LORA]
    gd = p[..., o1 + DECAY_LORA + ICLR_LORA:]
    w_log = -jax.nn.softplus(-(w0 + jnp.tanh(wd) @ w_up)) - 0.5
    decay = jnp.exp(-jnp.exp(w_log.astype(jnp.float32)))
    a = jax.nn.sigmoid(a0 + ad @ a_up)
    g = jax.nn.sigmoid(gd) @ g_up
    heads = lambda t: t.astype(jnp.float32).reshape(B, T, H, N)
    kk = heads(k * k_k)
    kk = kk / jnp.maximum(jnp.linalg.norm(kk, axis=-1, keepdims=True), 1e-12)
    k = k * (1.0 + (a - 1.0) * k_a)
    r_h, k_h, v_h, a_h, w_h = heads(r), heads(k), heads(v), heads(a), heads(decay)
    b_h = kk * a_h

    def step(S, inp):
        r_t, w_t, k_t, v_t, kk_t, b_t = inp
        S_kk = jnp.einsum('bhvk,bhk->bhv', S, kk_t)
        S = S * w_t[:, :, None, :] - S_kk[..., None] * b_t[:, :, None, :] + v_t[..., None] * k_t[:, :, None, :]
        return S, jnp.einsum('bhvk,bhk->bhv', S, r_t)

    seq_first = lambda t: jnp.swapaxes(t, 0, 1)
    xs = (seq_first(r_h), seq_first(w_h), seq_first(k_h), seq_first(v_h), seq_first(kk), seq_first(b_h))
    s_last, o = lax.scan(step, s0.astype(jnp.float32), xs)
    o = seq_first(o)
    mean = jnp.mean(o, axis=-1, keepdims=True)
    var = jnp.mean(jnp.square(o - mean), axis=-1, keepdims=True)
    o = ((o - mean) * lax.rsqrt(var + GN_EPS)).reshape(B, T, W) * gn_w + gn_b
    bonus = jnp.sum(r_h * k_h * r_k, axis=-1, keepdims=True) * v_h
    out = (o + bonus.reshape(B, T, W)) * g
    return out.astype(p.dtype), s_last.astype(s0.dtype)

def mla_project(pm, pos, q_norm, w_uq, kv_norm, w_uk):
    B, T, _ = pm.shape
    c_q = rmsnorm(pm[..., :Q_LORA], q_norm)
    c_kv = rmsnorm(pm[..., Q_LORA:Q_LORA + KV_LORA], kv_norm)
    k_rope = rope(pm[..., Q_LORA + KV_LORA:], pos)
    q = (c_q @ w_uq).reshape(B, T, MLA_HEADS, QK_NOPE_DIM + QK_ROPE_DIM)
    q_rope = rope(q[..., QK_NOPE_DIM:], pos)
    q_lat = jnp.einsum('bthd,chd->bthc', q[..., :QK_NOPE_DIM], w_uk)
    return q_lat, q_rope, c_kv, k_rope

def mla_scores(q_lat, q_rope, c_kv, k_rope):
    s = jnp.einsum('bqhc,bkc->bhqk', q_lat, c_kv) + jnp.einsum('bqhr,bkr->bhqk', q_rope, k_rope)
    return s.astype(jnp.float32) * MLA_SCALE

def mla_attend_prompt(q_lat, q_rope, c_kv, k_rope):
    B, T, H, C = q_lat.shape
    nb = T // Q_BLOCK
    blocks = lambda t: jnp.moveaxis(t.reshape((B, nb, Q_BLOCK) + t.shape[2:]), 1, 0)
    k_pos = jnp.arange(T)

    def one_block(args):
        i, ql, qr = args
        s = mla_scores(ql, qr, c_kv, k_rope)
        q_pos = i * Q_BLOCK + jnp.arange(Q_BLOCK)
        s = jnp.where(k_pos[None, :] <= q_pos[:, None], s, -jnp.inf)
        pr = jax.nn.softmax(s, axis=-1).astype(c_kv.dtype)
        return jnp.einsum('bhqk,bkc->bqhc', pr, c_kv)

    o = lax.map(one_block, (jnp.arange(nb), blocks(q_lat), blocks(q_rope)))
    return jnp.moveaxis(o, 0, 1).reshape(B, T, H, C)

def mla_attend_sample(q_lat, q_rope, c_new, kr_new, ckv_past, kr_past):
    T = q_lat.shape[1]
    P = ckv_past.shape[1]
    s_past = mla_scores(q_lat, q_rope, ckv_past, kr_past)
    causal = jnp.tril(jnp.ones((T, T), dtype=bool))
    s_new = jnp.where(causal, mla_scores(q_lat, q_rope, c_new, kr_new), -jnp.inf)
    pr = jax.nn.softmax(jnp.concatenate([s_past, s_new], axis=-1), axis=-1).astype(c_new.dtype)
    return (jnp.einsum('bhqk,bkc->bqhc', pr[..., :P], ckv_past)
            + jnp.einsum('bhqk,bkc->bqhc', pr[..., P:], c_new))

def memory_kv(mem, g, w_k, w_v):
    m = rmsnorm(mem, g)
    shp = (mem.shape[0], mem.shape[1], MEM_HEADS, MEM_HEAD_DIM)
    return (m @ w_k).reshape(shp), (m @ w_v).reshape(shp)

def memory_cross_attend(h, mem_k, mem_v, w_q, w_o):
    B, T, _ = h.shape
    q = (h @ w_q).reshape(B, T, MEM_HEADS, MEM_HEAD_DIM)
    s = jnp.einsum('bthd,bmhd->bhtm', q, mem_k).astype(jnp.float32) * (MEM_HEAD_DIM ** -0.5)
    pr = jax.nn.softmax(s, axis=-1).astype(mem_v.dtype)
    return jnp.einsum('bhtm,bmhd->bthd', pr, mem_v).reshape(B, T, D_MODEL) @ w_o

def setup_inputs(seed: int = 0) -> dict:
    key = jax.random.key(seed)
    ks = iter(jax.random.split(key, 64))

    def nrm(shape, scale=1.0):
        return jax.random.normal(next(ks), shape, jnp.float32) * scale

    def gain(shape):
        return 1.0 + nrm(shape, 0.02)

    L, D = DEPTH, D_MODEL
    n_pages = PAST_LEN // PAGE_SIZE
    n_phys = (DEC_BATCH * n_pages * 5) // 4
    page_table = jax.random.permutation(next(ks), n_phys)[:DEC_BATCH * n_pages]
    page_table = page_table.reshape(DEC_BATCH, n_pages).astype(jnp.int32)
    return {
        'x_prompt': nrm((BATCH, SEQ, D)),
        'x_sample': nrm((DEC_BATCH, DEC_SEQ, D)),
        'cache_ckv': nrm((L, n_phys, PAGE_SIZE, KV_LORA)),
        'cache_krope': nrm((L, n_phys, PAGE_SIZE, QK_ROPE_DIM)),
        'state_wkv': nrm((L, DEC_BATCH, RWKV_HEADS, RWKV_HEAD_DIM, RWKV_HEAD_DIM), 0.3),
        'state_shift': nrm((L, DEC_BATCH, RWKV_PROJ)),
        'cache_mem_k': nrm((L, DEC_BATCH, N_MEM, MEM_HEADS, MEM_HEAD_DIM)),
        'cache_mem_v': nrm((L, DEC_BATCH, N_MEM, MEM_HEADS, MEM_HEAD_DIM)),
        'page_table': page_table,
        'mem_prompt': nrm((BATCH, N_MEM, D)),
        'norm_ffn1': gain((L, D)),
        'ffn1_w_gate': nrm((L, D, D_FF), D ** -0.5),
        'ffn1_w_up': nrm((L, D, D_FF), D ** -0.5),
        'ffn1_w_down': nrm((L, D_FF, D), D_FF ** -0.5),
        'norm_mix': gain((L, D)),
        'w_in': nrm((L, D, IN_PROJ), D ** -0.5),
        'shift_mu': jax.random.uniform(next(ks), (L, RWKV_PROJ), jnp.float32, 0.1, 0.9),
        'rwkv_w0': nrm((L, RWKV_WIDTH), 0.5),
        'rwkv_w_up': nrm((L, DECAY_LORA, RWKV_WIDTH), 0.5 * DECAY_LORA ** -0.5),
        'rwkv_a0': nrm((L, RWKV_WIDTH), 0.5),
        'rwkv_a_up': nrm((L, ICLR_LORA, RWKV_WIDTH), 0.5 * ICLR_LORA ** -0.5),
        'rwkv_g_up': nrm((L, GATE_LORA, RWKV_WIDTH), 2.0 * GATE_LORA ** -0.5),
        'rwkv_k_k': 0.85 + nrm((L, RWKV_WIDTH), 0.05),
        'rwkv_k_a': 1.0 + nrm((L, RWKV_WIDTH), 0.05),
        'rwkv_r_k': nrm((L, RWKV_HEADS, RWKV_HEAD_DIM), 0.1),
        'rwkv_gn_w': gain((L, RWKV_WIDTH)),
        'rwkv_gn_b': nrm((L, RWKV_WIDTH), 0.02),
        'mla_q_norm': gain((L, Q_LORA)),
        'mla_w_uq': nrm((L, Q_LORA, MLA_HEADS * (QK_NOPE_DIM + QK_ROPE_DIM)), Q_LORA ** -0.5),
        'mla_kv_norm': gain((L, KV_LORA)),
        'mla_w_uk': nrm((L, KV_LORA, MLA_HEADS, QK_NOPE_DIM), KV_LORA ** -0.5),
        'mla_w_uv': nrm((L, KV_LORA, MLA_HEADS, V_HEAD_DIM), KV_LORA ** -0.5),
        'w_out': nrm((L, MIX_WIDTH, D), MIX_WIDTH ** -0.5),
        'norm_cross': gain((L, D)),
        'norm_mem': gain((L, D)),
        'mem_w_q': nrm((L, D, D), D ** -0.5),
        'mem_w_k': nrm((L, D, D), D ** -0.5),
        'mem_w_v': nrm((L, D, D), D ** -0.5),
        'mem_w_o': nrm((L, D, D), D ** -0.5),
        'norm_ffn2': gain((L, D)),
        'ffn2_w_gate': nrm((L, D, D_FF), D ** -0.5),
        'ffn2_w_up': nrm((L, D, D_FF), D ** -0.5),
        'ffn2_w_down': nrm((L, D_FF, D), D_FF ** -0.5),
        'norm_final': gain((D,)),
    }

def reference(x_prompt, x_sample, cache_ckv, cache_krope, state_wkv, state_shift, cache_mem_k, cache_mem_v,
              page_table, mem_prompt,
              norm_ffn1, ffn1_w_gate, ffn1_w_up, ffn1_w_down, norm_mix, w_in, shift_mu,
              rwkv_w0, rwkv_w_up, rwkv_a0, rwkv_a_up, rwkv_g_up, rwkv_k_k, rwkv_k_a, rwkv_r_k, rwkv_gn_w, rwkv_gn_b,
              mla_q_norm, mla_w_uq, mla_kv_norm, mla_w_uk, mla_w_uv, w_out,
              norm_cross, norm_mem, mem_w_q, mem_w_k, mem_w_v, mem_w_o,
              norm_ffn2, ffn2_w_gate, ffn2_w_up, ffn2_w_down, norm_final):

    def trunk(x, pos, shift0, wkv0, mem_k, mem_v, attend):
        B, T, _ = x.shape
        ckvs, krs, wkvs, shifts = [], [], [], []
        for l in range(DEPTH):
            h = rmsnorm(x, norm_ffn1[l])
            x = x + 0.5 * swiglu_ffn(h, ffn1_w_gate[l], ffn1_w_up[l], ffn1_w_down[l])
            h = rmsnorm(x, norm_mix[l])
            proj = h @ w_in[l]
            p_rwkv, shift_last = token_shift(proj[..., :RWKV_PROJ], shift0[l], shift_mu[l])
            o_rwkv, wkv_last = rwkv7_mix(p_rwkv, wkv0[l], rwkv_w0[l], rwkv_w_up[l], rwkv_a0[l], rwkv_a_up[l],
                                         rwkv_g_up[l], rwkv_k_k[l], rwkv_k_a[l], rwkv_r_k[l],
                                         rwkv_gn_w[l], rwkv_gn_b[l])
            q_lat, q_rope, c_kv, k_rope = mla_project(proj[..., RWKV_PROJ:], pos, mla_q_norm[l], mla_w_uq[l],
                                                      mla_kv_norm[l], mla_w_uk[l])
            o_lat = attend(l, q_lat, q_rope, c_kv, k_rope)
            o_mla = jnp.einsum('bthc,chd->bthd', o_lat, mla_w_uv[l]).reshape(B, T, MLA_WIDTH)
            x = x + jnp.concatenate([o_rwkv, o_mla], axis=-1) @ w_out[l]
            h = rmsnorm(x, norm_cross[l])
            x = x + memory_cross_attend(h, mem_k[l], mem_v[l], mem_w_q[l], mem_w_o[l])
            h = rmsnorm(x, norm_ffn2[l])
            x = x + 0.5 * swiglu_ffn(h, ffn2_w_gate[l], ffn2_w_up[l], ffn2_w_down[l])
            ckvs.append(c_kv)
            krs.append(k_rope)
            wkvs.append(wkv_last)
            shifts.append(shift_last)
        return rmsnorm(x, norm_final), jnp.stack(ckvs), jnp.stack(krs), jnp.stack(wkvs), jnp.stack(shifts)

    Bp, Tp, _ = x_prompt.shape
    mem_k_list, mem_v_list = [], []
    for l in range(DEPTH):
        mk, mv = memory_kv(mem_prompt, norm_mem[l], mem_w_k[l], mem_w_v[l])
        mem_k_list.append(mk)
        mem_v_list.append(mv)
    new_mem_k_prompt = jnp.stack(mem_k_list)
    new_mem_v_prompt = jnp.stack(mem_v_list)
    y_prompt, new_ckv_prompt, new_krope_prompt, new_wkv_prompt, new_shift_prompt = trunk(
        x_prompt, jnp.arange(Tp),
        jnp.zeros((DEPTH, Bp, RWKV_PROJ), x_prompt.dtype),
        jnp.zeros((DEPTH, Bp, RWKV_HEADS, RWKV_HEAD_DIM, RWKV_HEAD_DIM), state_wkv.dtype),
        new_mem_k_prompt, new_mem_v_prompt,
        lambda l, ql, qr, c, k: mla_attend_prompt(ql, qr, c, k))

    Bd, Td, _ = x_sample.shape
    past_len = page_table.shape[1] * PAGE_SIZE

    def attend_sample(l, ql, qr, c, k):
        ckv_past = cache_ckv[l, page_table].reshape(Bd, past_len, KV_LORA)
        kr_past = cache_krope[l, page_table].reshape(Bd, past_len, QK_ROPE_DIM)
        return mla_attend_sample(ql, qr, c, k, ckv_past, kr_past)

    y_sample, new_ckv_sample, new_krope_sample, new_wkv_sample, new_shift_sample = trunk(
        x_sample, past_len + jnp.arange(Td), state_shift, state_wkv, cache_mem_k, cache_mem_v, attend_sample)

    return (y_prompt, y_sample, new_ckv_prompt, new_krope_prompt, new_wkv_prompt, new_shift_prompt,
            new_mem_k_prompt, new_mem_v_prompt, new_ckv_sample, new_krope_sample, new_wkv_sample, new_shift_sample)


_drawn_inputs = setup_inputs


def setup_inputs(seed=0):
    import zlib

    import numpy as np

    out = dict(_drawn_inputs(seed))
    spreads = {}
    factors = {'cache_krope': 3.705,
     'norm_ffn1': 3.015,
     'rwkv_k_k': 3.164,
     'rwkv_gn_w': 2.78,
     'rwkv_gn_b': 2.702,
     'mla_q_norm': 8.0,
     'mla_kv_norm': 3.182,
     'norm_cross': 8.0,
     'norm_mem': 2.871,
     'norm_ffn2': 5.306,
     'norm_final': 2.772}
    for name, (base, spread) in spreads.items():
        noise = np.random.default_rng([zlib.crc32(name.encode()), seed]).standard_normal(out[name].shape)
        drawn = base * np.exp(spread * noise) if base else spread * noise
        out[name] = jnp.asarray(drawn.astype(out[name].dtype))
    for name, factor in factors.items():
        out[name] = (out[name] * factor).astype(out[name].dtype)
    return out
```

```python
from contextlib import ExitStack

import numpy as np

import concourse.bass as bass
from concourse import mybir

ALU = mybir.AluOpType
ACT = mybir.ActivationFunctionType
AX = mybir.AxisListType
F32 = mybir.dt.float32
I32 = mybir.dt.int32

P = 128
DEPTH, D, SEQ, NS = 2, 1024, 256, 8
NT = SEQ + NS
KD = D // P
FF = 2816
KF = FF // P
H, HD = 8, 64
NJ = H // 2
RW = 14
NOPE, ROPE, CL = 64, 32, 128
QT = 2
PAST, PAGE = 2048, 128
JS = PAST // P
PER = 8
CHUNK = 64
LEVELS = 6
MH, MD, NM = 4, 256, 256
MLA_SCALE = (NOPE + ROPE) ** -0.5
MEM_SCALE = MD ** -0.5
RMS_EPS, GN_EPS = 1e-6, 64e-5
DECAY_C = float(np.exp(-0.5))
NEG = -1e30

VEC = {}
for _name, _tiles in (("ffn1", 8), ("mix", 8), ("cross", 8), ("ffn2", 8), ("mem", 8), ("mu", 14), ("w0", 4),
                      ("a0", 4), ("k_k", 4), ("k_a", 4), ("r_k", 4), ("gn_w", 4), ("gn_b", 4), ("q_norm", 2),
                      ("kv_norm", 1)):
    VEC[_name] = (sum(t for _, t in VEC.values()), _tiles)
NV = sum(t for _, t in VEC.values())

CON = {}
for _name, _cols in (("ident", P), ("blk", P), ("rot", P), ("sel", 4 * P), ("cos", NT), ("sin", NT),
                     ("causal", P), ("mk", 2 * P), ("mb", 2 * P), ("lvl", LEVELS * P), ("neg0", P),
                     ("keep", SEQ)):
    CON[_name] = (sum(t for _, t in CON.values()), _cols)
NC_ = sum(t for _, t in CON.values())

SW = {}
for _name, _cols in (("uq_nope", QT * NJ * P), ("uq_rope", QT * 2 * P), ("uk", NJ * CL), ("uv", H * HD),
                     ("wa_up", H * HD), ("g_up", H * HD)):
    SW[_name] = (sum(t for _, t in SW.values()), _cols)
NSW = sum(t for _, t in SW.values())

C_IN, C_OUT, C_MEMK, C_MEMV, C_Q, C_O = 0, 9, 13, 17, 21, 25
C_BLOCKS = 29
C_SLOTS = 2


class Signal:

    def __init__(self, name, sem, total, where, unit):
        self.name, self.sem, self.unit, self.where = name, sem, unit, where
        self.base, self.per = total
        self.count = {"before": 0, "layer": 0, "after": 0}

    def by(self, instruction, times=1):
        instruction.then_inc(self.sem, self.unit)
        self.count[self.where["phase"]] += times

    def grant(self, engine):
        engine.sem_inc(self.sem, self.unit)
        self.count["before"] += 1

    def at(self, k):
        phase = self.where["phase"]
        if phase == "before":
            return self.sem, self.unit * k
        if phase == "after":
            return self.sem, self.unit * (self.base + DEPTH * self.per + k)
        return self.sem, self.where["layer"] * (self.unit * self.per) + (k + self.base) * self.unit


class Milestone:

    def __init__(self, shared, place):
        self.shared, self.place = shared, place

    def by(self, instruction):
        self.shared.by(instruction)
        self.place = self.shared.count["layer"]

    def at(self, k):
        return self.shared.at(self.place)


MILESTONES = {
    "tensor_milestones": "ckv_turned qs_ready snew_ready kk_norm sv_turned so_turned gn_mean bonus_ready gn_var "
                         "gate_up mmax_turned mmax_all msum_ready",
    "vector_milestones": "cq_ready ckv_ready kr_ready qs_out kk_raw logw_ready sv_ready state_ready so_ready so_out "
                         "z_cleared rkr_ready centred bonus_out rwkv_mixed memg_ready mmax_rows mmax_diag "
                         "ms_less_max msum_rows ms_prob_ready",
    "scalar_milestones": "kk_squared sv_decay sv_tok_ready gd_ready gn_squared gate_out ms_exp_ready",
}
MILESTONE_OF = {name: shared for shared, names in MILESTONES.items() for name in names.split()}


class Chain:

    def __init__(self, engine, done):
        self.engine, self.done = engine, done

    def __call__(self, instruction, signal=None):
        signal = signal or self.done
        signal.by(instruction)
        events = 1 if isinstance(signal, Milestone) else signal.count[signal.where["phase"]]
        self.engine.wait_ge(*signal.at(events))


class Region:

    def __init__(self, tensor, start, end):
        self.tensor, self.at, self.end = tensor, start, end

    def take(self, *dims, parts=P):
        n = int(np.prod(dims))
        assert self.at + n <= self.end, (self.at, n, self.end)
        ap = self.tensor[0:parts, self.at:self.at + n]
        self.at += n
        if len(dims) > 1:
            names = "abcd"[:len(dims)]
            ap = ap.rearrange(f"p ({' '.join(names)}) -> p {' '.join(names)}",
                              **{x: d for x, d in zip(names[1:], dims[1:])})
        return ap


def build(nc, t, totals):
    ctx = ExitStack()
    where = {"phase": "before", "layer": 0}
    signals, milestones = {}, {}

    def signal(name):
        if name in MILESTONE_OF:
            if name not in milestones:
                milestones[name] = Milestone(signal(MILESTONE_OF[name]), totals.get(name, 1))
            return milestones[name]
        if name not in signals:
            unit = 16 if "loaded" in name or "spread" in name or name == "stored" else 1
            signals[name] = Signal(name, ctx.enter_context(nc.semaphore(name)), totals.get(name, (0, 0)), where, unit)
        return signals[name]

    def sbuf(name, shape, dtype=F32):
        return ctx.enter_context(nc.sbuf_tensor(name, shape, dtype))

    with ctx:
        ctx.enter_context(nc.allow_non_contiguous_dma("small strided pieces"))
        bank = [ctx.enter_context(nc.psum_tensor(f"bank{i}", [P, 512], F32)) for i in range(8)]
        con = sbuf("con", [P, NC_])
        vectors = sbuf("vectors", [P, DEPTH * NV + KD])
        vec = sbuf("vec", [P, NV])
        ones = sbuf("ones", [P, P])
        xT = sbuf("xT", [P, KD, NT])
        hT = sbuf("hT", [P, KD, NT])
        sq = sbuf("sq", [P, KD, NT])
        rstd = sbuf("rstd", [P, NT])
        ring_a = sbuf("ring_a", [P, 2, 2, KD, P])
        ring_b = sbuf("ring_b", [P, 2, KF, P])
        ring_c = sbuf("ring_c", [P, C_SLOTS, 2 * D])
        shift0 = sbuf("shift0", [P, RW, NS])
        small = sbuf("small", [P, NSW])
        rows_idx = sbuf("rows_idx", [P, NS], I32)
        part_idx = sbuf("part_idx", [P, NS], I32)
        ARENA = 25140
        arena = sbuf("arena", [P, ARENA])
        vec_dram = nc.dram_tensor("sample_vectors", (6, NS, H * HD), F32, kind="Internal").ap()
        out_dram = nc.dram_tensor("sample_outputs", (NS, H * HD), F32, kind="Internal").ap()

        def c(name, *dims):
            at, n = CON[name]
            ap = con[:, at:at + n]
            return ap if not dims else ap.rearrange("p (a b) -> p a b", a=dims[0])

        def v(name, k=0):
            at, _ = VEC[name]
            return vec[:, at + k:at + k + 1]

        def sw(name, **dims):
            at, n = SW[name]
            ap = small[:, at:at + n]
            return ap.rearrange(f"p ({' '.join(dims)}) -> p {' '.join(dims)}", **dims) if dims else ap

        ident = c("ident")

        r = Region(arena, 0, ARENA)
        hidden = r.take(KF, NT)
        silu = r.take(2, NT)

        r = Region(arena, 0, ARENA)
        p = r.take(RW, NT)
        MIX = r.at
        r = Region(arena, MIX, ARENA)
        ptmp = r.take(2, NT + 1)
        diff = r.take(NT)
        shift_out = r.take(RW, NS + 1)
        cq = r.take(QT, NT)
        ckv = r.take(NT)
        kr_raw = r.take(NT)
        kr = r.take(NT)
        kr_group = r.take(4, SEQ)
        qn = r.take(NJ, NT)
        qr_raw = r.take(2, NT)
        qr = r.take(2, NT)
        qr_group = r.take(4, H, NS)
        qlat = r.take(H, NT)
        olat = r.take(H, NT)
        ckv_tok = r.take(2, CL)
        prob = r.take(2, 512)
        prob_t = r.take(3, 512)
        ckv_t = r.take(JS, P)
        kr_t = r.take(4, P)
        s_sc = r.take(JS, H)
        s_pr = r.take(JS, H)
        stat = r.take(12, 64)
        s_new = r.take(H, NS)
        past_ckv = r.take(2, JS * CL)
        past_kr = r.take(2, JS * ROPE)

        r = Region(arena, MIX, ARENA)
        logw = r.take(NJ, NT)
        cum = r.take(NJ, SEQ)
        iclr = r.take(NJ, NT)
        kk = r.take(NJ, NT)
        AR = r.take(NJ, 2, P)
        Bt = r.take(NJ, P)
        Kt = r.take(NJ, P)
        din = r.take(NJ, P)
        tok = r.take(4, 512)
        U = r.take(H * HD)
        Z = r.take(3, NJ * P)
        dcm = r.take(NJ, P)
        wstat = r.take(NT)
        SOLVE = r.at
        MR_b = r.take(H, 2 * P)
        MR_k = r.take(H, 2 * P)
        Ml = r.take(H, P)
        X = r.take(H, P)
        XT = r.take(H, P)
        Y = r.take(H, P)
        G, Y0, WT = Ml.rearrange("p a b -> p (a b)")[:, 0:512], X.rearrange("p a b -> p (a b)")[:, 0:512], Y[:, 0:NJ, :]
        dex, dinv = X[:, 0:NJ, :], X[:, NJ:H, :]
        r = Region(arena, SOLVE, ARENA)
        lora = r.take(2, NT)
        w1 = r.take(NJ, NT)
        w2 = r.take(NJ, NT)
        S = r.take(32, HD)
        St = r.take(32, HD)
        r = Region(arena, MIX + 4 * (NJ * NT), ARENA)
        sv = r.take(NJ, 6, NS)
        sv_tok = r.take(NJ * P)
        svb = r.take(6, HD)
        svv = r.take(32)
        skk = r.take(32)
        so = r.take(32)
        so_tok = r.take(NJ * P)
        assert r.at <= SOLVE
        r = Region(arena, SOLVE, ARENA)
        gate = r.take(NJ, NT)
        bonus = r.take(NJ, NT)
        e1 = r.take(NJ, NT)
        e2 = r.take(NJ, NT)
        mixT = hT

        r = Region(arena, 0, ARENA)
        memg = r.take(KD, NM)
        KT = r.take(KD, NM)
        V = r.take(2, D)
        q = r.take(KD, NT)
        o = r.take(KD, NT)
        m_prob = r.take(4, 512)
        m_prob_t = r.take(MH, 2, SEQ)
        mem_k = r.take(2, KD * NM)
        mem_v = r.take(2, 2 * D)
        m_sc = r.take(NS, 2, MH)
        m_st = r.take(8, NS * MH)
        oT = mixT[:, 0:NJ, :]

        def mm(out, lhsT, rhs, start=True, stop=True):
            return nc.tensor.matmul(out, lhsT, rhs, start=start, stop=stop)

        def tp(out, in_, n=P):
            return nc.tensor.transpose(out, in_, ident[0:n, 0:n])

        kept = {}

        def wait_apart(engine, *waits):
            for s, value in waits:
                engine.wait_ge(s, value)
            if engine.engine in kept:
                engine.reg_alu(kept[engine.engine], kept[engine.engine], 16 * 3, ALU.bitwise_and)

        def keep_register(engine):
            kept[engine.engine] = engine.alloc_register("kept")
            engine.reg_mov(kept[engine.engine], 16 * 3)

        def use_register(engine):
            engine.wait_ge(signal("inputs_loaded").sem, engine.snap(kept[engine.engine]))

        block = ctx.enter_context(nc.Block())

        @block.sync
        def _(sp):
            where["phase"] = "before"
            loaded = signal("inputs_loaded")
            loaded.by(sp.dma_start(con[:], t["constants"]))
            loaded.by(sp.dma_start(vectors[:], t["vectors"]))
            loaded.by(sp.dma_start(xT[:], t["x"]))

            def ffn(f, layer):
                gu, down = t[f"ffn{f + 1}_gu"], t[f"ffn{f + 1}_down"]
                with sp.Fori(0, KF // 2) as i:
                    for u in range(2):
                        sp.wait_ge(*signal(f"gu_used{u}").at(f * (KF // 2) + i))
                        signal(f"gu_loaded{u}").by(
                            sp.dma_start(ring_a[:, u], gu[layer, 2 * i + u]), KF // 2)
                with sp.Fori(0, KD // 2) as i:
                    for u in range(2):
                        sp.wait_ge(*signal(f"down_used{u}").at(f * (KD // 2) + i))
                        signal(f"down_loaded{u}").by(
                            sp.dma_start(ring_b[:, u], down[layer, 2 * i + u]), KD // 2)

            def used(n):
                for first, name in ((C_O, "cross_ready"), (C_Q, "mq_ready"), (C_MEMV, "v_ready"),
                                    (C_MEMK, "kt_ready"), (C_OUT, "mix_ready"), (C_IN, "proj_ready")):
                    if n >= first:
                        return signal(name).at(2 * (n - first) + 2)

            def blocks(layer):
                for n in range(C_BLOCKS):
                    sp.wait_ge(*(used(n - C_SLOTS) if n >= C_SLOTS else signal("cross_ready").at(0)))
                    signal(f"block_loaded{n % C_SLOTS}").by(
                        sp.dma_start(ring_c[:, n % C_SLOTS], t["blocks"][layer, n]))

            where["phase"] = "layer"
            with sp.Fori(0, DEPTH) as layer:
                where["layer"] = layer
                ffn(0, layer)
                blocks(layer)
                ffn(1, layer)

        @block.gpsimd
        def _(pool):
            chain = Chain(pool, signal("pool_step"))
            stored = signal("stored")
            where["phase"] = "before"
            signal("index_loaded").by(pool.dma_start(rows_idx[:], t["pages"]))
            signal("index_loaded").by(pool.dma_start(part_idx[:], t["page_part"]))
            ckv_rows = t["cache_ckv"].rearrange("l n (e t) c -> (l n e) (t c)", e=PER)
            kr_rows = t["cache_krope"].rearrange("l n (e t) c -> (l n e) (t c)", e=PER)

            def gather(b):
                at = bass.IndirectOffsetOnAxis(ap=rows_idx[:, b:b + 1], axis=0)
                signal(f"past_loaded{b % 2}").by(
                    pool.indirect_dma_start(past_ckv[:, b % 2, :], None, ckv_rows, at))
                signal(f"past_loaded{b % 2}").by(
                    pool.indirect_dma_start(past_kr[:, b % 2, :], None, kr_rows, at))

            where["phase"] = "layer"
            keep_register(pool)
            with pool.Fori(0, DEPTH) as layer:
                where["layer"] = layer
                wait_apart(pool, signal("mix_added").at(0),
                           signal("cross_added").at(0))
                signal("small_loaded").by(pool.dma_start(small[:], t["small"][layer]))
                signal("small_loaded").by(pool.dma_start(shift0[:], t["shift0"][layer]))
                wait_apart(pool, signal("index_ready").at(0))
                gather(0)
                gather(1)
                wait_apart(pool, signal("ckv_ready").at(1),
                           signal("kr_ready").at(1))
                stored.by(pool.dma_start(t["o_ckv"][layer], ckv))
                stored.by(pool.dma_start(t["o_krope"][layer], kr[0:ROPE, :]))
                for b in range(2, NS):
                    wait_apart(pool, signal("pv_ready").at(b - 1))
                    gather(b)
                wait_apart(pool, signal("shifted").at(RW))
                stored.by(pool.dma_start(t["o_shift"][layer], shift_out))
                wait_apart(pool, stored.at(3))
                wait_apart(pool, signal("omla_out").at(NJ),
                           signal("sample_out").at(NS))
                signal("state_loaded").by(
                    pool.dma_start(S, t["state_wkv"][layer].rearrange("b h (a v) k -> (b h a) v k", a=2)))
                wait_apart(pool, signal("sv_tok_ready").at(1))
                signal("sv_spread").by(
                    pool.dma_start(vec_dram.rearrange("n b f -> (n b) f"), sv_tok[0:6 * NS, :]))
                wait_apart(pool, signal("sv_spread").at(1))
                for n in range(6):
                    src = vec_dram[n].rearrange("b (h k) -> (b h) k", h=H)
                    src = src.rearrange("p (o k) -> p o k", o=1).broadcast_to([NS * H, 2, HD])
                    signal("svb_loaded").by(pool.dma_start(svb[:, n, :], src))
                signal("svb_loaded").by(
                    pool.dma_start(svv, vec_dram[5].rearrange("b (g v) -> (b g) v", v=32)))
                wait_apart(pool, signal("state_ready").at(1))
                stored.by(pool.dma_start(t["o_wkv_s"][layer], S.rearrange("p a b -> p (a b)")))
                wait_apart(pool, signal("so_ready").at(1))
                signal("so_spread").by(
                    pool.dma_start(out_dram.rearrange("b (g v) -> (b g) v", v=32), so))
                wait_apart(pool, signal("so_spread").at(1))
                signal("so_loaded").by(pool.dma_start(so_tok[0:NS, :], out_dram))
                wait_apart(pool, stored.at(4))
                for T in range(2):
                    for n in range(1, LEVELS):
                        k = T * (LEVELS - 1) + n
                        wait_apart(pool, signal("mb_out").at(4 * T + 4))
                        if n > 1:
                            pool.wait_ge(*signal("y_ready").at(2 * k - 2))
                        for g in range(2):
                            ins = nc.gpsimd.tensor_tensor(
                                Ml[:, 4 * g:4 * g + 4, :], MR_b[:, 4 * g:4 * g + 4, 0:P],
                                c("lvl", LEVELS)[:, n:n + 1, :].broadcast_to([P, 4, P]), ALU.mult)
                            signal("level_ready").by(ins)
                wait_apart(pool, signal("z_out").at(4))
                stored.by(pool.dma_start(t["o_wkv"][layer], Z[:, 1, :].rearrange("p (j v) -> p j v", j=NJ)))
                wait_apart(pool, stored.at(5))
                wait_apart(pool, signal("mix_added").at(KD))
                signal("mem_loaded").by(pool.dma_start(memg, t["mem"]))

                def load_keys(b):
                    if b >= 2:
                        wait_apart(pool, signal("mem_k_used").at(b - 1))
                    signal(f"mem_k_loaded{b % 2}").by(
                        pool.dma_start(mem_k[:, b % 2, :], t["mem_k"][layer, b].rearrange("p a b -> p (a b)")))

                def load_values(b):
                    if b >= 2:
                        wait_apart(pool, signal("mem_v_used").at(b - 1))
                    signal(f"mem_v_loaded{b % 2}").by(
                        pool.dma_start(mem_v[:, b % 2, :], t["mem_v"][layer, b].rearrange("p a b -> p (a b)")))

                for b in range(2):
                    load_keys(b)
                    load_values(b)
                wait_apart(pool, signal("kt_out").at(KD))
                stored.by(pool.dma_start(t["o_mem_k"][layer], KT))
                wait_apart(pool, signal("v_out").at(8))
                stored.by(pool.dma_start(t["o_mem_v"][layer], V))
                for b in range(2, NS):
                    load_keys(b)
                for b in range(2, NS):
                    load_values(b)
                wait_apart(pool, stored.at(7))
            use_register(pool)
            where["phase"] = "after"
            wait_apart(pool, signal("final_ready").at(1))
            stored.by(pool.dma_start(t["y"], hT[:]))
            wait_apart(pool, stored.at(1))

        @block.tensor
        def _(pe):
            def sum_squares(n):
                pe.wait_ge(*signal("sq_ready").at(n))
                for k in range(KD):
                    last = mm(bank[6][:, 0:NT], ones[:], sq[:, k, :], k == 0, k == KD - 1)
                signal("sumsq_ready").by(last)

            def ffn(f):
                wait_apart(pe, signal("h_ready").at(3 * f + 1))
                with pe.Fori(0, KF // 2) as i:
                    for u in range(2):
                        at = f * (KF // 2) + i
                        pe.wait_ge(*signal(f"gu_loaded{u}").at(at + 1))
                        pe.wait_ge(*signal(f"silu_ready{u}").at(at))
                        for k in range(KD):
                            last = mm(bank[u][:, 0:NT], ring_a[:, u, 0, k, :], hT[:, k, :], k == 0, k == KD - 1)
                        signal(f"gate_ready{u}").by(last, KF // 2)
                        pe.wait_ge(*signal(f"hidden_ready{u}").at(at))
                        for k in range(KD):
                            last = mm(bank[2 + u][:, 0:NT], ring_a[:, u, 1, k, :], hT[:, k, :], k == 0, k == KD - 1)
                        signal(f"gu_used{u}").by(last, KF // 2)
                wait_apart(pe, *(signal(f"hidden_ready{u}").at((f + 1) * (KF // 2)) for u in range(2)))
                with pe.Fori(0, KD // 2) as i:
                    for u in range(2):
                        at = f * (KD // 2) + i
                        pe.wait_ge(*signal(f"down_loaded{u}").at(at + 1))
                        pe.wait_ge(*signal(f"ffn_added{u}").at(at))
                        for k in range(KF):
                            last = mm(bank[4 + u][:, 0:NT], ring_b[:, u, k, :], hidden[:, k, :], k == 0, k == KF - 1)
                        signal(f"down_used{u}").by(last, KD // 2)

            def block_of(n):
                pe.wait_ge(*signal(f"block_loaded{n % C_SLOTS}").at(n // C_SLOTS + 1))
                return ring_c[:, n % C_SLOTS, :]

            def project(first, tile, n, rhs, ready, width=NT):
                blk = first + tile // 2
                if tile % 2 == 0:
                    block_of(blk)
                w = ring_c[:, blk % C_SLOTS, :].rearrange("p (u k n) -> p u k n", u=2, k=KD)
                for k in range(KD):
                    last = mm(bank[n][:, 0:width], w[:, tile % 2, k, :], rhs[:, k, 0:width], k == 0, k == KD - 1)
                signal(ready).by(last)
                return last

            def mixing():
                pe.wait_ge(*signal("h_ready").at(2))
                for n in range(18):
                    if n >= 4:
                        pe.wait_ge(*signal("proj_out").at(n - 3))
                    project(C_IN, n, n % 4, hT, "proj_ready")
                    if n == 5:
                        pe.wait_ge(*signal("mla_sq_ready").at(2))
                        for k in range(QT):
                            last = mm(bank[4][:, 0:NT], ones[:], sq[:, k, :], k == 0, k == QT - 1)
                        signal("mla_sum_ready").by(last)
                        signal("mla_sum_ready").by(mm(bank[5][:, 0:NT], ones[:], sq[:, QT, :]))
                        signal("rot_ready").by(mm(bank[6][:, 0:NT], c("rot"), kr_raw))
                pe.wait_ge(*signal("small_loaded").at(2))
                pe.wait_ge(*signal("cq_ready").at(1))
                pe.wait_ge(*signal("proj_out").at(18))
                un = sw("uq_nope", a=QT, j=NJ, n=P)
                ur = sw("uq_rope", a=QT, j=2, n=P)
                for j in range(NJ):
                    for k in range(QT):
                        last = mm(bank[j][:, 0:NT], un[:, k, j, :], cq[:, k, :], k == 0, k == QT - 1)
                    signal("q_ready").by(last)
                pe.wait_ge(*signal("ckv_ready").at(1))
                for g in range(2):
                    for k in range(QT):
                        last = mm(bank[4 + g][:, 0:NT], ur[:, k, g, :], cq[:, k, :], k == 0, k == QT - 1)
                    signal("q_ready").by(last)
                pe.wait_ge(*signal("kr_ready").at(1))
                for T in range(2):
                    last = tp(bank[6][:, T * P:T * P + P], ckv[:, T * P:T * P + P])
                signal("ckv_turned").by(last)
                for g in range(2):
                    pe.wait_ge(*signal("q_out").at(NJ + g + 1))
                    signal("rot_ready").by(mm(bank[4 + g][:, 0:NT], c("rot"), qr_raw[:, g, :]))
                uk = sw("uk", j=NJ, n=CL)
                for h in range(H):
                    o0 = NOPE * (h % 2)
                    pe.wait_ge(*signal("q_out").at(min(NJ, h // 2 + 1) if h < 4 else NJ))
                    if h >= 4:
                        pe.wait_ge(*signal("qlat_out").at(h - 3))
                    signal("qlat_ready").by(mm(bank[h % 4][:, 0:NT], uk[o0:o0 + NOPE, h // 2, :],
                                               qn[o0:o0 + NOPE, h // 2, :]))
                pe.wait_ge(*signal("qr_ready").at(2))
                sel = c("sel", 4)
                for h in range(H):
                    last = mm(bank[7][:, h * NS:h * NS + NS], sel[:, h % 4, :], qr[:, h // 4, SEQ:NT])
                signal("qs_ready").by(last)
                pe.wait_ge(*signal("snew_products").at(2))
                mm(bank[6][:, 0:64], ones[:], stat[:, 0, :], True, False)
                signal("snew_ready").by(mm(bank[6][:, 0:64], ones[:], stat[:, 1, :], False, True))

                prompt_attention()
                sample_attention()

                uv = sw("uv")
                pe.wait_ge(*signal("olat_out").at(6))
                pe.wait_ge(*signal("sample_out").at(NS))
                for j in range(NJ):
                    for o0 in (0, 1):
                        h = 2 * j + o0
                        last = mm(bank[j][HD * o0:HD * o0 + HD, 0:NT], uv[:, h * HD:h * HD + HD], olat[:, h, :])
                    signal("omla_ready").by(last)

            def prompt_attention():
                units = [(0, 0, 4), (0, 4, 4)] + [(1, h, 2) for h in range(0, H, 2)]

                def scores(u):
                    qt, h0, nh = units[u]
                    if u >= 2:
                        pe.wait_ge(*signal("score_out").at(u - 1))
                    for i in range(nh):
                        h, n = h0 + i, (qt + 1) * P
                        out = bank[u % 2][:, i * n:i * n + n]
                        mm(out, qlat[:, h, qt * P:qt * P + P], ckv[:, 0:n], True, False)
                        last = mm(out, qr[:, h // 4, qt * P:qt * P + P], kr_group[:, h % 4, 0:n], False, True)
                    signal("score_ready").by(last)

                pe.wait_ge(*signal("qlat_out").at(H))
                scores(0)
                scores(1)
                for u, (qt, h0, nh) in enumerate(units):
                    pe.wait_ge(*signal("prob_ready").at(u + 1))
                    if u >= 2:
                        pe.wait_ge(*signal("prob_t_out").at(u - 1))
                    for i in range(4):
                        last = tp(bank[2 + u % 2][:, i * P:i * P + P], prob[:, u % 2, i * P:i * P + P])
                    signal("prob_t_ready").by(last)
                    if u + 2 < len(units):
                        scores(u + 2)
                    pe.wait_ge(*signal("prob_t_out").at(u + 1))
                    if u >= 2:
                        pe.wait_ge(*signal("olat_out").at(u - 1))
                    rhs = prob_t[:, u % 3, :]
                    if qt == 0:
                        last = mm(bank[4 + u % 2][:, 0:512], ckv_tok[:, 0, :], rhs)
                    else:
                        two = rhs.rearrange("p (h k q) -> p h k q", h=2, k=2)
                        for k in range(2):
                            last = mm(bank[4 + u % 2][:, 0:256], ckv_tok[:, k, :], two[:, :, k, :], k == 0, k == 1)
                    signal("olat_ready").by(last)

            def sample_attention():
                def turn(b):
                    pe.wait_ge(*signal(f"past_loaded{b % 2}").at(2 * (b // 2) + 2))
                    if b == 0:
                        pe.wait_ge(*signal("prob_t_out").at(6))
                        pe.wait_ge(*signal("olat_out").at(6))
                    else:
                        pe.wait_ge(*signal("past_t_dve").at(2 * b))
                        pe.wait_ge(*signal("past_t_act").at(3 * b))
                    for n in range(4):
                        for i in range(4):
                            j = 4 * n + i
                            last = tp(bank[n][:, i * P:i * P + P], past_ckv[:, b % 2, j * CL:j * CL + CL])
                        signal("turned").by(last)
                    for i in range(4):
                        last = tp(bank[4][:, i * P:i * P + P], past_kr[:, b % 2, i * P:i * P + P])
                    signal("turned").by(last)

                def scores(b):
                    pe.wait_ge(*signal("past_t_dve").at(2 * b + 2))
                    pe.wait_ge(*signal("past_t_act").at(3 * b + 3))
                    if b:
                        pe.wait_ge(*signal("s_out").at(b))
                    for j in range(JS):
                        out = bank[5][:, j * H:j * H + H]
                        mm(out, ckv_t[:, j, :], qlat[:, :, SEQ + b], True, False)
                        last = mm(out, kr_t[:, j // 4, :], qr_group[:, j % 4, :, b], False, True)
                    signal("s_ready").by(last)

                pe.wait_ge(*signal("qs_out").at(1))
                turn(0)
                scores(0)
                for b in range(NS):
                    if b + 1 < NS:
                        turn(b + 1)
                    pe.wait_ge(*signal("smax_rows").at(b + 1))
                    if b:
                        pe.wait_ge(*signal("sample_out").at(b))
                    signal("smax_turned").by(tp(bank[6][0:H, 0:P], stat[:, 2, 0:H]))
                    pe.wait_ge(*signal("smax_diag").at(b + 1))
                    signal("smax_all").by(mm(bank[6][:, P:P + H], ones[0:H, :], stat[0:H, 4, 0:H]))
                    if b + 1 < NS:
                        scores(b + 1)
                    pe.wait_ge(*signal("ssum_rows").at(b + 1))
                    signal("ssum_ready").by(mm(bank[6][:, 256:256 + H], ones[:], stat[:, 5, 0:H]))
                    for j in range(JS):
                        last = mm(bank[7][:, 0:H], past_ckv[:, b % 2, j * CL:j * CL + CL], s_pr[:, j, :],
                                  j == 0, j == JS - 1)
                    signal("pv_ready").by(last)

            def rwkv():
                wa = sw("wa_up")
                pe.wait_ge(*signal("lora_ready").at(2))
                pe.wait_ge(*signal("omla_out").at(NJ))
                for i in range(2):
                    for j in range(NJ):
                        last = mm(bank[4 * i + j][:, 0:NT], wa[64 * i:64 * i + 64, j * P:j * P + P],
                                  lora[64 * i:64 * i + 64, 0, :])
                    signal("wa_ready").by(last)
                pe.wait_ge(*signal("wa_out").at(2))
                pe.wait_ge(*signal("kk_squared").at(1))
                for j in range(NJ):
                    last = mm(bank[j][:, 0:NT], c("blk"), w2[:, j, :])
                signal("kk_norm").by(last)
                wait_apart(pe, signal("sv_ready").at(1))
                for j in range(NJ):
                    last = tp(bank[4][0:6 * NS, j * P:j * P + P], sv[:, j, :, :].rearrange("p n b -> p (n b)"))
                signal("sv_turned").by(last)
                wait_apart(pe, signal("so_loaded").at(1))
                for j in range(NJ):
                    last = tp(bank[5][:, j * NS:j * NS + NS], so_tok[0:NS, j * P:j * P + P], NS)
                signal("so_turned").by(last)
                pe.wait_ge(*signal("so_out").at(1))
                for T in range(2):
                    solve(T)
                    for cc in range(2):
                        chunk(T, cc)
                    outputs(T)
                pe.wait_ge(*signal("rwkv_out").at(2))
                pe.wait_ge(*signal("z_out").at(4))
                for j in range(NJ):
                    last = mm(bank[j][:, 0:NT], c("blk"), oT[:, j, :])
                signal("gn_mean").by(last)
                pe.wait_ge(*signal("rkr_ready").at(1))
                for j in range(NJ):
                    last = mm(bank[4 + j][:, 0:NT], c("blk"), e1[:, j, :])
                signal("bonus_ready").by(last)
                pe.wait_ge(*signal("gn_squared").at(1))
                pe.wait_ge(*signal("centred").at(1))
                for j in range(NJ):
                    last = mm(bank[j][:, 0:NT], c("blk"), e2[:, j, :])
                signal("gn_var").by(last)
                pe.wait_ge(*signal("bonus_out").at(1))
                pe.wait_ge(*signal("gd_ready").at(1))
                for j in range(NJ):
                    last = mm(bank[4 + j][:, 0:NT], sw("g_up")[:, j * P:j * P + P], wstat)
                signal("gate_up").by(last)

            def head(n):
                return 2 * (n % NJ) + n // NJ

            def solve(T):
                pe.wait_ge(*signal("operands_ready").at(T + 1))
                if T:
                    pe.wait_ge(*signal("rwkv_out").at(T))
                turned = [AR[:, :, 0, :], Bt, Kt, p[:, 8:12, T * P:T * P + P]]
                for n, src in enumerate(turned):
                    for j in range(NJ):
                        last = tp(bank[n][:, j * P:j * P + P], src[:, j, :])
                    signal("tok_turned").by(last)
                for n in range(4):
                    for i in range(2):
                        m = 2 * n + i
                        o0, j = HD * (m // NJ), m % NJ
                        last = mm(bank[4 + n][:, 256 * i:256 * i + 256], Bt[o0:o0 + HD, j, :],
                                  AR[o0:o0 + HD, j, :, :])
                    signal("pairs_ready").by(last)
                for n in range(4):
                    pe.wait_ge(*signal("tok_out").at(4 * T + n + 1))
                    for i in range(2):
                        m = 2 * n + i
                        o0, j = HD * (m // NJ), m % NJ
                        last = mm(bank[n][:, 256 * i:256 * i + 256], Kt[o0:o0 + HD, j, :],
                                  AR[o0:o0 + HD, j, :, :])
                    signal("pairs_ready").by(last)
                for g in range(2):
                    pe.wait_ge(*signal("mb_out").at(4 * T + g + 1))
                    for j in range(NJ):
                        last = mm(bank[4 + g][:, j * P:j * P + P], AR[HD * g:HD * g + HD, j, 0, :],
                                  Bt[HD * g:HD * g + HD, j, :])
                    signal("pairs_ready").by(last)
                pe.wait_ge(*signal("mk_out").at(4 * T + 4))
                for n in range(1, LEVELS):
                    for g in range(2):
                        k = 2 * (T * (LEVELS - 1) + n - 1) + g + 1
                        pe.wait_ge(*signal("level_ready").at(k))
                        pe.wait_ge(*signal("x_out").at(k + 2 * T))
                        for i in range(4):
                            m = 4 * g + i
                            last = mm(bank[g][:, i * P:i * P + P], Ml[:, m, :], X[:, m, :])
                        signal("y_ready").by(last)
                    for g in range(2):
                        k = 2 * (T * (LEVELS - 1) + n - 1) + g + 1
                        pe.wait_ge(*signal("y_out").at(k))
                        if n < LEVELS - 1:
                            for i in range(4):
                                m = 4 * g + i
                                mm(bank[2 + g][:, i * P:i * P + P], XT[:, m, :], Y[:, m, :])
                        for i in range(4):
                            m = 4 * g + i
                            last = mm(bank[4 + g][:, i * P:i * P + P], Y[:, m, :], XT[:, m, :])
                        signal("xy_ready").by(last)
                for m in range(H):
                    h = head(m)
                    last = mm(bank[6][:, h * HD:h * HD + HD], MR_k[:, m, 0:P], tok[:, 3, h * HD:h * HD + HD])
                signal("g_ready").by(last)
                pe.wait_ge(*signal("g_out").at(T + 1))
                pe.wait_ge(*signal("x_out").at(2 * (T + 1) * LEVELS))
                for m in range(H):
                    h = head(m)
                    last = mm(bank[7][:, h * HD:h * HD + HD], XT[:, m, :], G[:, h * HD:h * HD + HD])
                signal("y0_ready").by(last)
                for m in range(H):
                    h = head(m)
                    o0 = HD * (h % 2)
                    last = mm(bank[6][o0:o0 + HD, (h // 2) * P:(h // 2) * P + P], tok[:, 0, h * HD:h * HD + HD],
                              XT[:, m, :])
                signal("wt_ready").by(last)

            def chunk(T, cc):
                n, o0 = 2 * T + cc, CHUNK * cc
                if n:
                    pe.wait_ge(*signal("z_out").at(n))
                if cc == 0:
                    pe.wait_ge(*signal("wt_out").at(T + 1))
                if n == 0:
                    pe.wait_ge(*signal("z_cleared").at(1))
                for j in range(NJ):
                    last = mm(bank[0][o0:o0 + CHUNK, j * P:j * P + P], WT[:, j, o0:o0 + CHUNK],
                              Z[:, n % 3, j * P:j * P + P])
                signal("u_ready").by(last)
                pe.wait_ge(*signal("u_out").at(n + 1))
                for j in range(NJ):
                    cols = slice(j * P, j * P + P)
                    mm(bank[1][:, cols], tok[o0:o0 + CHUNK, 1, cols], U[o0:o0 + CHUNK, cols], True, False)
                    last = mm(bank[1][:, cols], tok[o0:o0 + CHUNK, 2, cols], tok[o0:o0 + CHUNK, 3, cols], False, True)
                signal("z_ready").by(last)

            def outputs(T):
                for j in range(NJ):
                    out = bank[2][:, j * P:j * P + P]
                    for cc in range(2):
                        nc.tensor.matmul(out[:, CHUNK * cc:CHUNK * cc + CHUNK], Z[:, (2 * T + cc) % 3, j * P:j * P + P],
                                         AR[:, j, 1, CHUNK * cc:CHUNK * cc + CHUNK], start=cc == 0, stop=False,
                                         skip_group_check=True)
                    for i in range(2):
                        h, m = 2 * j + i, NJ * i + j
                        part = out[HD * i:HD * i + HD, :]
                        nc.tensor.matmul(part, U[:, h * HD:h * HD + HD], MR_b[:, m, P:2 * P], start=False,
                                         stop=False, skip_group_check=True)
                        last = nc.tensor.matmul(part, tok[:, 3, h * HD:h * HD + HD], MR_k[:, m, P:2 * P],
                                                start=False, stop=True, skip_group_check=True)
                signal("rwkv_ready").by(last)

            def mix_out():
                pe.wait_ge(*signal("rwkv_mixed").at(1))
                for n in range(KD):
                    if n >= 4:
                        pe.wait_ge(*signal("mix_added").at(n - 3))
                    project(C_OUT, n, n % 4, mixT, "mix_ready")

            def cross():
                sum_squares(3)
                pe.wait_ge(*signal("memg_ready").at(1))
                pe.wait_ge(*signal("mix_added").at(KD))
                for n in range(KD):
                    if n >= 4:
                        pe.wait_ge(*signal("kt_out").at(n - 3))
                    project(C_MEMK, n, n % 4, memg, "kt_ready", NM)
                for blk in range(4):
                    w = block_of(C_MEMV + blk).rearrange("p (k n) -> p k n", k=KD)
                    for T in range(2):
                        n = 2 * blk + T
                        if n >= 2:
                            pe.wait_ge(*signal("v_out").at(n - 1))
                        for k in range(KD):
                            last = mm(bank[4 + T][:, 0:256], memg[:, k, T * P:T * P + P], w[:, k, :], k == 0, k == KD - 1)
                        signal("v_ready").by(last)
                sum_squares(4)
                pe.wait_ge(*signal("h_ready").at(3))
                for n in range(KD):
                    pe.wait_ge(*signal("kt_out" if n < 4 else "mq_out").at(KD if n < 4 else n - 3))
                    project(C_Q, n, n % 4, hT, "mq_ready")
                pe.wait_ge(*signal("mq_out").at(KD))
                pe.wait_ge(*signal("v_out").at(8))

                units = [(qt, hp) for hp in range(2) for qt in range(2)]

                def scores(u):
                    qt, hp = units[u]
                    if u >= 2:
                        pe.wait_ge(*signal("m_less_max").at(u - 1))
                    for i in range(2):
                        for dt in range(2):
                            k = 2 * (2 * hp + i) + dt
                            last = mm(bank[4 + u % 2][:, i * NM:i * NM + NM], q[:, k, qt * P:qt * P + P], KT[:, k, :],
                                      dt == 0, dt == 1)
                    signal("m_score_ready").by(last)

                scores(0)
                scores(1)
                for b in range(NS):
                    pe.wait_ge(*signal(f"mem_k_loaded{b % 2}").at(b // 2 + 1))
                    kt_b = mem_k[:, b % 2, :].rearrange("p (k m) -> p k m", k=KD)
                    for mt in range(2):
                        for h in range(MH):
                            for dt in range(2):
                                k = 2 * h + dt
                                col = (b * 2 + mt) * MH + h
                                last = mm(bank[3][:, col:col + 1], kt_b[:, k, mt * P:mt * P + P],
                                          q[:, k, SEQ + b:SEQ + b + 1], dt == 0, dt == 1)
                    signal("mem_k_used").by(last)
                for u in range(4):
                    pe.wait_ge(*signal("m_prob_ready").at(u + 1))
                    if u >= 2:
                        pe.wait_ge(*signal("m_prob_t_out").at(u - 1))
                    for i in range(4):
                        last = tp(bank[6 + u % 2][:, i * P:i * P + P], m_prob[:, u, i * P:i * P + P])
                    signal("m_prob_t_ready").by(last)
                    if u + 2 < 4:
                        scores(u + 2)
                for k in range(KD):
                    pe.wait_ge(*signal("m_prob_t_out").at(2 * (k // 4) + 2))
                    if k >= 2:
                        pe.wait_ge(*signal("mo_out").at(k - 1))
                    for mt in range(2):
                        last = mm(bank[k % 2][:, 0:SEQ], V[:, mt, k * P:k * P + P], m_prob_t[:, k // 2, mt, :],
                                  mt == 0, mt == 1)
                    signal("mo_ready").by(last)
                pe.wait_ge(*signal("mmax_rows").at(1))
                pe.wait_ge(*signal("m_less_max").at(4))
                signal("mmax_turned").by(tp(bank[4][0:32, 0:P], m_st[:, 0, :]))
                pe.wait_ge(*signal("mmax_diag").at(1))
                signal("mmax_all").by(mm(bank[4][:, P:P + 32], ones[0:32, :], m_st[0:32, 2, :]))
                pe.wait_ge(*signal("msum_rows").at(1))
                signal("msum_ready").by(mm(bank[4][:, 256:288], ones[:], m_st[:, 3, :]))
                pe.wait_ge(*signal("ms_prob_ready").at(1))
                for b in range(NS):
                    pe.wait_ge(*signal(f"mem_v_loaded{b % 2}").at(b // 2 + 1))
                    v_b = mem_v[:, b % 2, :].rearrange("p (m n) -> p m n", m=2)
                    for k in range(KD):
                        for mt in range(2):
                            last = mm(bank[5][:, k * NS + b:k * NS + b + 1], v_b[:, mt, k * P:k * P + P],
                                      m_sc[:, b, mt, k // 2:k // 2 + 1], mt == 0, mt == 1)
                    signal("mem_v_used").by(last)
                pe.wait_ge(*signal("mo_out").at(KD + 1))
                for n in range(KD):
                    if n >= 4:
                        pe.wait_ge(*signal("cross_added").at(n - 3))
                    project(C_O, n, n % 4, o, "cross_ready")

            where["phase"] = "before"
            pe.wait_ge(*signal("inputs_loaded").at(3))
            pe.wait_ge(*signal("ones_ready").at(1))
            keep_register(pe)
            for name in 'gu_used0 gu_used1 down_used0 down_used1 cross_ready'.split():
                signal(name).grant(pe)
            where["phase"] = "layer"
            with pe.Fori(0, DEPTH) as layer:
                where["layer"] = layer
                sum_squares(1)
                ffn(0)
                sum_squares(2)
                mixing()
                rwkv()
                mix_out()
                cross()
                sum_squares(5)
                ffn(1)
            use_register(pe)
            where["phase"] = "after"
            sum_squares(1)

        @block.scalar
        def _(act):
            chain = Chain(act, signal("act_step"))

            def run(out, in_, func=ACT.Copy, done=None, **more):
                chain(nc.scalar.activation(out, in_, func, **more), signal(done) if done else None)

            def root(ap):
                k = signal("root_ready").count[where["phase"]] + 1
                act.wait_ge(*signal("inverse_ready").at(k))
                run(ap, ap, ACT.Sqrt, "root_ready")

            def square(src):
                run(sq[:].rearrange("p a b -> p (a b)"), src.rearrange("p a b -> p (a b)"), ACT.Square, "sq_ready")
                root(rstd[:])

            def ffn(f):
                with act.Fori(0, KF // 2) as i:
                    for u in range(2):
                        at = f * (KF // 2) + i
                        act.wait_ge(*signal(f"gate_ready{u}").at(at + 1))
                        act.wait_ge(*signal(f"hidden_ready{u}").at(at))
                        signal(f"silu_ready{u}").by(
                            nc.scalar.activation(silu[:, u, :], bank[u][:, 0:NT], ACT.Silu), KF // 2)

            def mixing():
                dest = [cq[:, 0, :], cq[:, 1, :], ckv, kr_raw]
                for n in range(18):
                    act.wait_ge(*signal("proj_ready").at(n + 1))
                    if n >= 6:
                        act.wait_ge(*signal("shifted").at(n - 5))
                    run(dest[n] if n < 4 else ptmp[:, n % 2, 1:NT + 1], bank[n % 4][:, 0:NT], done="proj_out")
                    if n == 3:
                        run(sq[:, 0:QT, :].rearrange("p a b -> p (a b)"), cq.rearrange("p a b -> p (a b)"),
                            ACT.Square, "mla_sq_ready")
                        run(sq[:, QT, :], ckv, ACT.Square, "mla_sq_ready")
                    if n == 5:
                        root(rstd[:])
                        root(rstd[:])
                for j in range(NJ + 2):
                    act.wait_ge(*signal("q_ready").at(j + 1))
                    run(qn[:, j, :] if j < NJ else qr_raw[:, j - NJ, :], bank[j][:, 0:NT], done="q_out")
                for h in range(H):
                    act.wait_ge(*signal("qlat_ready").at(h + 1))
                    run(qlat[:, h, :], bank[h % 4][:, 0:NT], done="qlat_out")
                units = [(0, 0, 4), (0, 4, 4)] + [(1, h, 2) for h in range(0, H, 2)]

                def exponentials(u):
                    act.wait_ge(*signal("score_less_max").at(u + 1))
                    run(prob[:, u % 2, :], prob[:, u % 2, :], ACT.Exp, "exp_ready", scale=MLA_SCALE)

                exponentials(0)
                for u, (qt, h0, nh) in enumerate(units):
                    if u + 1 < len(units):
                        exponentials(u + 1)
                    act.wait_ge(*signal("prob_t_ready").at(u + 1))
                    run(prob_t[:, u % 3, :], bank[2 + u % 2][:, 0:512], done="prob_t_out")
                    act.wait_ge(*signal("olat_ready").at(u + 1))
                    n = nh * P
                    run(olat[:, h0:h0 + nh, qt * P:qt * P + P],
                        bank[4 + u % 2][:, 0:n].rearrange("p (h q) -> p h q", h=nh), done="olat_out")

                def turned(b):
                    act.wait_ge(*signal("turned").at(5 * b + 5))
                    if b:
                        act.wait_ge(*signal("s_ready").at(b))
                    for n in (2, 3):
                        run(ckv_t[:, 4 * n:4 * n + 4, :].rearrange("p a b -> p (a b)"), bank[n][:, 0:512],
                            done="past_t_act")
                    run(kr_t.rearrange("p a b -> p (a b)"), bank[4][:, 0:512], done="past_t_act")

                turned(0)
                for b in range(NS):
                    if b + 1 < NS:
                        turned(b + 1)
                    act.wait_ge(*signal("s_less_max").at(b + 1))
                    run(stat[:, 7, 0:H], stat[:, 7, 0:H], ACT.Exp, scale=MLA_SCALE)
                    run(s_pr.rearrange("p a b -> p (a b)"), s_sc.rearrange("p a b -> p (a b)"), ACT.Exp,
                        "s_exp_ready", scale=MLA_SCALE)
                for j in range(NJ):
                    act.wait_ge(*signal("omla_ready").at(j + 1))
                    run(mixT[:, NJ + j, :], bank[j][:, 0:NT], done="omla_out")

            def rwkv():
                act.wait_ge(*signal("sample_out").at(NS))
                act.wait_ge(*signal("stored").at(3))
                run(lora[0:64, 0, :], p[0:64, 12, :], ACT.Tanh, "lora_ready")
                run(lora[64:P, 0, :], p[64:P, 12, :], ACT.Copy, "lora_ready")
                act.wait_ge(*signal("wa_ready").at(1))
                for j in range(NJ):
                    run(w1[:, j, :], bank[j][:, 0:NT], ACT.Sigmoid, bias=v("w0", j),
                        done="wa_out" if j == NJ - 1 else None)
                act.wait_ge(*signal("wa_ready").at(2))
                for j in range(NJ):
                    run(iclr[:, j, :], bank[4 + j][:, 0:NT], ACT.Sigmoid, bias=v("a0", j),
                        done="wa_out" if j == NJ - 1 else None)
                act.wait_ge(*signal("kk_raw").at(1))
                run(w2.rearrange("p a b -> p (a b)"), kk.rearrange("p a b -> p (a b)"), ACT.Square, "kk_squared")
                act.wait_ge(*signal("logw_ready").at(1))
                run(sv[:, :, 1, :], logw[:, :, SEQ:NT], ACT.Exp, "sv_decay")
                root(w1.rearrange("p a b -> p (a b)"))
                act.wait_ge(*signal("sv_turned").at(1))
                run(sv_tok[0:6 * NS, :], bank[4][0:6 * NS, 0:512], done="sv_tok_ready")
                for T in range(2):
                    act.wait_ge(*signal("decays").at(T + 1))
                    ts = slice(T * P, T * P + P)
                    run(dex, dex, ACT.Exp)
                    run(din, cum[:, :, ts], ACT.Exp)
                    run(dinv, cum[:, :, ts], ACT.Exp, "decays_ready", scale=-1.0)
                    for n in range(4):
                        act.wait_ge(*signal("tok_turned").at(4 * T + n + 1))
                        run(tok[:, n, :], bank[n][:, 0:512], done="tok_out", scale=-1.0 if n == 1 else 1.0)
                    for n in range(1, LEVELS):
                        for g in range(2):
                            k = 2 * (T * (LEVELS - 1) + n - 1) + g + 1
                            act.wait_ge(*signal("y_ready").at(k))
                            if n > 1:
                                act.wait_ge(*signal("xy_ready").at(k - 2))
                            run(Y[:, 4 * g:4 * g + 4, :].rearrange("p a b -> p (a b)"), bank[g][:, 0:512], done="y_out")
                    act.wait_ge(*signal("g_ready").at(T + 1))
                    run(G, bank[6][:, 0:512], done="g_out")
                    act.wait_ge(*signal("y0_ready").at(T + 1))
                    run(Y0, bank[7][:, 0:512], done="y0_out")
                    act.wait_ge(*signal("wt_ready").at(T + 1))
                    run(WT.rearrange("p a b -> p (a b)"), bank[6][:, 0:512], done="wt_out")
                    act.wait_ge(*signal("rwkv_ready").at(T + 1))
                    run(oT[:, :, T * P:T * P + P], bank[2][:, 0:512].rearrange("p (j t) -> p j t", j=NJ),
                        done="rwkv_out")
                act.wait_ge(*signal("z_out").at(4))
                run(wstat, p[:, 13, :], ACT.Sigmoid, "gd_ready")
                act.wait_ge(*signal("centred").at(1))
                act.wait_ge(*signal("bonus_ready").at(1))
                run(e2.rearrange("p a b -> p (a b)"), oT_flat, ACT.Square, "gn_squared")
                root(e2.rearrange("p a b -> p (a b)"))
                act.wait_ge(*signal("gate_up").at(1))
                for j in range(NJ):
                    run(gate[:, j, :], bank[4 + j][:, 0:NT], done="gate_out" if j == NJ - 1 else None)

            oT_flat = oT.rearrange("p a b -> p (a b)")

            def cross():
                act.wait_ge(*signal("mem_loaded").at(1))
                run(sq[:, :, 0:NM], memg, ACT.Square, "sq_ready")
                root(rstd[:, 0:NM])
                for n in range(KD):
                    act.wait_ge(*signal("kt_ready").at(n + 1))
                    run(KT[:, n, :], bank[n % 4][:, 0:NM], done="kt_out")
                square(xT[:])
                for n in range(KD):
                    act.wait_ge(*signal("mq_ready").at(n + 1))
                    run(q[:, n, :], bank[n % 4][:, 0:NT], done="mq_out")

                def exponentials(u):
                    act.wait_ge(*signal("m_less_max").at(u + 1))
                    run(m_prob[:, u, :], m_prob[:, u, :], ACT.Exp, "m_exp_ready", scale=MEM_SCALE)

                exponentials(0)
                for u in range(4):
                    if u + 1 < 4:
                        exponentials(u + 1)
                    qt, hp = u % 2, u // 2
                    act.wait_ge(*signal("m_prob_t_ready").at(u + 1))
                    run(m_prob_t[:, 2 * hp:2 * hp + 2, :, qt * P:qt * P + P].rearrange("p h k q -> p (h k) q"),
                        bank[6 + u % 2][:, 0:512].rearrange("p (a q) -> p a q", a=4), done="m_prob_t_out")
                for k in range(KD):
                    act.wait_ge(*signal("mo_ready").at(k + 1))
                    run(o[:, k, 0:SEQ], bank[k % 2][:, 0:SEQ], done="mo_out")
                act.wait_ge(*signal("ms_less_max").at(1))
                run(m_sc.rearrange("p a b c -> p (a b c)"), m_sc.rearrange("p a b c -> p (a b c)"), ACT.Exp,
                    "ms_exp_ready", scale=MEM_SCALE)
                act.wait_ge(*signal("mem_v_used").at(NS))
                run(o[:, :, SEQ:NT], bank[5][:, 0:KD * NS].rearrange("p (a b) -> p a b", a=KD), done="mo_out")

            where["phase"] = "before"
            act.wait_ge(*signal("inputs_loaded").at(3))
            for name in 'silu_ready0 silu_ready1'.split():
                signal(name).grant(act)
            where["phase"] = "layer"
            with act.Fori(0, DEPTH) as layer:
                where["layer"] = layer
                for u in range(2):
                    act.wait_ge(*signal(f"ffn_added{u}").at(0))
                square(xT[:])
                ffn(0)
                for u in range(2):
                    act.wait_ge(*signal(f"ffn_added{u}").at(KD // 2))
                square(xT[:])
                mixing()
                rwkv()
                act.wait_ge(*signal("mix_added").at(KD))
                cross()
                act.wait_ge(*signal("cross_added").at(KD))
                square(xT[:])
                ffn(1)
            where["phase"] = "after"
            for u in range(2):
                act.wait_ge(*signal(f"ffn_added{u}").at(0))
            square(xT[:])

        @block.vector
        def _(dve):
            chain = Chain(dve, signal("dve_step"))

            def out_of(done):
                return signal(done) if done else None

            def tt(out, a, b, op, done=None):
                chain(nc.vector.tensor_tensor(out, a, b, op), out_of(done))

            def ts(out, a, s1, op0, s2=None, op1=None, done=None):
                if op1 is None:
                    chain(nc.vector.tensor_scalar(out, a, s1, None, op0), out_of(done))
                else:
                    chain(nc.vector.tensor_scalar(out, a, s1, s2, op0, op1), out_of(done))

            def stt(out, a, s, b, op0, op1, done=None):
                chain(nc.vector.scalar_tensor_tensor(out=out, in0=a, scalar=s, in1=b, op0=op0, op1=op1), out_of(done))

            def copy(out, a, done=None):
                chain(nc.vector.tensor_copy(out, a), out_of(done))

            def largest(out, a, done=None):
                chain(nc.vector.tensor_reduce(out, a, AX.X, ALU.max), out_of(done))

            def total(out, a, done=None):
                chain(nc.vector.tensor_reduce(out, a, AX.X, ALU.add), out_of(done))

            def clear(out, done=None):
                chain(nc.vector.memset(out, 0.0), out_of(done))

            def over(ap, *shape):
                return ap.rearrange("p (o n) -> p o n", o=1).broadcast_to(list(shape))

            def last_dim(ap, *shape):
                return ap.rearrange("p (n o) -> p n o", o=1).broadcast_to(list(shape))

            def flat(ap):
                return ap.rearrange("p a b -> p (a b)")

            def root_of_inverse(ap):
                k = signal("inverse_ready").count[where["phase"]] + 1
                chain(nc.vector.reciprocal(ap, ap), signal("inverse_ready"))
                dve.wait_ge(*signal("root_ready").at(k))

            def inverse_rms(out, sums, n, eps):
                ts(out, sums, 1.0 / n, ALU.mult, eps, ALU.add)
                root_of_inverse(out)

            def norm(n, gain, src, dst, done, width=NT):
                dve.wait_ge(*signal("sumsq_ready").at(n))
                inverse_rms(rstd[:, 0:width], bank[6][:, 0:width], D, RMS_EPS)
                for k in range(KD):
                    stt(dst[:, k, 0:width], src[:, k, 0:width], gain(k), rstd[:, 0:width], ALU.mult, ALU.mult,
                        done if k == KD - 1 else None)

            def ffn(f):
                wait_apart(dve, signal("h_ready").at(3 * f + 1))
                with dve.Fori(0, KF // 2) as i:
                    for u in range(2):
                        at = f * (KF // 2) + i
                        dve.wait_ge(*signal(f"silu_ready{u}").at(at + 1))
                        dve.wait_ge(*signal(f"gu_used{u}").at(at + 1))
                        signal(f"hidden_ready{u}").by(
                            nc.vector.tensor_tensor(hidden[:, 2 * i + u, :], silu[:, u, :], bank[2 + u][:, 0:NT],
                                                    ALU.mult), KF // 2)
                with dve.Fori(0, KD // 2) as i:
                    for u in range(2):
                        at = f * (KD // 2) + i
                        dve.wait_ge(*signal(f"down_used{u}").at(at + 1))
                        signal(f"ffn_added{u}").by(
                            nc.vector.scalar_tensor_tensor(out=xT[:, 2 * i + u, :], in0=bank[4 + u][:, 0:NT],
                                                           scalar=0.5, in1=xT[:, 2 * i + u, :], op0=ALU.mult,
                                                           op1=ALU.add), KD // 2)
                for u in range(2):
                    dve.wait_ge(*signal(f"ffn_added{u}").at((f + 1) * (KD // 2)))

            def mixing():
                for u in range(2):
                    clear(ptmp[:, u, 0:1])
                clear(kr_group.rearrange("p a b -> p (a b)"))
                clear(qr_group.rearrange("p a b c -> p (a b c)"))
                dve.wait_ge(*signal("mla_sum_ready").at(1))
                inverse_rms(rstd[:], bank[4][:, 0:NT], QT * P, RMS_EPS)
                for k in range(QT):
                    stt(cq[:, k, :], cq[:, k, :], v("q_norm", k), rstd[:], ALU.mult, ALU.mult,
                        "cq_ready" if k else None)
                dve.wait_ge(*signal("mla_sum_ready").at(2))
                inverse_rms(rstd[:], bank[5][:, 0:NT], CL, RMS_EPS)
                stt(ckv, ckv, v("kv_norm"), rstd[:], ALU.mult, ALU.mult, "ckv_ready")
                dve.wait_ge(*signal("rot_ready").at(1))
                tt(kr, kr_raw, c("cos"), ALU.mult)
                tt(diff, bank[6][:, 0:NT], c("sin"), ALU.mult)
                tt(kr, kr, diff, ALU.add, "kr_ready")
                for g in range(4):
                    copy(kr_group[32 * g:32 * g + 32, g, :], kr[32 * g:32 * g + 32, 0:SEQ])
                dve.wait_ge(*signal("small_loaded").at(2))
                for n, j in enumerate([12, 13] + list(range(12))):
                    dve.wait_ge(*signal("proj_out").at(5 + n))
                    src = ptmp[:, n % 2, :]
                    tt(diff[:, 0:SEQ], src[:, 0:SEQ], src[:, 1:SEQ + 1], ALU.subtract)
                    tt(diff[:, SEQ:NT], shift0[:, j, :], src[:, SEQ + 1:NT + 1], ALU.subtract)
                    stt(p[:, j, :], diff, v("mu", j), src[:, 1:NT + 1], ALU.mult, ALU.add)
                    copy(shift_out[:, j, :], src[:, SEQ:NT + 1], "shifted")
                dve.wait_ge(*signal("ckv_turned").at(1))
                copy(ckv_tok.rearrange("p a b -> p (a b)"), bank[6][:, 0:256])
                for g in range(2):
                    dve.wait_ge(*signal("rot_ready").at(g + 2))
                    tt(qr[:, g, :], qr_raw[:, g, :], c("cos"), ALU.mult)
                    tt(diff, bank[4 + g][:, 0:NT], c("sin"), ALU.mult)
                    tt(qr[:, g, :], qr[:, g, :], diff, ALU.add, "qr_ready")
                dve.wait_ge(*signal("qs_ready").at(1))
                for g in range(4):
                    rows = slice(32 * g, 32 * g + 32)
                    copy(qr_group[rows, g, :, :], bank[7][rows, 0:64].rearrange("p (h b) -> p h b", h=H),
                         "qs_out" if g == 3 else None)
                dve.wait_ge(*signal("qlat_out").at(H))
                three = [P, H, NS]
                tt(stat[:, 0, :].rearrange("p (h b) -> p h b", h=H), qlat[:, :, SEQ:NT], over(ckv[:, SEQ:NT], *three),
                   ALU.mult, "snew_products")
                tt(stat[:, 1, :].rearrange("p (h b) -> p h b", h=H), qr_group[:, 0, :, :], over(kr[:, SEQ:NT], *three),
                   ALU.mult, "snew_products")
                dve.wait_ge(*signal("snew_ready").at(1))
                copy(s_new.rearrange("p a b -> p (a b)"), bank[6][:, 0:64])

                units = [(0, 0, 4), (0, 4, 4)] + [(1, h, 2) for h in range(0, H, 2)]

                def less_max(u):
                    qt, _, nh = units[u]
                    n = (qt + 1) * P
                    pr = prob[:, u % 2, :].rearrange("p (h k) -> p h k", h=nh)
                    ps = bank[u % 2][:, 0:512].rearrange("p (h k) -> p h k", h=nh)
                    dve.wait_ge(*signal("score_ready").at(u + 1))
                    if u >= 2:
                        dve.wait_ge(*signal("prob_t_ready").at(u - 1))
                    if qt:
                        copy(pr[:, :, 0:P], ps[:, :, 0:P])
                    tt(pr[:, :, n - P:n], ps[:, :, n - P:n], over(c("causal"), P, nh, P), ALU.add, "score_out")
                    largest(stat[:, 8, 0:nh], pr)
                    tt(pr, pr, last_dim(stat[:, 8, 0:nh], P, nh, n), ALU.subtract, "score_less_max")

                less_max(0)
                for u in range(len(units)):
                    if u + 1 < len(units):
                        less_max(u + 1)
                    qt, _, nh = units[u]
                    n = (qt + 1) * P
                    pr = prob[:, u % 2, :].rearrange("p (h k) -> p h k", h=nh)
                    dve.wait_ge(*signal("exp_ready").at(u + 1))
                    total(stat[:, 9, 0:nh], pr)
                    chain(nc.vector.reciprocal(stat[:, 9, 0:nh], stat[:, 9, 0:nh]))
                    tt(pr, pr, last_dim(stat[:, 9, 0:nh], P, nh, n), ALU.mult, "prob_ready")

                def turned(b):
                    dve.wait_ge(*signal("turned").at(5 * b + 2))
                    if b:
                        dve.wait_ge(*signal("s_ready").at(b))
                    for n in (0, 1):
                        copy(ckv_t[:, 4 * n:4 * n + 4, :].rearrange("p a b -> p (a b)"), bank[n][:, 0:512],
                             "past_t_dve")

                by_head = s_sc.rearrange("p j h -> p h j")
                turned(0)
                for b in range(NS):
                    dve.wait_ge(*signal("s_ready").at(b + 1))
                    copy(s_sc.rearrange("p a b -> p (a b)"), bank[5][:, 0:JS * H], "s_out")
                    largest(stat[:, 2, 0:H], by_head)
                    tt(stat[:, 2, 0:H], stat[:, 2, 0:H], s_new[:, :, b], ALU.max, "smax_rows")
                    if b + 1 < NS:
                        turned(b + 1)
                    dve.wait_ge(*signal("smax_turned").at(b + 1))
                    largest(stat[0:H, 3, 0:1], bank[6][0:H, 0:P])
                    ts(stat[0:H, 4, 0:H], ident[0:H, 0:H], stat[0:H, 3, 0:1], ALU.mult, done="smax_diag")
                    dve.wait_ge(*signal("smax_all").at(b + 1))
                    tt(stat[:, 7, 0:H], s_new[:, :, b], bank[6][:, P:P + H], ALU.subtract)
                    tt(s_sc, s_sc, over(bank[6][:, P:P + H], P, JS, H), ALU.subtract, "s_less_max")
                    dve.wait_ge(*signal("s_exp_ready").at(b + 1))
                    total(stat[:, 5, 0:H], s_pr.rearrange("p j h -> p h j"), "ssum_rows")
                    ts(stat[:, 8, 0:H], stat[:, 7, 0:H], ckv[:, SEQ + b:SEQ + b + 1], ALU.mult)
                    dve.wait_ge(*signal("ssum_ready").at(b + 1))
                    tt(stat[:, 6, 0:H], stat[:, 7, 0:H], bank[6][:, 256:256 + H], ALU.add)
                    chain(nc.vector.reciprocal(stat[:, 6, 0:H], stat[:, 6, 0:H]))
                    dve.wait_ge(*signal("pv_ready").at(b + 1))
                    tt(stat[:, 8, 0:H], stat[:, 8, 0:H], bank[7][:, 0:H], ALU.add)
                    tt(olat[:, :, SEQ + b], stat[:, 8, 0:H], stat[:, 6, 0:H], ALU.mult, "sample_out")

            def rwkv():
                rr, kc, vv = p[:, 0:NJ, :], p[:, NJ:2 * NJ, :], p[:, 2 * NJ:3 * NJ, :]
                dve.wait_ge(*signal("omla_out").at(NJ))
                dve.wait_ge(*signal("stored").at(3))
                for j in range(NJ):
                    ts(kk[:, j, :], kc[:, j, :], v("k_k", j), ALU.mult, done="kk_raw" if j == NJ - 1 else None)
                dve.wait_ge(*signal("wa_out").at(1))
                ts(flat(logw), flat(w1), -DECAY_C, ALU.mult, done="logw_ready")
                for j in range(NJ):
                    chain(nc.vector.tensor_tensor_scan(cum[:, j, :], c("keep"), logw[:, j, 0:SEQ], 0.0, ALU.mult,
                                                       ALU.add))
                dve.wait_ge(*signal("kk_norm").at(1))
                for j in range(NJ):
                    ts(w1[:, j, :], bank[j][:, 0:NT], 1e-24, ALU.max)
                root_of_inverse(flat(w1))
                tt(flat(kk), flat(kk), flat(w1), ALU.mult)
                dve.wait_ge(*signal("wa_out").at(2))
                for j in range(NJ):
                    ts(w1[:, j, :], iclr[:, j, :], -1.0, ALU.add, v("k_a", j), ALU.mult)
                stt(flat(kc), flat(w1), 1.0, flat(kc), ALU.add, ALU.mult)
                tt(flat(iclr), flat(iclr), flat(kk), ALU.mult)
                for n, src in ((0, rr), (2, kc), (3, kk), (4, iclr), (5, vv)):
                    copy(sv[:, :, n, :], src[:, :, SEQ:NT])
                dve.wait_ge(*signal("sv_decay").at(1))
                copy(sv[:, :, 0, :], rr[:, :, SEQ:NT], "sv_ready")
                dve.wait_ge(*signal("svb_loaded").at(7))
                dve.wait_ge(*signal("state_loaded").at(1))
                full = [P, 32, HD]

                def by_key(n):
                    return over(svb[:, n, :], *full)

                tt(St, S, by_key(3), ALU.mult)
                total(skk, St)
                tt(S, S, by_key(1), ALU.mult)
                tt(St, last_dim(skk, *full), by_key(4), ALU.mult)
                tt(S, S, St, ALU.subtract)
                tt(St, last_dim(svv, *full), by_key(2), ALU.mult)
                tt(S, S, St, ALU.add, "state_ready")
                tt(St, S, by_key(0), ALU.mult)
                total(so, St, "so_ready")
                dve.wait_ge(*signal("so_turned").at(1))
                copy(oT[:, :, SEQ:NT], bank[5][:, 0:NJ * NS].rearrange("p (a b) -> p a b", a=NJ), "so_out")
                dve.wait_ge(*signal("stored").at(4))
                clear(Z[:, 0, :], "z_cleared")
                for T in range(2):
                    cols = slice(T * P, T * P + P)
                    if T:
                        dve.wait_ge(*signal("rwkv_ready").at(T))
                    tt(dex, cum[:, :, cols], logw[:, :, cols], ALU.subtract, "decays")
                    dve.wait_ge(*signal("decays_ready").at(T + 1))
                    tt(AR[:, :, 0, :], kk[:, :, cols], dex, ALU.mult)
                    tt(AR[:, :, 1, :], rr[:, :, cols], din, ALU.mult)
                    tt(Bt, iclr[:, :, cols], dinv, ALU.mult)
                    tt(Kt, kc[:, :, cols], dinv, ALU.mult, "operands_ready")
                    for i in range(4):
                        dve.wait_ge(*signal("pairs_ready").at(10 * T + i + 1))
                        tt(MR_b[:, 2 * i:2 * i + 2, :], bank[4 + i][:, 0:512].rearrange("p (h n) -> p h n", h=2),
                           over(c("mb"), P, 2, 2 * P), ALU.mult, "mb_out")
                    for i in range(4):
                        dve.wait_ge(*signal("pairs_ready").at(10 * T + i + 5))
                        tt(MR_k[:, 2 * i:2 * i + 2, :], bank[i][:, 0:512].rearrange("p (h n) -> p h n", h=2),
                           over(c("mk"), P, 2, 2 * P), ALU.mult, "mk_out")
                    four = [P, 4, P]
                    for g in range(2):
                        hs = slice(4 * g, 4 * g + 4)
                        dve.wait_ge(*signal("pairs_ready").at(10 * T + g + 9))
                        tt(X[:, hs, :], bank[4 + g][:, 0:512].rearrange("p (h n) -> p h n", h=4),
                           over(c("neg0"), *four), ALU.mult)
                        tt(X[:, hs, :], X[:, hs, :], over(ident, *four), ALU.add)
                        tt(XT[:, hs, :], MR_b[:, hs, 0:P], over(c("lvl")[:, 0:P], *four), ALU.mult)
                        tt(XT[:, hs, :], XT[:, hs, :], over(ident, *four), ALU.add, "x_out")
                    for n in range(1, LEVELS):
                        for g in range(2):
                            hs = slice(4 * g, 4 * g + 4)
                            dve.wait_ge(*signal("xy_ready").at(2 * (T * (LEVELS - 1) + n - 1) + g + 1))
                            if n < LEVELS - 1:
                                tt(flat(X[:, hs, :]), flat(X[:, hs, :]), bank[2 + g][:, 0:512], ALU.subtract)
                            tt(flat(XT[:, hs, :]), flat(XT[:, hs, :]), bank[4 + g][:, 0:512], ALU.subtract, "x_out")
                    dve.wait_ge(*signal("y0_out").at(T + 1))
                    for cc in range(2):
                        n, o0 = 2 * T + cc, CHUNK * cc
                        tt(dcm, over(c("blk"), P, NJ, P),
                           din[:, :, o0 + CHUNK - 1:o0 + CHUNK].broadcast_to([P, NJ, P]), ALU.mult)
                        dve.wait_ge(*signal("u_ready").at(n + 1))
                        tt(U[o0:o0 + CHUNK, :], bank[0][o0:o0 + CHUNK, 0:512], Y0[o0:o0 + CHUNK, :], ALU.add, "u_out")
                        dve.wait_ge(*signal("z_ready").at(n + 1))
                        tt(Z[:, (n + 1) % 3, :], Z[:, n % 3, :], bank[1][:, 0:512], ALU.add)
                        tt(Z[:, (n + 1) % 3, :], Z[:, (n + 1) % 3, :], flat(dcm), ALU.mult, "z_out")
                dve.wait_ge(*signal("rwkv_out").at(2))
                tt(flat(e1), flat(rr), flat(kc), ALU.mult)
                for j in range(NJ):
                    ts(e1[:, j, :], e1[:, j, :], v("r_k", j), ALU.mult, done="rkr_ready" if j == NJ - 1 else None)
                dve.wait_ge(*signal("gn_mean").at(1))
                for j in range(NJ):
                    stt(oT[:, j, :], bank[j][:, 0:NT], -1.0 / HD, oT[:, j, :], ALU.mult, ALU.add,
                        "centred" if j == NJ - 1 else None)
                dve.wait_ge(*signal("bonus_ready").at(1))
                for j in range(NJ):
                    tt(bonus[:, j, :], bank[4 + j][:, 0:NT], vv[:, j, :], ALU.mult,
                       "bonus_out" if j == NJ - 1 else None)
                dve.wait_ge(*signal("gn_var").at(1))
                for j in range(NJ):
                    ts(e2[:, j, :], bank[j][:, 0:NT], 1.0 / HD, ALU.mult, GN_EPS, ALU.add)
                root_of_inverse(flat(e2))
                tt(flat(oT), flat(oT), flat(e2), ALU.mult)
                for j in range(NJ):
                    ts(oT[:, j, :], oT[:, j, :], v("gn_w", j), ALU.mult, v("gn_b", j), ALU.add)
                tt(flat(oT), flat(oT), flat(bonus), ALU.add)
                dve.wait_ge(*signal("gate_out").at(1))
                tt(flat(oT), flat(oT), flat(gate), ALU.mult, "rwkv_mixed")
                for n in range(KD):
                    dve.wait_ge(*signal("mix_ready").at(n + 1))
                    tt(xT[:, n, :], xT[:, n, :], bank[n % 4][:, 0:NT], ALU.add, "mix_added")

            def cross():
                dve.wait_ge(*signal("stored").at(5))
                norm(3, lambda k: v("mem", k), memg, memg, "memg_ready", NM)
                for n in range(8):
                    dve.wait_ge(*signal("v_ready").at(n + 1))
                    copy(V[:, n % 2, (n // 2) * 256:(n // 2) * 256 + 256], bank[4 + n % 2][:, 0:256], "v_out")
                norm(4, lambda k: v("cross", k), xT, hT, "h_ready")

                def less_max(u):
                    ps = bank[4 + u % 2][:, 0:512].rearrange("p (h k) -> p h k", h=2)
                    pr = m_prob[:, u, :].rearrange("p (h k) -> p h k", h=2)
                    dve.wait_ge(*signal("m_score_ready").at(u + 1))
                    largest(m_st[:, 6, 0:2], ps)
                    tt(pr, ps, last_dim(m_st[:, 6, 0:2], P, 2, NM), ALU.subtract, "m_less_max")

                less_max(0)
                for u in range(4):
                    if u + 1 < 4:
                        less_max(u + 1)
                    pr = m_prob[:, u, :].rearrange("p (h k) -> p h k", h=2)
                    dve.wait_ge(*signal("m_exp_ready").at(u + 1))
                    total(m_st[:, 7, 0:2], pr)
                    chain(nc.vector.reciprocal(m_st[:, 7, 0:2], m_st[:, 7, 0:2]))
                    tt(pr, pr, last_dim(m_st[:, 7, 0:2], P, 2, NM), ALU.mult, "m_prob_ready")

                def bh(n):
                    return m_st[:, n, :].rearrange("p (b h) -> p b h", b=NS)

                sc = bank[3][:, 0:NS * 2 * MH].rearrange("p (b m h) -> p b m h", b=NS, m=2)
                dve.wait_ge(*signal("mem_k_used").at(NS))
                chain(nc.vector.tensor_reduce(bh(0), sc.rearrange("p b m h -> p b h m"), AX.X, ALU.max),
                      signal("mmax_rows"))
                dve.wait_ge(*signal("mmax_turned").at(1))
                largest(m_st[0:32, 1, 0:1], bank[4][0:32, 0:P])
                ts(m_st[0:32, 2, :], ident[0:32, 0:32], m_st[0:32, 1, 0:1], ALU.mult, done="mmax_diag")
                dve.wait_ge(*signal("mmax_all").at(1))
                copy(m_st[:, 4, :], bank[4][:, P:P + 32])
                for m in range(2):
                    tt(m_sc[:, :, m, :], sc[:, :, m, :], bh(4), ALU.subtract, "ms_less_max" if m else None)
                dve.wait_ge(*signal("ms_exp_ready").at(1))
                tt(bh(3), m_sc[:, :, 0, :], m_sc[:, :, 1, :], ALU.add, "msum_rows")
                dve.wait_ge(*signal("msum_ready").at(1))
                chain(nc.vector.reciprocal(m_st[:, 5, :], bank[4][:, 256:288]))
                for m in range(2):
                    tt(m_sc[:, :, m, :], m_sc[:, :, m, :], bh(5), ALU.mult, "ms_prob_ready" if m else None)
                for n in range(KD):
                    dve.wait_ge(*signal("cross_ready").at(n + 1))
                    tt(xT[:, n, :], xT[:, n, :], bank[n % 4][:, 0:NT], ALU.add, "cross_added")

            where["phase"] = "before"
            chain(nc.vector.memset(ones[:], 1.0), signal("ones_ready"))
            dve.wait_ge(*signal("index_loaded").at(2))
            ts(rows_idx[:], rows_idx[:], PER, ALU.mult)
            tt(rows_idx[:], rows_idx[:], part_idx[:], ALU.add, "index_ready")
            dve.wait_ge(*signal("inputs_loaded").at(3))
            keep_register(dve)
            for name in 'hidden_ready0 hidden_ready1 ffn_added0 ffn_added1 mix_added cross_added'.split():
                signal(name).grant(dve)
            where["phase"] = "layer"
            with dve.Fori(0, DEPTH) as layer:
                where["layer"] = layer
                copy(vec[:], vectors[:, bass.ds(layer * NV, NV)])
                norm(1, lambda k: v("ffn1", k), xT, hT, "h_ready")
                ffn(0)
                norm(2, lambda k: v("mix", k), xT, hT, "h_ready")
                mixing()
                ts(rows_idx[:], rows_idx[:], t["cache_ckv"].shape[1] * PER, ALU.add, done="index_ready")
                rwkv()
                cross()
                norm(5, lambda k: v("ffn2", k), xT, hT, "h_ready")
                dve.wait_ge(*signal("stored").at(7))
                ffn(1)
            use_register(dve)
            where["phase"] = "after"
            norm(1, lambda k: vectors[:, DEPTH * NV + k:DEPTH * NV + k + 1], xT, hT, "final_ready")

    return ({name: (s.count["before"], s.count["layer"]) for name, s in signals.items()}
            | {name: m.place for name, m in milestones.items()})


def lay_out_constants():
    con = np.zeros((P, NC_), np.float32)

    def put(name, a):
        at, n = CON[name]
        con[:, at:at + n] = a.reshape(P, n)

    i = np.arange(P)
    row, col = i[:, None], i[None, :]
    put("ident", np.eye(P))
    put("blk", (row // HD == col // HD).astype(np.float32))
    rot = np.where((row == col + 16) & (col % 32 < 16), -1.0, 0.0) + np.where((row == col - 16) & (col % 32 >= 16), 1.0, 0.0)
    put("rot", rot)
    put("sel", np.stack([(row == 32 * g + col % 32) for g in range(4)], 1).astype(np.float32))
    pos = np.concatenate([np.arange(SEQ), np.full(NS, PAST)]).astype(np.float32)
    inv = np.float32(10000.0) ** (-np.arange(16, dtype=np.float32) / np.float32(16))
    ang = pos[None, :] * inv[i % 16][:, None]
    put("cos", np.cos(ang))
    put("sin", np.sin(ang))
    put("causal", np.where(col <= row, 0.0, NEG))
    same = row // CHUNK == col // CHUNK
    strict, incl = same & (row < col), same & (row <= col)
    put("mk", np.stack([strict, incl], 1).astype(np.float32))
    put("mb", np.stack([strict * 1.0, incl * -1.0], 1))

    def level(s, t, n):
        return (s // (2 << n) == t // (2 << n)) & (s // (1 << n) % 2 == 0) & (t // (1 << n) % 2 == 1)

    lvl = [level(row, col, n) * (-1.0 if n == 0 else 1.0) for n in range(LEVELS)]
    put("lvl", np.stack(lvl, 1))
    put("neg0", level(col, row, 0) * -1.0)
    put("keep", np.broadcast_to(np.arange(SEQ) % CHUNK != 0, (P, SEQ)).astype(np.float32))
    return con


def kernel(**inputs):
    import concourse.bacc as bacc
    from concourse.bass_utils import run_bass_kernel_spmd

    a = {k: np.asarray(v) for k, v in inputs.items()}
    L = DEPTH

    def cols(w, n):
        _, k, m = w.shape
        return w.reshape(L, k // P, P, m // n, n).transpose(0, 3, 2, 1, 4)

    def rows(v):
        return v.reshape(L, -1, P).transpose(0, 2, 1)

    arrays = {"constants": lay_out_constants()}
    for f in ("ffn1", "ffn2"):
        arrays[f"{f}_gu"] = np.stack([cols(a[f"{f}_w_gate"], P), cols(a[f"{f}_w_up"], P)], 3)
        arrays[f"{f}_down"] = cols(a[f"{f}_w_down"], P)
    w_in = a["w_in"]
    q0 = RW * P
    w_in = np.concatenate([w_in[:, :, q0:q0 + QT * P + CL]] + [w_in[:, :, q0 + QT * P + CL:]] * 4
                          + [w_in[:, :, q0 - 2 * P:q0], w_in[:, :, :q0 - 2 * P]], 2)

    def pairs(w):
        t = cols(w, P)
        return t.reshape(L, t.shape[1] // 2, 2, P, KD, P).transpose(0, 1, 3, 2, 4, 5).reshape(L, -1, P, 2 * D)

    arrays["blocks"] = np.concatenate([pairs(w_in), pairs(a["w_out"]), pairs(a["mem_w_k"]),
                                       cols(a["mem_w_v"], 2 * P).reshape(L, -1, P, 2 * D),
                                       pairs(a["mem_w_q"]), pairs(a["mem_w_o"])], 1)
    uq = a["mla_w_uq"].reshape(L, QT, P, H, NOPE + ROPE).transpose(0, 2, 1, 3, 4)
    uk = a["mla_w_uk"].transpose(0, 2, 3, 1).reshape(L, NJ, P, CL).transpose(0, 2, 1, 3)
    arrays["small"] = np.concatenate(
        [x.reshape(L, P, -1) for x in (uq[..., :NOPE], uq[..., NOPE:], uk, a["mla_w_uv"],
                                       np.concatenate([a["rwkv_w_up"], a["rwkv_a_up"]], 1), a["rwkv_g_up"])], 2)
    vec = np.concatenate([rows(v) for v in (
        a["norm_ffn1"], a["norm_mix"], a["norm_cross"], a["norm_ffn2"], a["norm_mem"], a["shift_mu"], a["rwkv_w0"],
        a["rwkv_a0"], a["rwkv_k_k"], a["rwkv_k_a"], a["rwkv_r_k"].reshape(L, -1), a["rwkv_gn_w"], a["rwkv_gn_b"],
        a["mla_q_norm"], a["mla_kv_norm"])], 2)
    arrays["vectors"] = np.concatenate([vec[0], vec[1], a["norm_final"].reshape(KD, P).T], 1)
    x = np.concatenate([a["x_prompt"][0], a["x_sample"][:, 0]], 0)
    arrays["x"] = x.T.reshape(KD, P, NT).transpose(1, 0, 2)
    arrays["mem"] = a["mem_prompt"][0].T.reshape(KD, P, NM).transpose(1, 0, 2)
    arrays["shift0"] = a["state_shift"].reshape(L, NS, RW, P).transpose(0, 3, 2, 1)
    arrays["cache_ckv"] = a["cache_ckv"]
    arrays["cache_krope"] = a["cache_krope"]
    arrays["state_wkv"] = a["state_wkv"]
    arrays["mem_k"] = a["cache_mem_k"].reshape(L, NS, NM, KD, P).transpose(0, 1, 4, 3, 2)
    arrays["mem_v"] = a["cache_mem_v"].reshape(L, NS, 2, P, D).transpose(0, 1, 3, 2, 4)
    arrays["pages"] = np.repeat(a["page_table"].T, PER, axis=0)
    arrays["page_part"] = np.repeat((np.arange(P, dtype=np.int32) % PER)[:, None], NS, axis=1)
    arrays = {k: np.ascontiguousarray(v) for k, v in arrays.items()}
    outs = {"y": (P, KD, NT), "o_ckv": (L, P, NT), "o_krope": (L, ROPE, NT), "o_wkv": (L, P, NJ, P),
            "o_shift": (L, P, RW, NS + 1), "o_mem_k": (L, P, KD, NM), "o_mem_v": (L, P, 2, D),
            "o_wkv_s": (L, P, 32 * HD)}

    totals = {}
    for _ in range(2):
        nc = bacc.Bacc("TRN2", target_bir_lowering=False, num_devices=1)
        t = {k: nc.dram_tensor(f"in_{k}", v.shape, mybir.dt.from_np(v.dtype), kind="ExternalInput").ap()
             for k, v in arrays.items()}
        t.update({k: nc.dram_tensor(f"out_{k}", s, F32, kind="ExternalOutput").ap() for k, s in outs.items()})
        totals = build(nc, t, totals)
    r = run_bass_kernel_spmd(nc, [{f"in_{k}": x for k, x in arrays.items()}], core_ids=[0]).results[0]
    got = {k: r[f"out_{k}"] for k in outs}

    y = got["y"].transpose(2, 1, 0).reshape(NT, D)
    ckv, kr = got["o_ckv"].transpose(0, 2, 1), got["o_krope"].transpose(0, 2, 1)
    wkv = np.stack([got["o_wkv"][:, HD * (h % 2):HD * (h % 2) + HD, h // 2, HD * (h % 2):HD * (h % 2) + HD]
                    for h in range(H)], 1).transpose(0, 1, 3, 2)[:, None]
    shift = got["o_shift"].transpose(0, 3, 2, 1).reshape(L, NS + 1, RW * P)
    mem_k = got["o_mem_k"].transpose(0, 3, 2, 1).reshape(L, 1, NM, MH, MD)
    mem_v = got["o_mem_v"].transpose(0, 2, 1, 3).reshape(L, 1, NM, MH, MD)
    out = (y[None, :SEQ], y[SEQ:, None], ckv[:, None, :SEQ], kr[:, None, :SEQ], wkv, shift[:, None, 0],
           mem_k, mem_v, ckv[:, SEQ:, None], kr[:, SEQ:, None], got["o_wkv_s"].reshape(L, NS, H, HD, HD),
           shift[:, 1:])
    return tuple(np.ascontiguousarray(o) for o in out)
```

```python
from contextlib import ExitStack

import numpy as np

import concourse.bass as bass
from concourse import mybir

ALU = mybir.AluOpType
ACT = mybir.ActivationFunctionType
AX = mybir.AxisListType
F32 = mybir.dt.float32
I32 = mybir.dt.int32

P = 128
DEPTH, D, SEQ, NS = 2, 1024, 256, 8
NT = SEQ + NS
KD = D // P
FF = 2816
KF = FF // P
H, HD = 8, 64
NJ = H // 2
RW = 14
NOPE, ROPE, CL = 64, 32, 128
QT = 2
PAST, PAGE = 2048, 128
JS = PAST // P
PER = 8
CHUNK = 64
LEVELS = 6
MH, MD, NM = 4, 256, 256
MLA_SCALE = (NOPE + ROPE) ** -0.5
MEM_SCALE = MD ** -0.5
RMS_EPS, GN_EPS = 1e-6, 64e-5
DECAY_C = float(np.exp(-0.5))
NEG = -1e30

VEC = {}
for _name, _tiles in (("ffn1", 8), ("mix", 8), ("cross", 8), ("ffn2", 8), ("mem", 8), ("mu", 14), ("w0", 4),
                      ("a0", 4), ("k_k", 4), ("k_a", 4), ("r_k", 4), ("gn_w", 4), ("gn_b", 4), ("q_norm", 2),
                      ("kv_norm", 1)):
    VEC[_name] = (sum(t for _, t in VEC.values()), _tiles)
NV = sum(t for _, t in VEC.values())

CON = {}
for _name, _cols in (("ident", P), ("blk", P), ("rot", P), ("sel", 4 * P), ("cos", NT), ("sin", NT),
                     ("causal", P), ("mk", 2 * P), ("mb", 2 * P), ("lvl", LEVELS * P), ("neg0", P),
                     ("keep", SEQ)):
    CON[_name] = (sum(t for _, t in CON.values()), _cols)
NC_ = sum(t for _, t in CON.values())

SW = {}
for _name, _cols in (("uq_nope", QT * NJ * P), ("uq_rope", QT * 2 * P), ("uk", NJ * CL), ("uv", H * HD),
                     ("wa_up", H * HD), ("g_up", H * HD)):
    SW[_name] = (sum(t for _, t in SW.values()), _cols)
NSW = sum(t for _, t in SW.values())

C_IN, C_OUT, C_MEMK, C_Q, C_MEMV, C_O = 0, 9, 13, 17, 21, 25
C_BLOCKS = 29
C_SLOTS = 2


class Signal:

    def __init__(self, name, sem, total, where, unit):
        self.name, self.sem, self.unit, self.where = name, sem, unit, where
        self.base, self.per = total
        self.count = {"before": 0, "layer": 0, "after": 0}

    def by(self, instruction, times=1):
        instruction.then_inc(self.sem, self.unit)
        self.count[self.where["phase"]] += times

    def grant(self, engine):
        engine.sem_inc(self.sem, self.unit)
        self.count["before"] += 1

    def at(self, k):
        phase = self.where["phase"]
        if phase == "before":
            return self.sem, self.unit * k
        if phase == "after":
            return self.sem, self.unit * (self.base + DEPTH * self.per + k)
        return self.sem, self.where["layer"] * (self.unit * self.per) + (k + self.base) * self.unit


class Milestone:

    def __init__(self, shared, place):
        self.shared, self.place = shared, place

    def by(self, instruction):
        self.shared.by(instruction)
        self.place = self.shared.count["layer"]

    def at(self, k):
        return self.shared.at(self.place)


MILESTONES = {
    "tensor_milestones": "ckv_turned qs_ready snew_ready kk_norm sv_turned so_turned gn_mean bonus_ready gn_var "
                         "gate_up",
    "vector_milestones": "cq_ready ckv_ready kr_ready qs_out kk_raw logw_ready sv_ready state_ready so_ready so_out "
                         "z_cleared rkr_ready centred bonus_out rwkv_mixed memg_ready ms_less_max "
                         "ms_prob_ready",
    "scalar_milestones": "kk_squared sv_decay sv_tok_ready gd_ready gn_squared gate_out ms_exp_ready",
}
MILESTONE_OF = {name: shared for shared, names in MILESTONES.items() for name in names.split()}


class Chain:

    def __init__(self, engine, done):
        self.engine, self.done = engine, done

    def __call__(self, instruction, signal=None):
        signal = signal or self.done
        signal.by(instruction)
        events = 1 if isinstance(signal, Milestone) else signal.count[signal.where["phase"]]
        self.engine.wait_ge(*signal.at(events))


class Region:

    def __init__(self, tensor, start, end):
        self.tensor, self.at, self.end = tensor, start, end

    def take(self, *dims, parts=P):
        n = int(np.prod(dims))
        assert self.at + n <= self.end, (self.at, n, self.end)
        ap = self.tensor[0:parts, self.at:self.at + n]
        self.at += n
        if len(dims) > 1:
            names = "abcd"[:len(dims)]
            ap = ap.rearrange(f"p ({' '.join(names)}) -> p {' '.join(names)}",
                              **{x: d for x, d in zip(names[1:], dims[1:])})
        return ap


def build(nc, t, totals):
    ctx = ExitStack()
    where = {"phase": "before", "layer": 0}
    signals, milestones = {}, {}

    def signal(name):
        if name in MILESTONE_OF:
            if name not in milestones:
                milestones[name] = Milestone(signal(MILESTONE_OF[name]), totals.get(name, 1))
            return milestones[name]
        if name not in signals:
            unit = 16 if "loaded" in name or "spread" in name or name == "stored" else 1
            signals[name] = Signal(name, ctx.enter_context(nc.semaphore(name)), totals.get(name, (0, 0)), where, unit)
        return signals[name]

    def sbuf(name, shape, dtype=F32):
        return ctx.enter_context(nc.sbuf_tensor(name, shape, dtype))

    with ctx:
        ctx.enter_context(nc.allow_non_contiguous_dma("small strided pieces"))
        bank = [ctx.enter_context(nc.psum_tensor(f"bank{i}", [P, 512], F32)) for i in range(8)]
        con = sbuf("con", [P, NC_])
        vectors = sbuf("vectors", [P, DEPTH * NV + KD])
        vec = sbuf("vec", [P, NV])
        ones = sbuf("ones", [P, P])
        xT = sbuf("xT", [P, KD, NT])
        hT = sbuf("hT", [P, KD, NT])
        sq = sbuf("sq", [P, KD, NT])
        rstd = sbuf("rstd", [P, NT])
        ring_a = sbuf("ring_a", [P, 2, 2, KD, P])
        ring_b = sbuf("ring_b", [P, 2, KF, P])
        ring_c = sbuf("ring_c", [P, C_SLOTS, 2 * D])
        shift0 = sbuf("shift0", [P, RW, NS])
        small = sbuf("small", [P, NSW])
        rows_idx = sbuf("rows_idx", [P, NS], I32)
        part_idx = sbuf("part_idx", [P, NS], I32)
        ARENA = 25140
        arena = sbuf("arena", [P, ARENA])
        vec_dram = nc.dram_tensor("sample_vectors", (6, NS, H * HD), F32, kind="Internal").ap()
        out_dram = nc.dram_tensor("sample_outputs", (NS, H * HD), F32, kind="Internal").ap()

        def c(name, *dims):
            at, n = CON[name]
            ap = con[:, at:at + n]
            return ap if not dims else ap.rearrange("p (a b) -> p a b", a=dims[0])

        def v(name, k=0):
            at, _ = VEC[name]
            return vec[:, at + k:at + k + 1]

        def sw(name, **dims):
            at, n = SW[name]
            ap = small[:, at:at + n]
            return ap.rearrange(f"p ({' '.join(dims)}) -> p {' '.join(dims)}", **dims) if dims else ap

        ident = c("ident")

        r = Region(arena, 0, ARENA)
        hidden = r.take(KF, NT)
        silu = r.take(2, NT)

        r = Region(arena, 0, ARENA)
        p = r.take(RW, NT)
        MIX = r.at
        r = Region(arena, MIX, ARENA)
        rows1 = r.at
        ptmp = r.take(2, NT + 1)
        diff = r.take(NT)
        cq = r.take(QT, NT)
        kr_raw = r.take(NT)
        qr = r.take(2, NT)
        past2 = r.at
        kr_group = r.take(4, SEQ)
        qn = r.take(NJ, NT)
        qr_raw = r.take(2, NT)
        rows0 = r.at
        prob = r.take(2, 512)
        prob_t = r.take(3, 512)
        shift_out = r.take(RW, NS + 1)
        ckv = r.take(NT)
        kr = r.take(NT)
        qr_group = r.take(4, H, NS)
        qlat = r.take(H, NT)
        olat = r.take(H, NT)
        ckv_tok = r.take(2, CL)
        stat = r.take(10, H)
        ckv_t = r.take(JS, P)
        kr_t = r.take(2, 4 * P)
        s_max = r.take(NS, 5)
        s_stat = r.take(4, NS)
        past_ckv = [r.take(JS * CL), r.take(JS * CL)]
        past_kr = [r.take(JS * ROPE), r.take(JS * ROPE)]
        r = Region(arena, past2, rows0)
        past_ckv.append(r.take(JS * CL))
        past_kr.append(r.take(JS * ROPE))
        r = Region(arena, rows0, rows0 + 5 * 512)
        s_rows = [r.take(PAST)]
        s_pt = r.take(JS, H)
        s_o = r.take(2, CL)
        r = Region(arena, rows1, past2)
        s_rows.append(r.take(PAST))

        r = Region(arena, MIX, ARENA)
        logw = r.take(NJ, NT)
        cum = r.take(NJ, SEQ)
        iclr = r.take(NJ, NT)
        kk = r.take(NJ, NT)
        AR = r.take(NJ, 2, P)
        Bt = r.take(NJ, P)
        Kt = r.take(NJ, P)
        din = r.take(NJ, P)
        tok = r.take(4, 512)
        U = r.take(H * HD)
        Z = r.take(3, NJ * P)
        dcm = r.take(NJ, P)
        wstat = r.take(NT)
        SOLVE = r.at
        MR_b = r.take(H, 2 * P)
        MR_k = r.take(H, 2 * P)
        Ml = r.take(H, P)
        X = r.take(H, P)
        XT = r.take(H, P)
        Y = r.take(H, P)
        G, Y0, WT = Ml.rearrange("p a b -> p (a b)")[:, 0:512], X.rearrange("p a b -> p (a b)")[:, 0:512], Y[:, 0:NJ, :]
        dex, dinv = X[:, 0:NJ, :], X[:, NJ:H, :]
        r = Region(arena, SOLVE, ARENA)
        lora = r.take(2, NT)
        w1 = r.take(NJ, NT)
        w2 = r.take(NJ, NT)
        S = r.take(32, HD)
        St = r.take(32, HD)
        r = Region(arena, MIX + 4 * (NJ * NT), ARENA)
        sv = r.take(NJ, 6, NS)
        sv_tok = r.take(NJ * P)
        svb = r.take(6, HD)
        svv = r.take(32)
        skk = r.take(32)
        so = r.take(32)
        so_tok = r.take(NJ * P)
        assert r.at <= SOLVE
        r = Region(arena, SOLVE, ARENA)
        gate = r.take(NJ, NT)
        bonus = r.take(NJ, NT)
        e1 = r.take(NJ, NT)
        e2 = r.take(NJ, NT)
        mixT = hT

        r = Region(arena, 0, ARENA)
        memg = r.take(KD, NM)
        KT = r.take(KD, NM)
        V = r.take(2, D)
        q = r.take(KD, NT)
        o = r.take(KD, NT)
        m_prob = r.take(4, 512)
        m_prob_t = r.take(MH, 2, SEQ)
        mem_k = r.take(2, KD * NM)
        mem_v = r.take(2, 2 * D)
        m_rows = r.take(NS, NM)
        m_pt = r.take(NS, 2, MH)
        m_st = r.take(8, 8)
        oT = mixT[:, 0:NJ, :]

        def mm(out, lhsT, rhs, start=True, stop=True):
            return nc.tensor.matmul(out, lhsT, rhs, start=start, stop=stop)

        def tp(out, in_, n=P):
            return nc.tensor.transpose(out, in_, ident[0:n, 0:n])

        kept = {}

        def wait_apart(engine, *waits):
            for s, value in waits:
                engine.wait_ge(s, value)
            if engine.engine in kept:
                engine.reg_alu(kept[engine.engine], kept[engine.engine], 16 * 3, ALU.bitwise_and)

        def keep_register(engine):
            kept[engine.engine] = engine.alloc_register("kept")
            engine.reg_mov(kept[engine.engine], 16 * 3)

        def use_register(engine):
            engine.wait_ge(signal("inputs_loaded").sem, engine.snap(kept[engine.engine]))

        block = ctx.enter_context(nc.Block())

        @block.sync
        def _(sp):
            where["phase"] = "before"
            loaded = signal("inputs_loaded")
            loaded.by(sp.dma_start(con[:], t["constants"]))
            loaded.by(sp.dma_start(vectors[:], t["vectors"]))
            loaded.by(sp.dma_start(xT[:], t["x"]))

            def ffn(f, layer):
                gu, down = t[f"ffn{f + 1}_gu"], t[f"ffn{f + 1}_down"]
                with sp.Fori(0, KF // 2) as i:
                    for u in range(2):
                        sp.wait_ge(*signal(f"gu_used{u}").at(f * (KF // 2) + i))
                        signal(f"gu_loaded{u}").by(
                            sp.dma_start(ring_a[:, u], gu[layer, 2 * i + u]), KF // 2)
                with sp.Fori(0, KD // 2) as i:
                    for u in range(2):
                        sp.wait_ge(*signal(f"down_used{u}").at(f * (KD // 2) + i))
                        signal(f"down_loaded{u}").by(
                            sp.dma_start(ring_b[:, u], down[layer, 2 * i + u]), KD // 2)

            def used(n):
                for first, name in ((C_O, "cross_ready"), (C_MEMV, "v_ready"), (C_Q, "mq_ready"),
                                    (C_MEMK, "kt_ready"), (C_OUT, "mix_ready"), (C_IN, "proj_ready")):
                    if n >= first:
                        return signal(name).at(2 * (n - first) + 2)

            def blocks(layer):
                for n in range(C_BLOCKS):
                    sp.wait_ge(*(used(n - C_SLOTS) if n >= C_SLOTS else signal("cross_ready").at(0)))
                    signal(f"block_loaded{n % C_SLOTS}").by(
                        sp.dma_start(ring_c[:, n % C_SLOTS], t["blocks"][layer, n]))

            where["phase"] = "layer"
            with sp.Fori(0, DEPTH) as layer:
                where["layer"] = layer
                ffn(0, layer)
                blocks(layer)
                ffn(1, layer)

        @block.gpsimd
        def _(pool):
            chain = Chain(pool, signal("pool_step"))
            stored = signal("stored")
            where["phase"] = "before"
            signal("index_loaded").by(pool.dma_start(rows_idx[:], t["pages"]))
            signal("index_loaded").by(pool.dma_start(part_idx[:], t["page_part"]))
            ckv_rows = t["cache_ckv"].rearrange("l n (e t) c -> (l n e) (t c)", e=PER)
            kr_rows = t["cache_krope"].rearrange("l n (e t) c -> (l n e) (t c)", e=PER)

            def gather(b):
                at = bass.IndirectOffsetOnAxis(ap=rows_idx[:, b:b + 1], axis=0)
                signal(f"past_loaded{b % 3}").by(pool.indirect_dma_start(past_ckv[b % 3], None, ckv_rows, at))
                signal(f"past_loaded{b % 3}").by(pool.indirect_dma_start(past_kr[b % 3], None, kr_rows, at))

            where["phase"] = "layer"
            keep_register(pool)
            with pool.Fori(0, DEPTH) as layer:
                where["layer"] = layer
                wait_apart(pool, signal("mix_added").at(0),
                           signal("cross_added").at(0))
                signal("small_loaded").by(pool.dma_start(small[:], t["small"][layer]))
                signal("small_loaded").by(pool.dma_start(shift0[:], t["shift0"][layer]))
                wait_apart(pool, signal("index_ready").at(0))
                gather(0)
                gather(1)
                wait_apart(pool, signal("ckv_ready").at(1),
                           signal("kr_ready").at(1))
                stored.by(pool.dma_start(t["o_ckv"][layer], ckv))
                stored.by(pool.dma_start(t["o_krope"][layer], kr[0:ROPE, :]))
                wait_apart(pool, signal("shifted").at(RW))
                stored.by(pool.dma_start(t["o_shift"][layer], shift_out))
                wait_apart(pool, signal("olat_out").at(6))
                gather(2)
                for b in range(3, NS):
                    wait_apart(pool, signal("pv_ready").at(b - 2))
                    gather(b)
                wait_apart(pool, stored.at(3))
                wait_apart(pool, signal("omla_out").at(NJ),
                           signal("sample_out").at(NS))
                signal("state_loaded").by(
                    pool.dma_start(S, t["state_wkv"][layer].rearrange("b h (a v) k -> (b h a) v k", a=2)))
                wait_apart(pool, signal("sv_tok_ready").at(1))
                signal("sv_spread").by(
                    pool.dma_start(vec_dram.rearrange("n b f -> (n b) f"), sv_tok[0:6 * NS, :]))
                wait_apart(pool, signal("sv_spread").at(1))
                for n in range(6):
                    src = vec_dram[n].rearrange("b (h k) -> (b h) k", h=H)
                    src = src.rearrange("p (o k) -> p o k", o=1).broadcast_to([NS * H, 2, HD])
                    signal("svb_loaded").by(pool.dma_start(svb[:, n, :], src))
                signal("svb_loaded").by(
                    pool.dma_start(svv, vec_dram[5].rearrange("b (g v) -> (b g) v", v=32)))
                wait_apart(pool, signal("state_ready").at(1))
                stored.by(pool.dma_start(t["o_wkv_s"][layer], S.rearrange("p a b -> p (a b)")))
                wait_apart(pool, signal("so_ready").at(1))
                signal("so_spread").by(
                    pool.dma_start(out_dram.rearrange("b (g v) -> (b g) v", v=32), so))
                wait_apart(pool, signal("so_spread").at(1))
                signal("so_loaded").by(pool.dma_start(so_tok[0:NS, :], out_dram))
                wait_apart(pool, stored.at(4))
                for T in range(2):
                    for n in range(1, LEVELS):
                        k = T * (LEVELS - 1) + n
                        wait_apart(pool, signal("mb_out").at(4 * T + 4))
                        if n > 1:
                            pool.wait_ge(*signal("y_ready").at(2 * k - 2))
                        for g in range(2):
                            ins = nc.gpsimd.tensor_tensor(
                                Ml[:, 4 * g:4 * g + 4, :], MR_b[:, 4 * g:4 * g + 4, 0:P],
                                c("lvl", LEVELS)[:, n:n + 1, :].broadcast_to([P, 4, P]), ALU.mult)
                            signal("level_ready").by(ins)
                wait_apart(pool, signal("z_out").at(4))
                stored.by(pool.dma_start(t["o_wkv"][layer], Z[:, 1, :].rearrange("p (j v) -> p j v", j=NJ)))
                wait_apart(pool, stored.at(5))
                wait_apart(pool, signal("mix_added").at(KD))
                signal("mem_loaded").by(pool.dma_start(memg, t["mem"]))

                def load_keys(b):
                    if b >= 2:
                        wait_apart(pool, signal("mem_k_used").at(b - 1))
                    signal(f"mem_k_loaded{b % 2}").by(
                        pool.dma_start(mem_k[:, b % 2, :], t["mem_k"][layer, b].rearrange("p a b -> p (a b)")))

                def load_values(b):
                    if b >= 2:
                        wait_apart(pool, signal("mem_v_used").at(b - 1))
                    signal(f"mem_v_loaded{b % 2}").by(
                        pool.dma_start(mem_v[:, b % 2, :], t["mem_v"][layer, b].rearrange("p a b -> p (a b)")))

                for b in range(2):
                    load_keys(b)
                    load_values(b)
                wait_apart(pool, signal("kt_out").at(KD))
                stored.by(pool.dma_start(t["o_mem_k"][layer], KT))
                for b in range(2, NS):
                    load_keys(b)
                wait_apart(pool, signal("v_out").at(8))
                stored.by(pool.dma_start(t["o_mem_v"][layer], V))
                for b in range(2, NS):
                    load_values(b)
                wait_apart(pool, stored.at(7))
            use_register(pool)
            where["phase"] = "after"
            wait_apart(pool, signal("final_ready").at(1))
            stored.by(pool.dma_start(t["y"], hT[:]))
            wait_apart(pool, stored.at(1))

        @block.tensor
        def _(pe):
            def sum_squares(n, into=6):
                pe.wait_ge(*signal("sq_ready").at(n))
                for k in range(KD):
                    last = mm(bank[into][:, 0:NT], ones[:], sq[:, k, :], k == 0, k == KD - 1)
                signal("sumsq_ready").by(last)

            def ffn(f):
                wait_apart(pe, signal("h_ready").at(3 * f + 1))
                with pe.Fori(0, KF // 2) as i:
                    for u in range(2):
                        at = f * (KF // 2) + i
                        pe.wait_ge(*signal(f"gu_loaded{u}").at(at + 1))
                        pe.wait_ge(*signal(f"silu_ready{u}").at(at))
                        for k in range(KD):
                            last = mm(bank[u][:, 0:NT], ring_a[:, u, 0, k, :], hT[:, k, :], k == 0, k == KD - 1)
                        signal(f"gate_ready{u}").by(last, KF // 2)
                        pe.wait_ge(*signal(f"hidden_ready{u}").at(at))
                        for k in range(KD):
                            last = mm(bank[2 + u][:, 0:NT], ring_a[:, u, 1, k, :], hT[:, k, :], k == 0, k == KD - 1)
                        signal(f"gu_used{u}").by(last, KF // 2)
                wait_apart(pe, *(signal(f"hidden_ready{u}").at((f + 1) * (KF // 2)) for u in range(2)))
                with pe.Fori(0, KD // 2) as i:
                    for u in range(2):
                        at = f * (KD // 2) + i
                        pe.wait_ge(*signal(f"down_loaded{u}").at(at + 1))
                        pe.wait_ge(*signal(f"ffn_added{u}").at(at))
                        for k in range(KF):
                            last = mm(bank[4 + u][:, 0:NT], ring_b[:, u, k, :], hidden[:, k, :], k == 0, k == KF - 1)
                        signal(f"down_used{u}").by(last, KD // 2)

            def block_of(n):
                pe.wait_ge(*signal(f"block_loaded{n % C_SLOTS}").at(n // C_SLOTS + 1))
                return ring_c[:, n % C_SLOTS, :]

            def project(first, tile, n, rhs, ready, width=NT):
                blk = first + tile // 2
                if tile % 2 == 0:
                    block_of(blk)
                w = ring_c[:, blk % C_SLOTS, :].rearrange("p (u k n) -> p u k n", u=2, k=KD)
                for k in range(KD):
                    last = mm(bank[n][:, 0:width], w[:, tile % 2, k, :], rhs[:, k, 0:width], k == 0, k == KD - 1)
                signal(ready).by(last)
                return last

            def mixing():
                pe.wait_ge(*signal("h_ready").at(2))
                for n in range(18):
                    if n >= 4:
                        pe.wait_ge(*signal("proj_out").at(n - 3))
                    project(C_IN, n, n % 4, hT, "proj_ready")
                    if n == 5:
                        pe.wait_ge(*signal("mla_sq_ready").at(2))
                        for k in range(QT):
                            last = mm(bank[4][:, 0:NT], ones[:], sq[:, k, :], k == 0, k == QT - 1)
                        signal("mla_sum_ready").by(last)
                        signal("mla_sum_ready").by(mm(bank[5][:, 0:NT], ones[:], sq[:, QT, :]))
                        signal("rot_ready").by(mm(bank[6][:, 0:NT], c("rot"), kr_raw))
                pe.wait_ge(*signal("small_loaded").at(2))
                pe.wait_ge(*signal("cq_ready").at(1))
                pe.wait_ge(*signal("proj_out").at(18))
                un = sw("uq_nope", a=QT, j=NJ, n=P)
                ur = sw("uq_rope", a=QT, j=2, n=P)
                for j in range(NJ):
                    for k in range(QT):
                        last = mm(bank[j][:, 0:NT], un[:, k, j, :], cq[:, k, :], k == 0, k == QT - 1)
                    signal("q_ready").by(last)
                pe.wait_ge(*signal("ckv_ready").at(1))
                for g in range(2):
                    for k in range(QT):
                        last = mm(bank[4 + g][:, 0:NT], ur[:, k, g, :], cq[:, k, :], k == 0, k == QT - 1)
                    signal("q_ready").by(last)
                pe.wait_ge(*signal("kr_ready").at(1))
                for T in range(2):
                    last = tp(bank[6][:, T * P:T * P + P], ckv[:, T * P:T * P + P])
                signal("ckv_turned").by(last)
                for g in range(2):
                    pe.wait_ge(*signal("q_out").at(NJ + g + 1))
                    signal("rot_ready").by(mm(bank[4 + g][:, 0:NT], c("rot"), qr_raw[:, g, :]))
                uk = sw("uk", j=NJ, n=CL)
                for h in range(H):
                    o0 = NOPE * (h % 2)
                    pe.wait_ge(*signal("q_out").at(min(NJ, h // 2 + 1) if h < 4 else NJ))
                    if h >= 4:
                        pe.wait_ge(*signal("qlat_out").at(h - 3))
                    signal("qlat_ready").by(mm(bank[h % 4][:, 0:NT], uk[o0:o0 + NOPE, h // 2, :],
                                               qn[o0:o0 + NOPE, h // 2, :]))
                pe.wait_ge(*signal("qr_ready").at(2))
                sel = c("sel", 4)
                for h in range(H):
                    last = mm(bank[7][:, h * NS:h * NS + NS], sel[:, h % 4, :], qr[:, h // 4, SEQ:NT])
                signal("qs_ready").by(last)
                prompt_attention()
                sample_attention()

                uv = sw("uv")
                pe.wait_ge(*signal("olat_out").at(6))
                pe.wait_ge(*signal("sample_out").at(NS))
                for j in range(NJ):
                    for o0 in (0, 1):
                        h = 2 * j + o0
                        last = mm(bank[j][HD * o0:HD * o0 + HD, 0:NT], uv[:, h * HD:h * HD + HD], olat[:, h, :])
                    signal("omla_ready").by(last)

            def prompt_attention():
                units = [(0, 0, 4), (0, 4, 4)] + [(1, h, 2) for h in range(0, H, 2)]

                def scores(u):
                    qt, h0, nh = units[u]
                    if u >= 2:
                        pe.wait_ge(*signal("score_out").at(u - 1))
                    for i in range(nh):
                        h, n = h0 + i, (qt + 1) * P
                        out = bank[u % 2][:, i * n:i * n + n]
                        mm(out, qlat[:, h, qt * P:qt * P + P], ckv[:, 0:n], True, False)
                        last = mm(out, qr[:, h // 4, qt * P:qt * P + P], kr_group[:, h % 4, 0:n], False, True)
                    signal("score_ready").by(last)

                pe.wait_ge(*signal("qlat_out").at(H))
                scores(0)
                scores(1)
                for u, (qt, h0, nh) in enumerate(units):
                    pe.wait_ge(*signal("prob_ready").at(u + 1))
                    if u >= 2:
                        pe.wait_ge(*signal("prob_t_out").at(u - 1))
                    for i in range(4):
                        last = tp(bank[2 + u % 2][:, i * P:i * P + P], prob[:, u % 2, i * P:i * P + P])
                    signal("prob_t_ready").by(last)
                    if u + 2 < len(units):
                        scores(u + 2)
                    pe.wait_ge(*signal("prob_t_out").at(u + 1))
                    if u >= 2:
                        pe.wait_ge(*signal("olat_out").at(u - 1))
                    rhs = prob_t[:, u % 3, :]
                    if qt == 0:
                        last = mm(bank[4 + u % 2][:, 0:512], ckv_tok[:, 0, :], rhs)
                    else:
                        two = rhs.rearrange("p (h k q) -> p h k q", h=2, k=2)
                        for k in range(2):
                            last = mm(bank[4 + u % 2][:, 0:256], ckv_tok[:, k, :], two[:, :, k, :], k == 0, k == 1)
                    signal("olat_ready").by(last)

            def sample_attention():

                def turn(m):
                    b, n = m // 4, m % 4
                    if n == 0:
                        pe.wait_ge(*signal(f"past_loaded{b % 3}").at(2 * (b // 3) + 2))
                    if m >= 3:
                        pe.wait_ge(*signal("ckv_t_out").at(m - 2))
                    if n == 0:
                        if b:
                            pe.wait_ge(*signal("kr_t_out").at(b))
                        for i in range(4):
                            last = tp(bank[7][:, i * P:i * P + P], past_kr[b % 3][:, i * P:i * P + P])
                        signal("kr_turned").by(last)
                    for i in range(4):
                        j = 4 * n + i
                        last = tp(bank[m % 3][:, i * P:i * P + P], past_ckv[b % 3][:, j * CL:j * CL + CL])
                    signal("turned").by(last)

                def scores(m):
                    b, n = m // 4, m % 4
                    pe.wait_ge(*signal("ckv_t_out").at(m + 1))
                    if n == 0:
                        pe.wait_ge(*signal("kr_t_out").at(b + 1))
                    if m >= 2:
                        pe.wait_ge(*signal("s_rows_out").at(m - 1))
                    out = bank[4 + m % 2]
                    mm(out[0:H, 0:512], qlat[:, :, SEQ + b], ckv_t[:, 4 * n:4 * n + 4, :], True, False)
                    for g in range(4):
                        last = mm(out[0:H, g * P:g * P + P], qr_group[:, g, :, b], kr_t[:, b % 2, n * P:n * P + P], False, g == 3)
                    signal("s_ready").by(last)

                def turn_probabilities(b):
                    wait_apart(pe, signal("s_exp_ready").at(b + 1))
                    if b:
                        wait_apart(pe, signal("pt_out").at(b))
                    for j in range(JS):
                        last = tp(bank[3][:, j * H:j * H + H], s_rows[b % 2][0:H, j * P:j * P + P], H)
                    signal("pt_ready").by(last)

                def values(b):
                    pe.wait_ge(*signal("pt_out").at(b + 1))
                    if b:
                        pe.wait_ge(*signal("sample_out").at(b))
                    mm(bank[6][0:H, P:2 * P], ckv[:, SEQ + b:SEQ + b + 1].broadcast_to([P, H]), ident)
                    for j in range(JS):
                        last = mm(bank[6][0:H, 0:P], s_pt[:, j, :], past_ckv[b % 3][:, j * CL:j * CL + CL],
                                  j == 0, j == JS - 1)
                    signal("pv_ready").by(last)

                def turn_outputs(b):
                    wait_apart(pe, signal("o_rows").at(b + 1))
                    if b:
                        wait_apart(pe, signal("sample_out").at(b))
                    signal("o_turned").by(tp(bank[6][:, 256:256 + H], s_o[0:H, b % 2, :], H))

                pe.wait_ge(*signal("qs_out").at(1))
                pe.wait_ge(*signal("prob_t_out").at(6))
                pe.wait_ge(*signal("olat_out").at(6))
                for b in range(NS):
                    out = bank[6][0:H, 272 + b:273 + b]
                    mm(out, qlat[:, :, SEQ + b], ckv[:, SEQ + b:SEQ + b + 1], True, False)
                    last = mm(out, qr_group[:, 0, :, b], kr[:, SEQ + b:SEQ + b + 1], False, True)
                signal("snew_ready").by(last)
                for m in range(4 * NS + 6):
                    if m < 4 * NS:
                        turn(m)
                    if 0 <= m - 2 < 4 * NS:
                        scores(m - 2)
                    if m >= 7:
                        stage, b = (turn_probabilities, values, turn_outputs, None)[(m - 7) % 4], (m - 7) // 4
                        if stage and b < NS:
                            stage(b)

            def rwkv():
                wa = sw("wa_up")
                pe.wait_ge(*signal("lora_ready").at(2))
                pe.wait_ge(*signal("omla_out").at(NJ))
                for i in range(2):
                    for j in range(NJ):
                        last = mm(bank[4 * i + j][:, 0:NT], wa[64 * i:64 * i + 64, j * P:j * P + P],
                                  lora[64 * i:64 * i + 64, 0, :])
                    signal("wa_ready").by(last)
                pe.wait_ge(*signal("wa_out").at(2))
                pe.wait_ge(*signal("kk_squared").at(1))
                for j in range(NJ):
                    last = mm(bank[j][:, 0:NT], c("blk"), w2[:, j, :])
                signal("kk_norm").by(last)
                wait_apart(pe, signal("sv_ready").at(1))
                for j in range(NJ):
                    last = tp(bank[4][0:6 * NS, j * P:j * P + P], sv[:, j, :, :].rearrange("p n b -> p (n b)"))
                signal("sv_turned").by(last)
                wait_apart(pe, signal("so_loaded").at(1))
                for j in range(NJ):
                    last = tp(bank[5][:, j * NS:j * NS + NS], so_tok[0:NS, j * P:j * P + P], NS)
                signal("so_turned").by(last)
                pe.wait_ge(*signal("so_out").at(1))
                for T in range(2):
                    solve(T)
                    for cc in range(2):
                        chunk(T, cc)
                    outputs(T)
                pe.wait_ge(*signal("rwkv_out").at(2))
                pe.wait_ge(*signal("z_out").at(4))
                for j in range(NJ):
                    last = mm(bank[j][:, 0:NT], c("blk"), oT[:, j, :])
                signal("gn_mean").by(last)
                pe.wait_ge(*signal("rkr_ready").at(1))
                for j in range(NJ):
                    last = mm(bank[4 + j][:, 0:NT], c("blk"), e1[:, j, :])
                signal("bonus_ready").by(last)
                pe.wait_ge(*signal("gn_squared").at(1))
                pe.wait_ge(*signal("centred").at(1))
                for j in range(NJ):
                    last = mm(bank[j][:, 0:NT], c("blk"), e2[:, j, :])
                signal("gn_var").by(last)
                pe.wait_ge(*signal("bonus_out").at(1))
                pe.wait_ge(*signal("gd_ready").at(1))
                for j in range(NJ):
                    last = mm(bank[4 + j][:, 0:NT], sw("g_up")[:, j * P:j * P + P], wstat)
                signal("gate_up").by(last)

            def head(n):
                return 2 * (n % NJ) + n // NJ

            def solve(T):
                pe.wait_ge(*signal("operands_ready").at(T + 1))
                if T:
                    pe.wait_ge(*signal("rwkv_out").at(T))
                turned = [AR[:, :, 0, :], Bt, Kt, p[:, 8:12, T * P:T * P + P]]
                for n, src in enumerate(turned):
                    for j in range(NJ):
                        last = tp(bank[n][:, j * P:j * P + P], src[:, j, :])
                    signal("tok_turned").by(last)
                for n in range(4):
                    for i in range(2):
                        m = 2 * n + i
                        o0, j = HD * (m // NJ), m % NJ
                        last = mm(bank[4 + n][:, 256 * i:256 * i + 256], Bt[o0:o0 + HD, j, :],
                                  AR[o0:o0 + HD, j, :, :])
                    signal("pairs_ready").by(last)
                for n in range(4):
                    pe.wait_ge(*signal("tok_out").at(4 * T + n + 1))
                    for i in range(2):
                        m = 2 * n + i
                        o0, j = HD * (m // NJ), m % NJ
                        last = mm(bank[n][:, 256 * i:256 * i + 256], Kt[o0:o0 + HD, j, :],
                                  AR[o0:o0 + HD, j, :, :])
                    signal("pairs_ready").by(last)
                for g in range(2):
                    pe.wait_ge(*signal("mb_out").at(4 * T + g + 1))
                    for j in range(NJ):
                        last = mm(bank[4 + g][:, j * P:j * P + P], AR[HD * g:HD * g + HD, j, 0, :],
                                  Bt[HD * g:HD * g + HD, j, :])
                    signal("pairs_ready").by(last)
                pe.wait_ge(*signal("mk_out").at(4 * T + 4))
                for n in range(1, LEVELS):
                    for g in range(2):
                        k = 2 * (T * (LEVELS - 1) + n - 1) + g + 1
                        pe.wait_ge(*signal("level_ready").at(k))
                        pe.wait_ge(*signal("x_out").at(k + 2 * T))
                        for i in range(4):
                            m = 4 * g + i
                            last = mm(bank[g][:, i * P:i * P + P], Ml[:, m, :], X[:, m, :])
                        signal("y_ready").by(last)
                    for g in range(2):
                        k = 2 * (T * (LEVELS - 1) + n - 1) + g + 1
                        pe.wait_ge(*signal("y_out").at(k))
                        if n < LEVELS - 1:
                            for i in range(4):
                                m = 4 * g + i
                                mm(bank[2 + g][:, i * P:i * P + P], XT[:, m, :], Y[:, m, :])
                        for i in range(4):
                            m = 4 * g + i
                            last = mm(bank[4 + g][:, i * P:i * P + P], Y[:, m, :], XT[:, m, :])
                        signal("xy_ready").by(last)
                for m in range(H):
                    h = head(m)
                    last = mm(bank[6][:, h * HD:h * HD + HD], MR_k[:, m, 0:P], tok[:, 3, h * HD:h * HD + HD])
                signal("g_ready").by(last)
                pe.wait_ge(*signal("g_out").at(T + 1))
                pe.wait_ge(*signal("x_out").at(2 * (T + 1) * LEVELS))
                for m in range(H):
                    h = head(m)
                    last = mm(bank[7][:, h * HD:h * HD + HD], XT[:, m, :], G[:, h * HD:h * HD + HD])
                signal("y0_ready").by(last)
                for m in range(H):
                    h = head(m)
                    o0 = HD * (h % 2)
                    last = mm(bank[6][o0:o0 + HD, (h // 2) * P:(h // 2) * P + P], tok[:, 0, h * HD:h * HD + HD],
                              XT[:, m, :])
                signal("wt_ready").by(last)

            def chunk(T, cc):
                n, o0 = 2 * T + cc, CHUNK * cc
                if n:
                    pe.wait_ge(*signal("z_out").at(n))
                if cc == 0:
                    pe.wait_ge(*signal("wt_out").at(T + 1))
                if n == 0:
                    pe.wait_ge(*signal("z_cleared").at(1))
                for j in range(NJ):
                    last = mm(bank[0][o0:o0 + CHUNK, j * P:j * P + P], WT[:, j, o0:o0 + CHUNK],
                              Z[:, n % 3, j * P:j * P + P])
                signal("u_ready").by(last)
                pe.wait_ge(*signal("u_out").at(n + 1))
                for j in range(NJ):
                    cols = slice(j * P, j * P + P)
                    mm(bank[1][:, cols], tok[o0:o0 + CHUNK, 1, cols], U[o0:o0 + CHUNK, cols], True, False)
                    last = mm(bank[1][:, cols], tok[o0:o0 + CHUNK, 2, cols], tok[o0:o0 + CHUNK, 3, cols], False, True)
                signal("z_ready").by(last)

            def outputs(T):
                for j in range(NJ):
                    out = bank[2][:, j * P:j * P + P]
                    for cc in range(2):
                        nc.tensor.matmul(out[:, CHUNK * cc:CHUNK * cc + CHUNK], Z[:, (2 * T + cc) % 3, j * P:j * P + P],
                                         AR[:, j, 1, CHUNK * cc:CHUNK * cc + CHUNK], start=cc == 0, stop=False,
                                         skip_group_check=True)
                    for i in range(2):
                        h, m = 2 * j + i, NJ * i + j
                        part = out[HD * i:HD * i + HD, :]
                        nc.tensor.matmul(part, U[:, h * HD:h * HD + HD], MR_b[:, m, P:2 * P], start=False,
                                         stop=False, skip_group_check=True)
                        last = nc.tensor.matmul(part, tok[:, 3, h * HD:h * HD + HD], MR_k[:, m, P:2 * P],
                                                start=False, stop=True, skip_group_check=True)
                signal("rwkv_ready").by(last)

            def mix_out():
                pe.wait_ge(*signal("rwkv_mixed").at(1))
                for n in range(KD):
                    if n >= 4:
                        pe.wait_ge(*signal("mix_added").at(n - 3))
                    project(C_OUT, n, n % 4, mixT, "mix_ready")

            def cross():
                sum_squares(3)
                sum_squares(4, 5)
                pe.wait_ge(*signal("memg_ready").at(1))
                pe.wait_ge(*signal("mix_added").at(KD))
                for n in range(KD):
                    if n >= 4:
                        pe.wait_ge(*signal("kt_out").at(n - 3))
                    project(C_MEMK, n, n % 4, memg, "kt_ready", NM)
                pe.wait_ge(*signal("h_ready").at(3))
                for n in range(KD):
                    pe.wait_ge(*signal("kt_out" if n < 4 else "mq_out").at(KD if n < 4 else n - 3))
                    project(C_Q, n, n % 4, hT, "mq_ready")
                pe.wait_ge(*signal("mq_out").at(KD))
                for n in range(8):
                    b, T = n, n % 2
                    w = (block_of(C_MEMV + n // 2) if T == 0 else w)
                    wv = w.rearrange("p (k n) -> p k n", k=KD)
                    if n >= 2:
                        pe.wait_ge(*signal("v_out").at(n - 1))
                    for k in range(KD):
                        last = mm(bank[4 + T][:, 0:256], memg[:, k, T * P:T * P + P], wv[:, k, :], k == 0, k == KD - 1)
                    signal("v_ready").by(last)
                    pe.wait_ge(*signal(f"mem_k_loaded{b % 2}").at(b // 2 + 1))
                    if b >= 4 and b % 2 == 0:
                        pe.wait_ge(*signal("ms_rows").at(b // 2 - 1))
                    kt_b = mem_k[:, b % 2, :].rearrange("p (k m) -> p k m", k=KD)
                    for h in range(MH):
                        out = bank[6 + b // 2 % 2][32 * h:32 * h + 32, (b % 2) * NM:(b % 2) * NM + NM]
                        for dt in range(2):
                            k = 2 * h + dt
                            last = mm(out, q[:, k, SEQ + b:SEQ + b + 1].broadcast_to([P, 32]), kt_b[:, k, :],
                                      dt == 0, dt == 1)
                    signal("mem_k_used").by(last)
                pe.wait_ge(*signal("v_out").at(8))

                units = [(qt, hp) for hp in range(2) for qt in range(2)]

                def scores(u):
                    qt, hp = units[u]
                    if u >= 2:
                        pe.wait_ge(*signal("m_less_max").at(u - 1))
                    for i in range(2):
                        for dt in range(2):
                            k = 2 * (2 * hp + i) + dt
                            last = mm(bank[4 + u % 2][:, i * NM:i * NM + NM], q[:, k, qt * P:qt * P + P], KT[:, k, :],
                                      dt == 0, dt == 1)
                    signal("m_score_ready").by(last)

                scores(0)
                scores(1)
                pe.wait_ge(*signal("ms_rows").at(4))
                for u in range(4):
                    pe.wait_ge(*signal("m_prob_ready").at(u + 1))
                    if u >= 2:
                        pe.wait_ge(*signal("m_prob_t_out").at(u - 1))
                    for i in range(4):
                        last = tp(bank[6 + u % 2][:, i * P:i * P + P], m_prob[:, u, i * P:i * P + P])
                    signal("m_prob_t_ready").by(last)
                    if u + 2 < 4:
                        scores(u + 2)
                for k in range(KD):
                    pe.wait_ge(*signal("m_prob_t_out").at(2 * (k // 4) + 2))
                    if k >= 2:
                        pe.wait_ge(*signal("mo_out").at(k - 1))
                    for mt in range(2):
                        last = mm(bank[k % 2][:, 0:SEQ], V[:, mt, k * P:k * P + P], m_prob_t[:, k // 2, mt, :],
                                  mt == 0, mt == 1)
                    signal("mo_ready").by(last)
                pe.wait_ge(*signal("ms_prob_ready").at(1))
                pe.wait_ge(*signal("m_less_max").at(4))
                for n in range(4):
                    for i in range(4):
                        b, mt = 2 * n + i // 2, i % 2
                        last = tp(bank[2 + n][:, i * P:i * P + P], m_rows[:, b, mt * P:mt * P + P])
                    signal("m_pt_ready").by(last)
                pe.wait_ge(*signal("m_prob_t_out").at(4))
                for b in range(NS):
                    pe.wait_ge(*signal(f"mem_v_loaded{b % 2}").at(b // 2 + 1))
                    pe.wait_ge(*signal("m_pt_out").at(b // 2 + 1))
                    if b >= 4 and b % 2 == 0:
                        pe.wait_ge(*signal("ms_outputs").at(b // 2 - 1))
                    v_b = mem_v[:, b % 2, :].rearrange("p (m n) -> p m n", m=2)
                    for h in range(MH):
                        out = bank[6 + b // 2 % 2][32 * h:32 * h + 32, (b % 2) * MD:(b % 2) * MD + MD]
                        for mt in range(2):
                            last = mm(out, m_pt[:, b, mt, h:h + 1].broadcast_to([P, 32]),
                                      v_b[:, mt, h * MD:h * MD + MD], mt == 0, mt == 1)
                    signal("mem_v_used").by(last)
                for n in range(4):
                    pe.wait_ge(*signal("ms_outputs").at(n + 1))
                    for i in range(4):
                        b, dt = 2 * n + i // 2, i % 2
                        last = tp(bank[2 + n][:, i * P:i * P + P], m_rows[:, b, dt * P:dt * P + P])
                    signal("mo_turned").by(last)
                pe.wait_ge(*signal("mo_out").at(KD + 4))
                for n in range(KD):
                    if n >= 4:
                        pe.wait_ge(*signal("cross_added").at(n - 3))
                    project(C_O, n, n % 4, o, "cross_ready")

            where["phase"] = "before"
            pe.wait_ge(*signal("inputs_loaded").at(3))
            pe.wait_ge(*signal("ones_ready").at(1))
            keep_register(pe)
            for name in 'gu_used0 gu_used1 down_used0 down_used1 cross_ready'.split():
                signal(name).grant(pe)
            where["phase"] = "layer"
            with pe.Fori(0, DEPTH) as layer:
                where["layer"] = layer
                sum_squares(1)
                ffn(0)
                sum_squares(2)
                mixing()
                rwkv()
                mix_out()
                cross()
                sum_squares(5)
                ffn(1)
            use_register(pe)
            where["phase"] = "after"
            sum_squares(1)

        @block.scalar
        def _(act):
            chain = Chain(act, signal("act_step"))

            def run(out, in_, func=ACT.Copy, done=None, **more):
                chain(nc.scalar.activation(out, in_, func, **more), signal(done) if done else None)

            def root(ap):
                k = signal("root_ready").count[where["phase"]] + 1
                act.wait_ge(*signal("inverse_ready").at(k))
                run(ap, ap, ACT.Sqrt, "root_ready")

            def square(src):
                run(sq[:].rearrange("p a b -> p (a b)"), src.rearrange("p a b -> p (a b)"), ACT.Square, "sq_ready")
                root(rstd[:])

            def ffn(f):
                with act.Fori(0, KF // 2) as i:
                    for u in range(2):
                        at = f * (KF // 2) + i
                        act.wait_ge(*signal(f"gate_ready{u}").at(at + 1))
                        act.wait_ge(*signal(f"hidden_ready{u}").at(at))
                        signal(f"silu_ready{u}").by(
                            nc.scalar.activation(silu[:, u, :], bank[u][:, 0:NT], ACT.Silu), KF // 2)

            def mixing():
                dest = [cq[:, 0, :], cq[:, 1, :], ckv, kr_raw]
                for n in range(18):
                    act.wait_ge(*signal("proj_ready").at(n + 1))
                    if n >= 6:
                        act.wait_ge(*signal("shifted").at(n - 5))
                    run(dest[n] if n < 4 else ptmp[:, n % 2, 1:NT + 1], bank[n % 4][:, 0:NT], done="proj_out")
                    if n == 3:
                        run(sq[:, 0:QT, :].rearrange("p a b -> p (a b)"), cq.rearrange("p a b -> p (a b)"),
                            ACT.Square, "mla_sq_ready")
                        run(sq[:, QT, :], ckv, ACT.Square, "mla_sq_ready")
                    if n == 5:
                        root(rstd[:])
                        root(rstd[:])
                for j in range(NJ + 2):
                    act.wait_ge(*signal("q_ready").at(j + 1))
                    run(qn[:, j, :] if j < NJ else qr_raw[:, j - NJ, :], bank[j][:, 0:NT], done="q_out")
                for h in range(H):
                    act.wait_ge(*signal("qlat_ready").at(h + 1))
                    run(qlat[:, h, :], bank[h % 4][:, 0:NT], done="qlat_out")
                units = [(0, 0, 4), (0, 4, 4)] + [(1, h, 2) for h in range(0, H, 2)]

                def exponentials(u):
                    act.wait_ge(*signal("score_less_max").at(u + 1))
                    run(prob[:, u % 2, :], prob[:, u % 2, :], ACT.Exp, "exp_ready", scale=MLA_SCALE)

                exponentials(0)
                for u, (qt, h0, nh) in enumerate(units):
                    if u + 1 < len(units):
                        exponentials(u + 1)
                    act.wait_ge(*signal("prob_t_ready").at(u + 1))
                    run(prob_t[:, u % 3, :], bank[2 + u % 2][:, 0:512], done="prob_t_out")
                    act.wait_ge(*signal("olat_ready").at(u + 1))
                    n = nh * P
                    run(olat[:, h0:h0 + nh, qt * P:qt * P + P],
                        bank[4 + u % 2][:, 0:n].rearrange("p (h q) -> p h q", h=nh), done="olat_out")
                for m in range(4 * NS + 6):
                    if m < 4 * NS and m % 4 == 0:
                        act.wait_ge(*signal("kr_turned").at(m // 4 + 1))
                        if m >= 8:
                            act.wait_ge(*signal("s_ready").at(m - 4))
                        run(kr_t[:, m // 4 % 2, :], bank[7][:, 0:512], done="kr_t_out")
                    if 0 <= m - 2 < 4 * NS:
                        b, n = (m - 2) // 4, (m - 2) % 4
                        act.wait_ge(*signal("s_ready").at(m - 1))
                        if n == 0 and b >= 2:
                            act.wait_ge(*signal("pt_ready").at(b - 1))
                            act.wait_ge(*signal("s_sum_ready").at(b - 1))
                        run(s_rows[b % 2][0:H, n * 512:n * 512 + 512], bank[4 + m % 2][0:H, 0:512], done="s_rows_out")
                        if n == 3:
                            act.wait_ge(*signal("s_bias_ready").at(b + 1))
                            bias = s_stat[0:H, 0, b:b + 1]
                            run(s_stat[0:H, 1, b:b + 1], s_max[0:H, b, 4:5], ACT.Exp, scale=MLA_SCALE, bias=bias)
                            run(s_rows[b % 2][0:H, :], s_rows[b % 2][0:H, :], ACT.Exp, "s_exp_ready", scale=MLA_SCALE,
                                bias=bias)
                    if m >= 7 and (m - 7) % 4 == 0:
                        b = (m - 7) // 4
                        act.wait_ge(*signal("pt_ready").at(b + 1))
                        if b:
                            act.wait_ge(*signal("pv_ready").at(b))
                        run(s_pt.rearrange("p a b -> p (a b)"), bank[3][:, 0:P], done="pt_out")
                for j in range(NJ):
                    act.wait_ge(*signal("omla_ready").at(j + 1))
                    run(mixT[:, NJ + j, :], bank[j][:, 0:NT], done="omla_out")

            def rwkv():
                act.wait_ge(*signal("sample_out").at(NS))
                act.wait_ge(*signal("stored").at(3))
                run(lora[0:64, 0, :], p[0:64, 12, :], ACT.Tanh, "lora_ready")
                run(lora[64:P, 0, :], p[64:P, 12, :], ACT.Copy, "lora_ready")
                act.wait_ge(*signal("wa_ready").at(1))
                for j in range(NJ):
                    run(w1[:, j, :], bank[j][:, 0:NT], ACT.Sigmoid, bias=v("w0", j),
                        done="wa_out" if j == NJ - 1 else None)
                act.wait_ge(*signal("wa_ready").at(2))
                for j in range(NJ):
                    run(iclr[:, j, :], bank[4 + j][:, 0:NT], ACT.Sigmoid, bias=v("a0", j),
                        done="wa_out" if j == NJ - 1 else None)
                act.wait_ge(*signal("kk_raw").at(1))
                run(w2.rearrange("p a b -> p (a b)"), kk.rearrange("p a b -> p (a b)"), ACT.Square, "kk_squared")
                act.wait_ge(*signal("logw_ready").at(1))
                run(sv[:, :, 1, :], logw[:, :, SEQ:NT], ACT.Exp, "sv_decay")
                root(w1.rearrange("p a b -> p (a b)"))
                act.wait_ge(*signal("sv_turned").at(1))
                run(sv_tok[0:6 * NS, :], bank[4][0:6 * NS, 0:512], done="sv_tok_ready")
                for T in range(2):
                    act.wait_ge(*signal("decays").at(T + 1))
                    ts = slice(T * P, T * P + P)
                    run(dex, dex, ACT.Exp)
                    run(din, cum[:, :, ts], ACT.Exp)
                    run(dinv, cum[:, :, ts], ACT.Exp, "decays_ready", scale=-1.0)
                    for n in range(4):
                        act.wait_ge(*signal("tok_turned").at(4 * T + n + 1))
                        run(tok[:, n, :], bank[n][:, 0:512], done="tok_out", scale=-1.0 if n == 1 else 1.0)
                    for n in range(1, LEVELS):
                        for g in range(2):
                            k = 2 * (T * (LEVELS - 1) + n - 1) + g + 1
                            act.wait_ge(*signal("y_ready").at(k))
                            if n > 1:
                                act.wait_ge(*signal("xy_ready").at(k - 2))
                            run(Y[:, 4 * g:4 * g + 4, :].rearrange("p a b -> p (a b)"), bank[g][:, 0:512], done="y_out")
                    act.wait_ge(*signal("g_ready").at(T + 1))
                    run(G, bank[6][:, 0:512], done="g_out")
                    act.wait_ge(*signal("y0_ready").at(T + 1))
                    run(Y0, bank[7][:, 0:512], done="y0_out")
                    act.wait_ge(*signal("wt_ready").at(T + 1))
                    run(WT.rearrange("p a b -> p (a b)"), bank[6][:, 0:512], done="wt_out")
                    act.wait_ge(*signal("rwkv_ready").at(T + 1))
                    run(oT[:, :, T * P:T * P + P], bank[2][:, 0:512].rearrange("p (j t) -> p j t", j=NJ),
                        done="rwkv_out")
                act.wait_ge(*signal("z_out").at(4))
                run(wstat, p[:, 13, :], ACT.Sigmoid, "gd_ready")
                act.wait_ge(*signal("centred").at(1))
                act.wait_ge(*signal("bonus_ready").at(1))
                run(e2.rearrange("p a b -> p (a b)"), oT_flat, ACT.Square, "gn_squared")
                root(e2.rearrange("p a b -> p (a b)"))
                act.wait_ge(*signal("gate_up").at(1))
                for j in range(NJ):
                    run(gate[:, j, :], bank[4 + j][:, 0:NT], done="gate_out" if j == NJ - 1 else None)

            oT_flat = oT.rearrange("p a b -> p (a b)")

            def cross():
                act.wait_ge(*signal("mem_loaded").at(1))
                run(sq[:, :, 0:NM], memg, ACT.Square, "sq_ready")
                root(rstd[:, 0:NM])
                square(xT[:])
                for n in range(KD):
                    act.wait_ge(*signal("kt_ready").at(n + 1))
                    run(KT[:, n, :], bank[n % 4][:, 0:NM], done="kt_out")
                for n in range(KD):
                    act.wait_ge(*signal("mq_ready").at(n + 1))
                    run(q[:, n, :], bank[n % 4][:, 0:NT], done="mq_out")

                def rows(n):
                    return m_rows[:, 2 * n:2 * n + 2, :].rearrange("p b m -> p (b m)")

                for n in range(4):
                    act.wait_ge(*signal("mem_k_used").at(2 * n + 2))
                    run(rows(n), bank[6 + n % 2][:, 0:512], done="ms_rows")

                def exponentials(u):
                    act.wait_ge(*signal("m_less_max").at(u + 1))
                    run(m_prob[:, u, :], m_prob[:, u, :], ACT.Exp, "m_exp_ready", scale=MEM_SCALE)

                exponentials(0)
                for u in range(4):
                    if u + 1 < 4:
                        exponentials(u + 1)
                    qt, hp = u % 2, u // 2
                    act.wait_ge(*signal("m_prob_t_ready").at(u + 1))
                    run(m_prob_t[:, 2 * hp:2 * hp + 2, :, qt * P:qt * P + P].rearrange("p h k q -> p (h k) q"),
                        bank[6 + u % 2][:, 0:512].rearrange("p (a q) -> p a q", a=4), done="m_prob_t_out")
                act.wait_ge(*signal("ms_less_max").at(1))
                run(m_rows.rearrange("p b m -> p (b m)"), m_rows.rearrange("p b m -> p (b m)"), ACT.Exp,
                    "ms_exp_ready", scale=MEM_SCALE)
                for k in range(KD):
                    act.wait_ge(*signal("mo_ready").at(k + 1))
                    run(o[:, k, 0:SEQ], bank[k % 2][:, 0:SEQ], done="mo_out")
                for n in range(4):
                    act.wait_ge(*signal("m_pt_ready").at(n + 1))
                    run(m_pt[:, 2 * n:2 * n + 2, :, :].rearrange("p b m h -> p (b m) h"),
                        bank[2 + n][:, 0:512].rearrange("p (a h x) -> p a h x", a=4, h=MH)[:, :, :, 0], done="m_pt_out")
                for n in range(4):
                    act.wait_ge(*signal("mem_v_used").at(2 * n + 2))
                    run(rows(n), bank[6 + n % 2][:, 0:512], done="ms_outputs")
                for n in range(4):
                    act.wait_ge(*signal("mo_turned").at(n + 1))
                    for b in range(2):
                        run(o[:, :, SEQ + 2 * n + b].rearrange("p (h t) -> p t h", t=2),
                            bank[2 + n][:, 256 * b:256 * b + 256].rearrange("p (t h x) -> p t h x", t=2, h=MH)[:, :, :, 0],
                            done="mo_out" if b else None)

            where["phase"] = "before"
            act.wait_ge(*signal("inputs_loaded").at(3))
            for name in 'silu_ready0 silu_ready1'.split():
                signal(name).grant(act)
            where["phase"] = "layer"
            with act.Fori(0, DEPTH) as layer:
                where["layer"] = layer
                for u in range(2):
                    act.wait_ge(*signal(f"ffn_added{u}").at(0))
                square(xT[:])
                ffn(0)
                for u in range(2):
                    act.wait_ge(*signal(f"ffn_added{u}").at(KD // 2))
                square(xT[:])
                mixing()
                rwkv()
                act.wait_ge(*signal("mix_added").at(KD))
                cross()
                act.wait_ge(*signal("cross_added").at(KD))
                square(xT[:])
                ffn(1)
            where["phase"] = "after"
            for u in range(2):
                act.wait_ge(*signal(f"ffn_added{u}").at(0))
            square(xT[:])

        @block.vector
        def _(dve):
            chain = Chain(dve, signal("dve_step"))

            def out_of(done):
                return signal(done) if done else None

            def tt(out, a, b, op, done=None):
                chain(nc.vector.tensor_tensor(out, a, b, op), out_of(done))

            def ts(out, a, s1, op0, s2=None, op1=None, done=None):
                if op1 is None:
                    chain(nc.vector.tensor_scalar(out, a, s1, None, op0), out_of(done))
                else:
                    chain(nc.vector.tensor_scalar(out, a, s1, s2, op0, op1), out_of(done))

            def stt(out, a, s, b, op0, op1, done=None):
                chain(nc.vector.scalar_tensor_tensor(out=out, in0=a, scalar=s, in1=b, op0=op0, op1=op1), out_of(done))

            def copy(out, a, done=None):
                chain(nc.vector.tensor_copy(out, a), out_of(done))

            def largest(out, a, done=None):
                chain(nc.vector.tensor_reduce(out, a, AX.X, ALU.max), out_of(done))

            def total(out, a, done=None):
                chain(nc.vector.tensor_reduce(out, a, AX.X, ALU.add), out_of(done))

            def clear(out, done=None):
                chain(nc.vector.memset(out, 0.0), out_of(done))

            def over(ap, *shape):
                return ap.rearrange("p (o n) -> p o n", o=1).broadcast_to(list(shape))

            def last_dim(ap, *shape):
                return ap.rearrange("p (n o) -> p n o", o=1).broadcast_to(list(shape))

            def flat(ap):
                return ap.rearrange("p a b -> p (a b)")

            def root_of_inverse(ap):
                k = signal("inverse_ready").count[where["phase"]] + 1
                chain(nc.vector.reciprocal(ap, ap), signal("inverse_ready"))
                dve.wait_ge(*signal("root_ready").at(k))

            def inverse_rms(out, sums, n, eps):
                ts(out, sums, 1.0 / n, ALU.mult, eps, ALU.add)
                root_of_inverse(out)

            def norm(n, gain, src, dst, done, width=NT, into=6):
                dve.wait_ge(*signal("sumsq_ready").at(n))
                inverse_rms(rstd[:, 0:width], bank[into][:, 0:width], D, RMS_EPS)
                for k in range(KD):
                    stt(dst[:, k, 0:width], src[:, k, 0:width], gain(k), rstd[:, 0:width], ALU.mult, ALU.mult,
                        done if k == KD - 1 else None)

            def ffn(f):
                wait_apart(dve, signal("h_ready").at(3 * f + 1))
                with dve.Fori(0, KF // 2) as i:
                    for u in range(2):
                        at = f * (KF // 2) + i
                        dve.wait_ge(*signal(f"silu_ready{u}").at(at + 1))
                        dve.wait_ge(*signal(f"gu_used{u}").at(at + 1))
                        signal(f"hidden_ready{u}").by(
                            nc.vector.tensor_tensor(hidden[:, 2 * i + u, :], silu[:, u, :], bank[2 + u][:, 0:NT],
                                                    ALU.mult), KF // 2)
                with dve.Fori(0, KD // 2) as i:
                    for u in range(2):
                        at = f * (KD // 2) + i
                        dve.wait_ge(*signal(f"down_used{u}").at(at + 1))
                        signal(f"ffn_added{u}").by(
                            nc.vector.scalar_tensor_tensor(out=xT[:, 2 * i + u, :], in0=bank[4 + u][:, 0:NT],
                                                           scalar=0.5, in1=xT[:, 2 * i + u, :], op0=ALU.mult,
                                                           op1=ALU.add), KD // 2)
                for u in range(2):
                    dve.wait_ge(*signal(f"ffn_added{u}").at((f + 1) * (KD // 2)))

            def mixing():
                for u in range(2):
                    clear(ptmp[:, u, 0:1])
                clear(kr_group.rearrange("p a b -> p (a b)"))
                clear(qr_group.rearrange("p a b c -> p (a b c)"))
                dve.wait_ge(*signal("mla_sum_ready").at(1))
                inverse_rms(rstd[:], bank[4][:, 0:NT], QT * P, RMS_EPS)
                for k in range(QT):
                    stt(cq[:, k, :], cq[:, k, :], v("q_norm", k), rstd[:], ALU.mult, ALU.mult,
                        "cq_ready" if k else None)
                dve.wait_ge(*signal("mla_sum_ready").at(2))
                inverse_rms(rstd[:], bank[5][:, 0:NT], CL, RMS_EPS)
                stt(ckv, ckv, v("kv_norm"), rstd[:], ALU.mult, ALU.mult, "ckv_ready")
                dve.wait_ge(*signal("rot_ready").at(1))
                tt(kr, kr_raw, c("cos"), ALU.mult)
                tt(diff, bank[6][:, 0:NT], c("sin"), ALU.mult)
                tt(kr, kr, diff, ALU.add, "kr_ready")
                for g in range(4):
                    copy(kr_group[32 * g:32 * g + 32, g, :], kr[32 * g:32 * g + 32, 0:SEQ])
                dve.wait_ge(*signal("small_loaded").at(2))
                for n, j in enumerate([12, 13] + list(range(12))):
                    dve.wait_ge(*signal("proj_out").at(5 + n))
                    src = ptmp[:, n % 2, :]
                    tt(diff[:, 0:SEQ], src[:, 0:SEQ], src[:, 1:SEQ + 1], ALU.subtract)
                    tt(diff[:, SEQ:NT], shift0[:, j, :], src[:, SEQ + 1:NT + 1], ALU.subtract)
                    stt(p[:, j, :], diff, v("mu", j), src[:, 1:NT + 1], ALU.mult, ALU.add)
                    copy(shift_out[:, j, :], src[:, SEQ:NT + 1], "shifted")
                dve.wait_ge(*signal("ckv_turned").at(1))
                copy(ckv_tok.rearrange("p a b -> p (a b)"), bank[6][:, 0:256])
                for g in range(2):
                    dve.wait_ge(*signal("rot_ready").at(g + 2))
                    tt(qr[:, g, :], qr_raw[:, g, :], c("cos"), ALU.mult)
                    tt(diff, bank[4 + g][:, 0:NT], c("sin"), ALU.mult)
                    tt(qr[:, g, :], qr[:, g, :], diff, ALU.add, "qr_ready")
                dve.wait_ge(*signal("qs_ready").at(1))
                for g in range(4):
                    rows = slice(32 * g, 32 * g + 32)
                    copy(qr_group[rows, g, :, :], bank[7][rows, 0:64].rearrange("p (h b) -> p h b", h=H),
                         "qs_out" if g == 3 else None)

                units = [(0, 0, 4), (0, 4, 4)] + [(1, h, 2) for h in range(0, H, 2)]

                def less_max(u):
                    qt, _, nh = units[u]
                    n = (qt + 1) * P
                    pr = prob[:, u % 2, :].rearrange("p (h k) -> p h k", h=nh)
                    ps = bank[u % 2][:, 0:512].rearrange("p (h k) -> p h k", h=nh)
                    dve.wait_ge(*signal("score_ready").at(u + 1))
                    if u >= 2:
                        dve.wait_ge(*signal("prob_t_ready").at(u - 1))
                    if qt:
                        copy(pr[:, :, 0:P], ps[:, :, 0:P])
                    tt(pr[:, :, n - P:n], ps[:, :, n - P:n], over(c("causal"), P, nh, P), ALU.add, "score_out")
                    largest(stat[:, 8, 0:nh], pr)
                    tt(pr, pr, last_dim(stat[:, 8, 0:nh], P, nh, n), ALU.subtract, "score_less_max")

                less_max(0)
                for u in range(len(units)):
                    if u + 1 < len(units):
                        less_max(u + 1)
                    qt, _, nh = units[u]
                    n = (qt + 1) * P
                    pr = prob[:, u % 2, :].rearrange("p (h k) -> p h k", h=nh)
                    dve.wait_ge(*signal("exp_ready").at(u + 1))
                    total(stat[:, 9, 0:nh], pr)
                    chain(nc.vector.reciprocal(stat[:, 9, 0:nh], stat[:, 9, 0:nh]))
                    tt(pr, pr, last_dim(stat[:, 9, 0:nh], P, nh, n), ALU.mult, "prob_ready")

                dve.wait_ge(*signal("snew_ready").at(1))
                copy(s_max[0:H, :, 4], bank[6][0:H, 272:280])
                for m in range(4 * NS + 6):
                    if m < 4 * NS:
                        dve.wait_ge(*signal("turned").at(m + 1))
                        if m >= 4:
                            dve.wait_ge(*signal("s_ready").at(m - 3))
                        n = m % 4
                        copy(ckv_t[:, 4 * n:4 * n + 4, :].rearrange("p a b -> p (a b)"), bank[m % 3][:, 0:512],
                             "ckv_t_out")
                    if 0 <= m - 2 < 4 * NS:
                        b, n = (m - 2) // 4, (m - 2) % 4
                        dve.wait_ge(*signal("s_rows_out").at(m - 1))
                        largest(s_max[0:H, b, n:n + 1], s_rows[b % 2][0:H, n * 512:n * 512 + 512])
                        if n == 3:
                            largest(s_stat[0:H, 0, b:b + 1], s_max[0:H, b, :])
                            ts(s_stat[0:H, 0, b:b + 1], s_stat[0:H, 0, b:b + 1], -MLA_SCALE, ALU.mult,
                               done="s_bias_ready")
                    if m < 6:
                        continue
                    b = (m - 6) // 4
                    if (m - 6) % 4 == 0:
                        dve.wait_ge(*signal("s_exp_ready").at(b + 1))
                        total(s_stat[0:H, 2, b:b + 1], s_rows[b % 2][0:H, :], "s_sum_ready")
                        tt(s_stat[0:H, 2, b:b + 1], s_stat[0:H, 2, b:b + 1], s_stat[0:H, 1, b:b + 1], ALU.add)
                        chain(nc.vector.reciprocal(s_stat[0:H, 2, b:b + 1], s_stat[0:H, 2, b:b + 1]))
                    if (m - 6) % 4 == 2:
                        dve.wait_ge(*signal("pv_ready").at(b + 1))
                        if b >= 2:
                            dve.wait_ge(*signal("o_turned").at(b - 1))
                        ts(s_o[0:H, b % 2, :], bank[6][0:H, P:2 * P], s_stat[0:H, 1, b:b + 1], ALU.mult)
                        tt(s_o[0:H, b % 2, :], s_o[0:H, b % 2, :], bank[6][0:H, 0:P], ALU.add)
                        ts(s_o[0:H, b % 2, :], s_o[0:H, b % 2, :], s_stat[0:H, 2, b:b + 1], ALU.mult, done="o_rows")
                    if (m - 6) % 4 == 3:
                        dve.wait_ge(*signal("o_turned").at(b + 1))
                        copy(olat[:, :, SEQ + b], bank[6][:, 256:256 + H], "sample_out")

            def rwkv():
                rr, kc, vv = p[:, 0:NJ, :], p[:, NJ:2 * NJ, :], p[:, 2 * NJ:3 * NJ, :]
                dve.wait_ge(*signal("omla_out").at(NJ))
                dve.wait_ge(*signal("stored").at(3))
                for j in range(NJ):
                    ts(kk[:, j, :], kc[:, j, :], v("k_k", j), ALU.mult, done="kk_raw" if j == NJ - 1 else None)
                dve.wait_ge(*signal("wa_out").at(1))
                ts(flat(logw), flat(w1), -DECAY_C, ALU.mult, done="logw_ready")
                for j in range(NJ):
                    chain(nc.vector.tensor_tensor_scan(cum[:, j, :], c("keep"), logw[:, j, 0:SEQ], 0.0, ALU.mult,
                                                       ALU.add))
                dve.wait_ge(*signal("kk_norm").at(1))
                for j in range(NJ):
                    ts(w1[:, j, :], bank[j][:, 0:NT], 1e-24, ALU.max)
                root_of_inverse(flat(w1))
                tt(flat(kk), flat(kk), flat(w1), ALU.mult)
                dve.wait_ge(*signal("wa_out").at(2))
                for j in range(NJ):
                    ts(w1[:, j, :], iclr[:, j, :], -1.0, ALU.add, v("k_a", j), ALU.mult)
                stt(flat(kc), flat(w1), 1.0, flat(kc), ALU.add, ALU.mult)
                tt(flat(iclr), flat(iclr), flat(kk), ALU.mult)
                for n, src in ((0, rr), (2, kc), (3, kk), (4, iclr), (5, vv)):
                    copy(sv[:, :, n, :], src[:, :, SEQ:NT])
                dve.wait_ge(*signal("sv_decay").at(1))
                copy(sv[:, :, 0, :], rr[:, :, SEQ:NT], "sv_ready")
                dve.wait_ge(*signal("svb_loaded").at(7))
                dve.wait_ge(*signal("state_loaded").at(1))
                full = [P, 32, HD]

                def by_key(n):
                    return over(svb[:, n, :], *full)

                tt(St, S, by_key(3), ALU.mult)
                total(skk, St)
                tt(S, S, by_key(1), ALU.mult)
                tt(St, last_dim(skk, *full), by_key(4), ALU.mult)
                tt(S, S, St, ALU.subtract)
                tt(St, last_dim(svv, *full), by_key(2), ALU.mult)
                tt(S, S, St, ALU.add, "state_ready")
                tt(St, S, by_key(0), ALU.mult)
                total(so, St, "so_ready")
                dve.wait_ge(*signal("so_turned").at(1))
                copy(oT[:, :, SEQ:NT], bank[5][:, 0:NJ * NS].rearrange("p (a b) -> p a b", a=NJ), "so_out")
                dve.wait_ge(*signal("stored").at(4))
                clear(Z[:, 0, :], "z_cleared")
                for T in range(2):
                    cols = slice(T * P, T * P + P)
                    if T:
                        dve.wait_ge(*signal("rwkv_ready").at(T))
                    tt(dex, cum[:, :, cols], logw[:, :, cols], ALU.subtract, "decays")
                    dve.wait_ge(*signal("decays_ready").at(T + 1))
                    tt(AR[:, :, 0, :], kk[:, :, cols], dex, ALU.mult)
                    tt(AR[:, :, 1, :], rr[:, :, cols], din, ALU.mult)
                    tt(Bt, iclr[:, :, cols], dinv, ALU.mult)
                    tt(Kt, kc[:, :, cols], dinv, ALU.mult, "operands_ready")
                    for i in range(4):
                        dve.wait_ge(*signal("pairs_ready").at(10 * T + i + 1))
                        tt(MR_b[:, 2 * i:2 * i + 2, :], bank[4 + i][:, 0:512].rearrange("p (h n) -> p h n", h=2),
                           over(c("mb"), P, 2, 2 * P), ALU.mult, "mb_out")
                    for i in range(4):
                        dve.wait_ge(*signal("pairs_ready").at(10 * T + i + 5))
                        tt(MR_k[:, 2 * i:2 * i + 2, :], bank[i][:, 0:512].rearrange("p (h n) -> p h n", h=2),
                           over(c("mk"), P, 2, 2 * P), ALU.mult, "mk_out")
                    four = [P, 4, P]
                    for g in range(2):
                        hs = slice(4 * g, 4 * g + 4)
                        dve.wait_ge(*signal("pairs_ready").at(10 * T + g + 9))
                        tt(X[:, hs, :], bank[4 + g][:, 0:512].rearrange("p (h n) -> p h n", h=4),
                           over(c("neg0"), *four), ALU.mult)
                        tt(X[:, hs, :], X[:, hs, :], over(ident, *four), ALU.add)
                        tt(XT[:, hs, :], MR_b[:, hs, 0:P], over(c("lvl")[:, 0:P], *four), ALU.mult)
                        tt(XT[:, hs, :], XT[:, hs, :], over(ident, *four), ALU.add, "x_out")
                    for n in range(1, LEVELS):
                        for g in range(2):
                            hs = slice(4 * g, 4 * g + 4)
                            dve.wait_ge(*signal("xy_ready").at(2 * (T * (LEVELS - 1) + n - 1) + g + 1))
                            if n < LEVELS - 1:
                                tt(flat(X[:, hs, :]), flat(X[:, hs, :]), bank[2 + g][:, 0:512], ALU.subtract)
                            tt(flat(XT[:, hs, :]), flat(XT[:, hs, :]), bank[4 + g][:, 0:512], ALU.subtract, "x_out")
                    dve.wait_ge(*signal("y0_out").at(T + 1))
                    for cc in range(2):
                        n, o0 = 2 * T + cc, CHUNK * cc
                        tt(dcm, over(c("blk"), P, NJ, P),
                           din[:, :, o0 + CHUNK - 1:o0 + CHUNK].broadcast_to([P, NJ, P]), ALU.mult)
                        dve.wait_ge(*signal("u_ready").at(n + 1))
                        tt(U[o0:o0 + CHUNK, :], bank[0][o0:o0 + CHUNK, 0:512], Y0[o0:o0 + CHUNK, :], ALU.add, "u_out")
                        dve.wait_ge(*signal("z_ready").at(n + 1))
                        tt(Z[:, (n + 1) % 3, :], Z[:, n % 3, :], bank[1][:, 0:512], ALU.add)
                        tt(Z[:, (n + 1) % 3, :], Z[:, (n + 1) % 3, :], flat(dcm), ALU.mult, "z_out")
                dve.wait_ge(*signal("rwkv_out").at(2))
                tt(flat(e1), flat(rr), flat(kc), ALU.mult)
                for j in range(NJ):
                    ts(e1[:, j, :], e1[:, j, :], v("r_k", j), ALU.mult, done="rkr_ready" if j == NJ - 1 else None)
                dve.wait_ge(*signal("gn_mean").at(1))
                for j in range(NJ):
                    stt(oT[:, j, :], bank[j][:, 0:NT], -1.0 / HD, oT[:, j, :], ALU.mult, ALU.add,
                        "centred" if j == NJ - 1 else None)
                dve.wait_ge(*signal("bonus_ready").at(1))
                for j in range(NJ):
                    tt(bonus[:, j, :], bank[4 + j][:, 0:NT], vv[:, j, :], ALU.mult,
                       "bonus_out" if j == NJ - 1 else None)
                dve.wait_ge(*signal("gn_var").at(1))
                for j in range(NJ):
                    ts(e2[:, j, :], bank[j][:, 0:NT], 1.0 / HD, ALU.mult, GN_EPS, ALU.add)
                root_of_inverse(flat(e2))
                tt(flat(oT), flat(oT), flat(e2), ALU.mult)
                for j in range(NJ):
                    ts(oT[:, j, :], oT[:, j, :], v("gn_w", j), ALU.mult, v("gn_b", j), ALU.add)
                tt(flat(oT), flat(oT), flat(bonus), ALU.add)
                dve.wait_ge(*signal("gate_out").at(1))
                tt(flat(oT), flat(oT), flat(gate), ALU.mult, "rwkv_mixed")
                for n in range(KD):
                    dve.wait_ge(*signal("mix_ready").at(n + 1))
                    tt(xT[:, n, :], xT[:, n, :], bank[n % 4][:, 0:NT], ALU.add, "mix_added")

            def cross():
                dve.wait_ge(*signal("stored").at(5))
                norm(3, lambda k: v("mem", k), memg, memg, "memg_ready", NM)
                norm(4, lambda k: v("cross", k), xT, hT, "h_ready", into=5)
                for n in range(8):
                    dve.wait_ge(*signal("v_ready").at(n + 1))
                    copy(V[:, n % 2, (n // 2) * 256:(n // 2) * 256 + 256], bank[4 + n % 2][:, 0:256], "v_out")

                def less_max(u):
                    ps = bank[4 + u % 2][:, 0:512].rearrange("p (h k) -> p h k", h=2)
                    pr = m_prob[:, u, :].rearrange("p (h k) -> p h k", h=2)
                    dve.wait_ge(*signal("m_score_ready").at(u + 1))
                    largest(m_st[:, 6, 0:2], ps)
                    tt(pr, ps, last_dim(m_st[:, 6, 0:2], P, 2, NM), ALU.subtract, "m_less_max")

                less_max(0)
                for u in range(4):
                    if u + 1 < 4:
                        less_max(u + 1)
                    pr = m_prob[:, u, :].rearrange("p (h k) -> p h k", h=2)
                    dve.wait_ge(*signal("m_exp_ready").at(u + 1))
                    total(m_st[:, 7, 0:2], pr)
                    chain(nc.vector.reciprocal(m_st[:, 7, 0:2], m_st[:, 7, 0:2]))
                    tt(pr, pr, last_dim(m_st[:, 7, 0:2], P, 2, NM), ALU.mult, "m_prob_ready")

                dve.wait_ge(*signal("ms_rows").at(4))
                largest(m_st[:, 0, :], m_rows)
                tt(m_rows, m_rows, last_dim(m_st[:, 0, :], P, NS, NM), ALU.subtract, "ms_less_max")
                dve.wait_ge(*signal("ms_exp_ready").at(1))
                total(m_st[:, 1, :], m_rows)
                chain(nc.vector.reciprocal(m_st[:, 1, :], m_st[:, 1, :]))
                tt(m_rows, m_rows, last_dim(m_st[:, 1, :], P, NS, NM), ALU.mult, "ms_prob_ready")
                for n in range(KD):
                    dve.wait_ge(*signal("cross_ready").at(n + 1))
                    tt(xT[:, n, :], xT[:, n, :], bank[n % 4][:, 0:NT], ALU.add, "cross_added")

            where["phase"] = "before"
            chain(nc.vector.memset(ones[:], 1.0), signal("ones_ready"))
            dve.wait_ge(*signal("index_loaded").at(2))
            ts(rows_idx[:], rows_idx[:], PER, ALU.mult)
            tt(rows_idx[:], rows_idx[:], part_idx[:], ALU.add, "index_ready")
            dve.wait_ge(*signal("inputs_loaded").at(3))
            keep_register(dve)
            for name in 'hidden_ready0 hidden_ready1 ffn_added0 ffn_added1 mix_added cross_added'.split():
                signal(name).grant(dve)
            where["phase"] = "layer"
            with dve.Fori(0, DEPTH) as layer:
                where["layer"] = layer
                copy(vec[:], vectors[:, bass.ds(layer * NV, NV)])
                norm(1, lambda k: v("ffn1", k), xT, hT, "h_ready")
                ffn(0)
                norm(2, lambda k: v("mix", k), xT, hT, "h_ready")
                mixing()
                ts(rows_idx[:], rows_idx[:], t["cache_ckv"].shape[1] * PER, ALU.add, done="index_ready")
                rwkv()
                cross()
                norm(5, lambda k: v("ffn2", k), xT, hT, "h_ready")
                dve.wait_ge(*signal("stored").at(7))
                ffn(1)
            use_register(dve)
            where["phase"] = "after"
            norm(1, lambda k: vectors[:, DEPTH * NV + k:DEPTH * NV + k + 1], xT, hT, "final_ready")

    return ({name: (s.count["before"], s.count["layer"]) for name, s in signals.items()}
            | {name: m.place for name, m in milestones.items()})


def lay_out_constants():
    con = np.zeros((P, NC_), np.float32)

    def put(name, a):
        at, n = CON[name]
        con[:, at:at + n] = a.reshape(P, n)

    i = np.arange(P)
    row, col = i[:, None], i[None, :]
    put("ident", np.eye(P))
    put("blk", (row // HD == col // HD).astype(np.float32))
    rot = np.where((row == col + 16) & (col % 32 < 16), -1.0, 0.0) + np.where((row == col - 16) & (col % 32 >= 16), 1.0, 0.0)
    put("rot", rot)
    put("sel", np.stack([(row == 32 * g + col % 32) for g in range(4)], 1).astype(np.float32))
    pos = np.concatenate([np.arange(SEQ), np.full(NS, PAST)]).astype(np.float32)
    inv = np.float32(10000.0) ** (-np.arange(16, dtype=np.float32) / np.float32(16))
    ang = pos[None, :] * inv[i % 16][:, None]
    put("cos", np.cos(ang))
    put("sin", np.sin(ang))
    put("causal", np.where(col <= row, 0.0, NEG))
    same = row // CHUNK == col // CHUNK
    strict, incl = same & (row < col), same & (row <= col)
    put("mk", np.stack([strict, incl], 1).astype(np.float32))
    put("mb", np.stack([strict * 1.0, incl * -1.0], 1))

    def level(s, t, n):
        return (s // (2 << n) == t // (2 << n)) & (s // (1 << n) % 2 == 0) & (t // (1 << n) % 2 == 1)

    lvl = [level(row, col, n) * (-1.0 if n == 0 else 1.0) for n in range(LEVELS)]
    put("lvl", np.stack(lvl, 1))
    put("neg0", level(col, row, 0) * -1.0)
    put("keep", np.broadcast_to(np.arange(SEQ) % CHUNK != 0, (P, SEQ)).astype(np.float32))
    return con


def kernel(**inputs):
    import concourse.bacc as bacc
    from concourse.bass_utils import run_bass_kernel_spmd

    a = {k: np.asarray(v) for k, v in inputs.items()}
    L = DEPTH

    def cols(w, n):
        _, k, m = w.shape
        return w.reshape(L, k // P, P, m // n, n).transpose(0, 3, 2, 1, 4)

    def rows(v):
        return v.reshape(L, -1, P).transpose(0, 2, 1)

    arrays = {"constants": lay_out_constants()}
    for f in ("ffn1", "ffn2"):
        arrays[f"{f}_gu"] = np.stack([cols(a[f"{f}_w_gate"], P), cols(a[f"{f}_w_up"], P)], 3)
        arrays[f"{f}_down"] = cols(a[f"{f}_w_down"], P)
    w_in = a["w_in"]
    q0 = RW * P
    w_in = np.concatenate([w_in[:, :, q0:q0 + QT * P + CL]] + [w_in[:, :, q0 + QT * P + CL:]] * 4
                          + [w_in[:, :, q0 - 2 * P:q0], w_in[:, :, :q0 - 2 * P]], 2)

    def pairs(w):
        t = cols(w, P)
        return t.reshape(L, t.shape[1] // 2, 2, P, KD, P).transpose(0, 1, 3, 2, 4, 5).reshape(L, -1, P, 2 * D)

    arrays["blocks"] = np.concatenate([pairs(w_in), pairs(a["w_out"]), pairs(a["mem_w_k"]),
                                       pairs(a["mem_w_q"]), cols(a["mem_w_v"], 2 * P).reshape(L, -1, P, 2 * D),
                                       pairs(a["mem_w_o"])], 1)
    uq = a["mla_w_uq"].reshape(L, QT, P, H, NOPE + ROPE).transpose(0, 2, 1, 3, 4)
    uk = a["mla_w_uk"].transpose(0, 2, 3, 1).reshape(L, NJ, P, CL).transpose(0, 2, 1, 3)
    arrays["small"] = np.concatenate(
        [x.reshape(L, P, -1) for x in (uq[..., :NOPE], uq[..., NOPE:], uk, a["mla_w_uv"],
                                       np.concatenate([a["rwkv_w_up"], a["rwkv_a_up"]], 1), a["rwkv_g_up"])], 2)
    vec = np.concatenate([rows(v) for v in (
        a["norm_ffn1"], a["norm_mix"], a["norm_cross"], a["norm_ffn2"], a["norm_mem"], a["shift_mu"], a["rwkv_w0"],
        a["rwkv_a0"], a["rwkv_k_k"], a["rwkv_k_a"], a["rwkv_r_k"].reshape(L, -1), a["rwkv_gn_w"], a["rwkv_gn_b"],
        a["mla_q_norm"], a["mla_kv_norm"])], 2)
    arrays["vectors"] = np.concatenate([vec[0], vec[1], a["norm_final"].reshape(KD, P).T], 1)
    x = np.concatenate([a["x_prompt"][0], a["x_sample"][:, 0]], 0)
    arrays["x"] = x.T.reshape(KD, P, NT).transpose(1, 0, 2)
    arrays["mem"] = a["mem_prompt"][0].T.reshape(KD, P, NM).transpose(1, 0, 2)
    arrays["shift0"] = a["state_shift"].reshape(L, NS, RW, P).transpose(0, 3, 2, 1)
    arrays["cache_ckv"] = a["cache_ckv"]
    arrays["cache_krope"] = a["cache_krope"]
    arrays["state_wkv"] = a["state_wkv"]
    arrays["mem_k"] = a["cache_mem_k"].reshape(L, NS, NM, KD, P).transpose(0, 1, 4, 3, 2)
    arrays["mem_v"] = a["cache_mem_v"].reshape(L, NS, 2, P, D).transpose(0, 1, 3, 2, 4)
    arrays["pages"] = np.repeat(a["page_table"].T, PER, axis=0)
    arrays["page_part"] = np.repeat((np.arange(P, dtype=np.int32) % PER)[:, None], NS, axis=1)
    arrays = {k: np.ascontiguousarray(v) for k, v in arrays.items()}
    outs = {"y": (P, KD, NT), "o_ckv": (L, P, NT), "o_krope": (L, ROPE, NT), "o_wkv": (L, P, NJ, P),
            "o_shift": (L, P, RW, NS + 1), "o_mem_k": (L, P, KD, NM), "o_mem_v": (L, P, 2, D),
            "o_wkv_s": (L, P, 32 * HD)}

    totals = {}
    for _ in range(2):
        nc = bacc.Bacc("TRN2", target_bir_lowering=False, num_devices=1)
        t = {k: nc.dram_tensor(f"in_{k}", v.shape, mybir.dt.from_np(v.dtype), kind="ExternalInput").ap()
             for k, v in arrays.items()}
        t.update({k: nc.dram_tensor(f"out_{k}", s, F32, kind="ExternalOutput").ap() for k, s in outs.items()})
        totals = build(nc, t, totals)
    r = run_bass_kernel_spmd(nc, [{f"in_{k}": x for k, x in arrays.items()}], core_ids=[0]).results[0]
    got = {k: r[f"out_{k}"] for k in outs}

    y = got["y"].transpose(2, 1, 0).reshape(NT, D)
    ckv, kr = got["o_ckv"].transpose(0, 2, 1), got["o_krope"].transpose(0, 2, 1)
    wkv = np.stack([got["o_wkv"][:, HD * (h % 2):HD * (h % 2) + HD, h // 2, HD * (h % 2):HD * (h % 2) + HD]
                    for h in range(H)], 1).transpose(0, 1, 3, 2)[:, None]
    shift = got["o_shift"].transpose(0, 3, 2, 1).reshape(L, NS + 1, RW * P)
    mem_k = got["o_mem_k"].transpose(0, 3, 2, 1).reshape(L, 1, NM, MH, MD)
    mem_v = got["o_mem_v"].transpose(0, 2, 1, 3).reshape(L, 1, NM, MH, MD)
    out = (y[None, :SEQ], y[SEQ:, None], ckv[:, None, :SEQ], kr[:, None, :SEQ], wkv, shift[:, None, 0],
           mem_k, mem_v, ckv[:, SEQ:, None], kr[:, SEQ:, None], got["o_wkv_s"].reshape(L, NS, H, HD, HD),
           shift[:, 1:])
    return tuple(np.ascontiguousarray(o) for o in out)
```

```python
from contextlib import ExitStack

import numpy as np

import concourse.bass as bass
from concourse import mybir

ALU = mybir.AluOpType
ACT = mybir.ActivationFunctionType
AX = mybir.AxisListType
F32 = mybir.dt.float32
I32 = mybir.dt.int32

P = 128
DEPTH, D, SEQ, NS = 2, 1024, 256, 8
NT = SEQ + NS
KD = D // P
FF = 2816
KF = FF // P
H, HD = 8, 64
NJ = H // 2
RW = 14
NOPE, ROPE, CL = 64, 32, 128
QT = 2
PAST, PAGE = 2048, 128
JS = PAST // P
PER = 8
SV_STEP = 15
CHUNK = 64
LEVELS = 6
MH, MD, NM = 4, 256, 256
MLA_SCALE = (NOPE + ROPE) ** -0.5
MEM_SCALE = MD ** -0.5
RMS_EPS, GN_EPS = 1e-6, 64e-5
DECAY_C = float(np.exp(-0.5))
NEG = -1e30

VEC = {}
for _name, _tiles in (("ffn1", 8), ("mix", 8), ("cross", 8), ("ffn2", 8), ("mem", 8), ("mu", 14), ("w0", 4),
                      ("a0", 4), ("k_k", 4), ("k_a", 4), ("r_k", 4), ("gn_w", 4), ("gn_b", 4), ("q_norm", 2),
                      ("kv_norm", 1)):
    VEC[_name] = (sum(t for _, t in VEC.values()), _tiles)
NV = sum(t for _, t in VEC.values())

CON = {}
for _name, _cols in (("ident", P), ("blk", P), ("rot", P), ("sel", 4 * P), ("cos", NT), ("sin", NT),
                     ("causal", P), ("mk", 2 * P), ("mb", 2 * P), ("lvl", LEVELS * P), ("neg0", P),
                     ("keep", SEQ)):
    CON[_name] = (sum(t for _, t in CON.values()), _cols)
NC_ = sum(t for _, t in CON.values())

SW = {}
for _name, _cols in (("uq_nope", QT * NJ * P), ("uq_rope", QT * 2 * P), ("uk", NJ * CL), ("uv", H * HD),
                     ("wa_up", H * HD), ("g_up", H * HD)):
    SW[_name] = (sum(t for _, t in SW.values()), _cols)
NSW = sum(t for _, t in SW.values())

C_IN, C_OUT, C_Q, C_MEMK, C_MEMV, C_O = 0, 9, 13, 17, 21, 25
C_BLOCKS = 29
C_SLOTS = 2


class Signal:

    def __init__(self, name, sem, total, where, unit):
        self.name, self.sem, self.unit, self.where = name, sem, unit, where
        self.base, self.per = total
        self.count = {"before": 0, "layer": 0, "after": 0}

    def by(self, instruction, times=1):
        instruction.then_inc(self.sem, self.unit)
        self.count[self.where["phase"]] += times

    def grant(self, engine):
        engine.sem_inc(self.sem, self.unit)
        self.count["before"] += 1

    def at(self, k):
        phase = self.where["phase"]
        if phase == "before":
            return self.sem, self.unit * k
        if phase == "after":
            return self.sem, self.unit * (self.base + DEPTH * self.per + k)
        return self.sem, self.where["layer"] * (self.unit * self.per) + (k + self.base) * self.unit


class Milestone:

    def __init__(self, shared, place):
        self.shared, self.place = shared, place

    def by(self, instruction):
        self.shared.by(instruction)
        self.place = self.shared.count["layer"]

    def at(self, k):
        return self.shared.at(self.place)


MILESTONES = {
    "tensor_milestones": "ckv_turned qs_ready snew_ready sv_turned so_turned gn_mean bonus_ready gn_var "
                         "gate_up",
    "vector_milestones": "cq_ready ckv_ready kr_ready qs_out kk_raw logw_ready sv_ready state_ready so_ready so_out "
                         "z_cleared rkr_ready centred bonus_out memg_ready ms_less_max "
                         "ms_prob_ready",
    "scalar_milestones": "kk_squared decay_ready iclr_ready sv_decay sv_tok_ready gd_ready gn_squared gate_out ms_exp_ready",
}
MILESTONE_OF = {name: shared for shared, names in MILESTONES.items() for name in names.split()}


class Chain:

    def __init__(self, engine, done):
        self.engine, self.done = engine, done

    def __call__(self, instruction, signal=None):
        signal = signal or self.done
        signal.by(instruction)
        events = 1 if isinstance(signal, Milestone) else signal.count[signal.where["phase"]]
        self.engine.wait_ge(*signal.at(events))


class Region:

    def __init__(self, tensor, start, end):
        self.tensor, self.at, self.end = tensor, start, end

    def take(self, *dims, parts=P):
        n = int(np.prod(dims))
        assert self.at + n <= self.end, (self.at, n, self.end)
        ap = self.tensor[0:parts, self.at:self.at + n]
        self.at += n
        if len(dims) > 1:
            names = "abcd"[:len(dims)]
            ap = ap.rearrange(f"p ({' '.join(names)}) -> p {' '.join(names)}",
                              **{x: d for x, d in zip(names[1:], dims[1:])})
        return ap


def build(nc, t, totals):
    ctx = ExitStack()
    where = {"phase": "before", "layer": 0}
    signals, milestones = {}, {}

    def signal(name):
        if name in MILESTONE_OF:
            if name not in milestones:
                milestones[name] = Milestone(signal(MILESTONE_OF[name]), totals.get(name, 1))
            return milestones[name]
        if name not in signals:
            unit = 16 if "loaded" in name or "spread" in name or name == "stored" else 1
            signals[name] = Signal(name, ctx.enter_context(nc.semaphore(name)), totals.get(name, (0, 0)), where, unit)
        return signals[name]

    def sbuf(name, shape, dtype=F32):
        return ctx.enter_context(nc.sbuf_tensor(name, shape, dtype))

    with ctx:
        ctx.enter_context(nc.allow_non_contiguous_dma("small strided pieces"))
        bank = [ctx.enter_context(nc.psum_tensor(f"bank{i}", [P, 512], F32)) for i in range(8)]
        con = sbuf("con", [P, NC_])
        vectors = sbuf("vectors", [P, DEPTH * NV + KD])
        vec = sbuf("vec", [P, NV])
        ones = sbuf("ones", [P, P])
        xT = sbuf("xT", [P, KD, NT])
        hT = sbuf("hT", [P, KD, NT])
        sq = sbuf("sq", [P, KD, NT])
        rstd = sbuf("rstd", [P, NT])
        ring_a = sbuf("ring_a", [P, 2, 2, KD, P])
        ring_b = sbuf("ring_b", [P, 2, KF, P])
        ring_c = sbuf("ring_c", [P, C_SLOTS, 2 * D])
        shift0 = sbuf("shift0", [P, RW, NS])
        small = sbuf("small", [P, NSW])
        spare = sbuf("spare", [P, 1])
        rows_idx = sbuf("rows_idx", [P, NS], I32)
        part_idx = sbuf("part_idx", [P, NS], I32)
        ARENA = 25140
        arena = sbuf("arena", [P, ARENA])
        vec_dram = nc.dram_tensor("sample_vectors", (6, NS, H * HD), F32, kind="Internal").ap()
        out_dram = nc.dram_tensor("sample_outputs", (NS, H * HD), F32, kind="Internal").ap()

        def c(name, *dims):
            at, n = CON[name]
            ap = con[:, at:at + n]
            return ap if not dims else ap.rearrange("p (a b) -> p a b", a=dims[0])

        def v(name, k=0):
            at, _ = VEC[name]
            return vec[:, at + k:at + k + 1]

        def sw(name, **dims):
            at, n = SW[name]
            ap = small[:, at:at + n]
            return ap.rearrange(f"p ({' '.join(dims)}) -> p {' '.join(dims)}", **dims) if dims else ap

        ident = c("ident")
        squares, mem_squares = sq[:, 2, :], sq[:, 3, :]

        r = Region(arena, 0, ARENA)
        hidden = r.take(KF, NT)
        silu = r.take(2, NT)

        r = Region(arena, 0, ARENA)
        p = r.take(RW, NT)
        MIX = r.at
        r = Region(arena, MIX, ARENA)
        rows1 = r.at
        ptmp = r.take(2, NT + 1)
        diff = r.take(NT)
        cq = r.take(QT, NT)
        kr_raw = r.take(NT)
        qr = r.take(2, NT)
        past2 = r.at
        kr_group = r.take(4, SEQ)
        qn = r.take(NJ, NT)
        qr_raw = r.take(2, NT)
        rows0 = r.at
        prob = r.take(2, 512)
        prob_t = r.take(3, 512)
        shift_out = r.take(RW, NS + 1)
        ckv = r.take(NT)
        kr = r.take(NT)
        qr_group = r.take(4, H, NS)
        qlat = r.take(H, NT)
        olat = r.take(H, NT)
        ckv_tok = r.take(2, CL)
        stat = r.take(10, H)
        ckv_t = r.take(JS, P)
        kr_t = r.take(2, 4 * P)
        s_max = r.take(NS, 5)
        s_stat = r.take(4, NS)
        past_ckv = [r.take(JS * CL), r.take(JS * CL)]
        past_kr = [r.take(JS * ROPE), r.take(JS * ROPE)]
        r = Region(arena, past2, rows0)
        past_ckv.append(r.take(JS * CL))
        past_kr.append(r.take(JS * ROPE))
        r = Region(arena, rows0, rows0 + 5 * 512)
        s_rows = [r.take(PAST)]
        s_pt = r.take(JS, H)
        s_o = r.take(2, CL)
        r = Region(arena, rows1, past2)
        s_rows.append(r.take(PAST))

        r = Region(arena, MIX, ARENA)
        AR = [r.take(NJ, 2, P)]
        Bt = [r.take(NJ, P)]
        Kt = [r.take(NJ, P)]
        din = [r.take(NJ, P)]
        tok = r.take(4, 512)
        U = r.take(H * HD)
        Z = r.take(3, NJ * P)
        dcm = r.take(NJ, P)
        wstat = r.take(NT)
        SOLVE = r.at
        MR_b = r.take(H, 2 * P)
        MR_k = r.take(H, 2 * P)
        Ml = r.take(H, P)
        X = r.take(H, P)
        XT = r.take(H, P)
        Y = r.take(H, P)
        G, Y0, WT = Ml.rearrange("p a b -> p (a b)")[:, 0:512], X.rearrange("p a b -> p (a b)")[:, 0:512], Y[:, 0:NJ, :]
        dex, dinv = [X[:, 0:NJ, :]], [X[:, NJ:H, :]]
        r = Region(ring_b[:].rearrange("p u k n -> p (u k n)"), 0, 2 * KF * P)
        logw = r.take(NJ, NT)
        cum = r.take(NJ, SEQ)
        iclr = r.take(NJ, NT)
        kk = r.take(NJ, NT)
        w1 = r.take(NJ, NT)
        svb = r.take(6, HD)
        r = Region(ring_a[:].rearrange("p u g k n -> p (u g k n)"), 0, 4 * KD * P)
        S = r.take(32, HD)
        w2 = Region(r.tensor, r.at, r.end).take(NJ, NT)
        St = r.take(32, HD)
        r = Region(r.tensor, 0, r.end)
        AR.append(r.take(NJ, 2, P))
        for half in (Bt, Kt, din, dex, dinv):
            half.append(r.take(NJ, P))
        r = Region(sq[:].rearrange("p k n -> p (k n)"), 3 * NT, KD * NT)
        lora = r.take(NT)
        sv = r.take(NJ, 6, NS)
        sv_tok = Region(r.tensor, 0, 3 * NT).take(NJ * P)
        svv = r.take(32)
        skk = r.take(32)
        so = r.take(32)
        so_tok = r.take(NJ * P)
        r = Region(arena, SOLVE, ARENA)
        gate = r.take(NJ, NT)
        bonus = r.take(NJ, NT)
        e1 = r.take(NJ, NT)
        e2 = r.take(NJ, NT)
        mixT = hT

        r = Region(arena, 0, ARENA)
        memg = r.take(KD, NM)
        KT = r.take(KD, NM)
        V = r.take(2, D)
        q = r.take(KD, NT)
        o = r.take(KD, NT)
        m_prob = r.take(4, 512)
        m_prob_t = r.take(MH, 2, SEQ)
        mem_k = r.take(2, KD * NM)
        mem_v = r.take(2, 2 * D)
        m_rows = r.take(NS, NM)
        m_pt = r.take(NS, 2, MH)
        m_st = r.take(8, 8)
        oT = mixT[:, 0:NJ, :]

        def mm(out, lhsT, rhs, start=True, stop=True):
            return nc.tensor.matmul(out, lhsT, rhs, start=start, stop=stop)

        def tp(out, in_, n=P):
            return nc.tensor.transpose(out, in_, ident[0:n, 0:n])

        kept = {}

        def wait_apart(engine, *waits):
            for s, value in waits:
                engine.wait_ge(s, value)
            if engine.engine in kept:
                engine.reg_alu(kept[engine.engine], kept[engine.engine], 16 * 3, ALU.bitwise_and)

        def keep_register(engine):
            kept[engine.engine] = engine.alloc_register("kept")
            engine.reg_mov(kept[engine.engine], 16 * 3)

        def use_register(engine):
            engine.wait_ge(signal("inputs_loaded").sem, engine.snap(kept[engine.engine]))

        block = ctx.enter_context(nc.Block())

        @block.sync
        def _(sp):
            where["phase"] = "before"
            loaded = signal("inputs_loaded")
            loaded.by(sp.dma_start(con[:], t["constants"]))
            loaded.by(sp.dma_start(vectors[:], t["vectors"]))
            loaded.by(sp.dma_start(xT[:], t["x"]))

            def ffn(f, layer):
                gu, down = t[f"ffn{f + 1}_gu"], t[f"ffn{f + 1}_down"]
                with sp.Fori(0, KF // 2) as i:
                    for u in range(2):
                        sp.wait_ge(*signal(f"gu_used{u}").at(f * (KF // 2) + i))
                        signal(f"gu_loaded{u}").by(
                            sp.dma_start(ring_a[:, u], gu[layer, 2 * i + u]), KF // 2)
                with sp.Fori(0, KD // 2) as i:
                    for u in range(2):
                        sp.wait_ge(*signal(f"down_used{u}").at(f * (KD // 2) + i))
                        signal(f"down_loaded{u}").by(
                            sp.dma_start(ring_b[:, u], down[layer, 2 * i + u]), KD // 2)

            def used(n):
                for first, name in ((C_O, "cross_ready"), (C_MEMV, "v_ready"), (C_MEMK, "kt_ready"),
                                    (C_Q, "mq_ready"), (C_OUT, "mix_ready"), (C_IN, "proj_ready")):
                    if n >= first:
                        return signal(name).at(2 * (n - first) + 2)

            def blocks(layer):
                for n in range(C_BLOCKS):
                    sp.wait_ge(*(used(n - C_SLOTS) if n >= C_SLOTS else signal("cross_ready").at(0)))
                    signal(f"block_loaded{n % C_SLOTS}").by(
                        sp.dma_start(ring_c[:, n % C_SLOTS], t["blocks"][layer, n]))

            where["phase"] = "layer"
            with sp.Fori(0, DEPTH) as layer:
                where["layer"] = layer
                ffn(0, layer)
                blocks(layer)
                ffn(1, layer)

        @block.gpsimd
        def _(pool):
            chain = Chain(pool, signal("pool_step"))
            stored = signal("stored")
            where["phase"] = "before"
            signal("index_loaded").by(pool.dma_start(rows_idx[:], t["pages"]))
            signal("index_loaded").by(pool.dma_start(part_idx[:], t["page_part"]))
            ckv_rows = t["cache_ckv"].rearrange("l n (e t) c -> (l n e) (t c)", e=PER)
            kr_rows = t["cache_krope"].rearrange("l n (e t) c -> (l n e) (t c)", e=PER)

            def gather(b):
                at = bass.IndirectOffsetOnAxis(ap=rows_idx[:, b:b + 1], axis=0)
                signal(f"past_loaded{b % 3}").by(pool.indirect_dma_start(past_ckv[b % 3], None, ckv_rows, at))
                signal(f"past_loaded{b % 3}").by(pool.indirect_dma_start(past_kr[b % 3], None, kr_rows, at))

            where["phase"] = "layer"
            keep_register(pool)
            with pool.Fori(0, DEPTH) as layer:
                where["layer"] = layer
                wait_apart(pool, signal("mix_added").at(0),
                           signal("cross_added").at(0))
                signal("small_loaded").by(pool.dma_start(small[:], t["small"][layer]))
                signal("small_loaded").by(pool.dma_start(shift0[:], t["shift0"][layer]))
                wait_apart(pool, signal("index_ready").at(0))
                gather(0)
                gather(1)
                wait_apart(pool, signal("ckv_ready").at(1),
                           signal("kr_ready").at(1))
                stored.by(pool.dma_start(t["o_ckv"][layer], ckv))
                stored.by(pool.dma_start(t["o_krope"][layer], kr[0:ROPE, :]))
                wait_apart(pool, signal("shifted").at(RW))
                stored.by(pool.dma_start(t["o_shift"][layer], shift_out))
                wait_apart(pool, signal("olat_out").at(6))
                gather(2)
                signal("state_loaded").by(
                    pool.dma_start(S, t["state_wkv"][layer].rearrange("b h (a v) k -> (b h a) v k", a=2)))
                for b in range(3, NS):
                    wait_apart(pool, signal("pv_ready").at(b - 2))
                    gather(b)
                    if b != NS - 2:
                        continue
                    wait_apart(pool, signal("sv_tok_ready").at(1))
                    signal("sv_spread").by(
                        pool.dma_start(vec_dram.rearrange("n b f -> (n b) f"), sv_tok[0:6 * NS, :]))
                    wait_apart(pool, signal("sv_spread").at(1))
                    for n in range(6):
                        src = vec_dram[n].rearrange("b (h k) -> (b h) k", h=H)
                        src = src.rearrange("p (o k) -> p o k", o=1).broadcast_to([NS * H, 2, HD])
                        signal("svb_loaded").by(pool.dma_start(svb[:, n, :], src))
                    signal("svb_loaded").by(
                        pool.dma_start(svv, vec_dram[5].rearrange("b (g v) -> (b g) v", v=32)))
                wait_apart(pool, stored.at(3))
                wait_apart(pool, signal("state_ready").at(1))
                stored.by(pool.dma_start(t["o_wkv_s"][layer], S.rearrange("p a b -> p (a b)")))
                wait_apart(pool, signal("so_ready").at(1))
                signal("so_spread").by(
                    pool.dma_start(out_dram.rearrange("b (g v) -> (b g) v", v=32), so))
                wait_apart(pool, signal("so_spread").at(1))
                signal("so_loaded").by(pool.dma_start(so_tok[0:NS, :], out_dram))
                wait_apart(pool, stored.at(4))
                for T in range(2):
                    for n in range(1, LEVELS):
                        k = T * (LEVELS - 1) + n
                        wait_apart(pool, signal("mb_out").at(4 * T + 4))
                        if n > 1:
                            pool.wait_ge(*signal("y_ready").at(2 * k - 2))
                        for g in range(2):
                            ins = nc.gpsimd.tensor_tensor(
                                Ml[:, 4 * g:4 * g + 4, :], MR_b[:, 4 * g:4 * g + 4, 0:P],
                                c("lvl", LEVELS)[:, n:n + 1, :].broadcast_to([P, 4, P]), ALU.mult)
                            signal("level_ready").by(ins)
                wait_apart(pool, signal("z_out").at(4))
                stored.by(pool.dma_start(t["o_wkv"][layer], Z[:, 1, :].rearrange("p (j v) -> p j v", j=NJ)))
                wait_apart(pool, stored.at(5))
                wait_apart(pool, signal("rwkv_mixed").at(NJ))
                signal("mem_loaded").by(pool.dma_start(memg, t["mem"]))

                def load_keys(b):
                    if b >= 2:
                        wait_apart(pool, signal("mem_k_used").at(b - 1))
                    signal(f"mem_k_loaded{b % 2}").by(
                        pool.dma_start(mem_k[:, b % 2, :], t["mem_k"][layer, b].rearrange("p a b -> p (a b)")))

                def load_values(b):
                    if b >= 2:
                        wait_apart(pool, signal("mem_v_used").at(b - 1))
                    signal(f"mem_v_loaded{b % 2}").by(
                        pool.dma_start(mem_v[:, b % 2, :], t["mem_v"][layer, b].rearrange("p a b -> p (a b)")))

                wait_apart(pool, signal("mix_added").at(KD))
                for b in range(2):
                    load_keys(b)
                    load_values(b)
                wait_apart(pool, signal("kt_out").at(KD))
                stored.by(pool.dma_start(t["o_mem_k"][layer], KT))
                for b in range(2, NS):
                    load_keys(b)
                wait_apart(pool, signal("v_out").at(8))
                stored.by(pool.dma_start(t["o_mem_v"][layer], V))
                for b in range(2, NS):
                    load_values(b)
                wait_apart(pool, stored.at(7))
            use_register(pool)
            where["phase"] = "after"
            wait_apart(pool, signal("final_ready").at(1))
            stored.by(pool.dma_start(t["y"], hT[:]))
            wait_apart(pool, stored.at(1))

        @block.tensor
        def _(pe):
            def sum_squares(into=6, memory=False):
                signal("sumsq_ready").by(mm(bank[into][:, 0:NT], ones[:], mem_squares if memory else squares))

            def ffn(f):
                wait_apart(pe, signal("h_ready").at(6 * f + 1))
                with pe.Fori(0, KF // 2) as i:
                    for u in range(2):
                        at = f * (KF // 2) + i
                        pe.wait_ge(*signal(f"gu_loaded{u}").at(at + 1))
                        pe.wait_ge(*signal(f"silu_ready{u}").at(at))
                        for k in range(KD):
                            if k == KD // 2:
                                pe.wait_ge(*signal("h_ready").at(6 * f + 2))
                            last = mm(bank[u][:, 0:NT], ring_a[:, u, 0, k, :], hT[:, k, :], k == 0, k == KD - 1)
                        signal(f"gate_ready{u}").by(last, KF // 2)
                        pe.wait_ge(*signal(f"hidden_ready{u}").at(at))
                        for k in range(KD):
                            last = mm(bank[2 + u][:, 0:NT], ring_a[:, u, 1, k, :], hT[:, k, :], k == 0, k == KD - 1)
                        signal(f"gu_used{u}").by(last, KF // 2)
                wait_apart(pe, *(signal(f"hidden_ready{u}").at((f + 1) * (KF // 2)) for u in range(2)))
                with pe.Fori(0, KD // 2) as i:
                    for u in range(2):
                        at = f * (KD // 2) + i
                        pe.wait_ge(*signal(f"down_loaded{u}").at(at + 1))
                        pe.wait_ge(*signal(f"ffn_added{u}").at(at))
                        for k in range(KF):
                            last = mm(bank[4 + u][:, 0:NT], ring_b[:, u, k, :], hidden[:, k, :], k == 0, k == KF - 1)
                        signal(f"down_used{u}").by(last, KD // 2)

            def block_of(n):
                pe.wait_ge(*signal(f"block_loaded{n % C_SLOTS}").at(n // C_SLOTS + 1))
                return ring_c[:, n % C_SLOTS, :]

            def project(first, tile, n, rhs, ready, width=NT, h=None):
                blk = first + tile // 2
                if tile % 2 == 0:
                    block_of(blk)
                w = ring_c[:, blk % C_SLOTS, :].rearrange("p (u k n) -> p u k n", u=2, k=KD)
                for k in range(KD):
                    if h and tile == 0 and k % (KD // 2) == 0:
                        pe.wait_ge(*signal("h_ready").at(h + 2 * k // KD))
                    last = mm(bank[n][:, 0:width], w[:, tile % 2, k, :], rhs[:, k, 0:width], k == 0, k == KD - 1)
                signal(ready).by(last)
                return last

            def mixing():
                for n in range(18):
                    if n >= 4:
                        pe.wait_ge(*signal("proj_out").at(n - 3))
                    project(C_IN, n, n % 4, hT, "proj_ready", h=3)
                    if n == 5:
                        pe.wait_ge(*signal("mla_sq_ready").at(2))
                        for k in range(QT):
                            last = mm(bank[4][:, 0:NT], ones[:], sq[:, k, :], k == 0, k == QT - 1)
                        signal("mla_sum_ready").by(last)
                        signal("mla_sum_ready").by(mm(bank[5][:, 0:NT], ones[:], sq[:, QT, :]))
                        signal("rot_ready").by(mm(bank[6][:, 0:NT], c("rot"), kr_raw))
                pe.wait_ge(*signal("small_loaded").at(2))
                pe.wait_ge(*signal("cq_ready").at(1))
                pe.wait_ge(*signal("proj_out").at(18))
                un = sw("uq_nope", a=QT, j=NJ, n=P)
                ur = sw("uq_rope", a=QT, j=2, n=P)
                for j in range(NJ):
                    for k in range(QT):
                        last = mm(bank[j][:, 0:NT], un[:, k, j, :], cq[:, k, :], k == 0, k == QT - 1)
                    signal("q_ready").by(last)
                pe.wait_ge(*signal("ckv_ready").at(1))
                for g in range(2):
                    for k in range(QT):
                        last = mm(bank[4 + g][:, 0:NT], ur[:, k, g, :], cq[:, k, :], k == 0, k == QT - 1)
                    signal("q_ready").by(last)
                pe.wait_ge(*signal("kr_ready").at(1))
                for T in range(2):
                    last = tp(bank[6][:, T * P:T * P + P], ckv[:, T * P:T * P + P])
                signal("ckv_turned").by(last)
                for g in range(2):
                    pe.wait_ge(*signal("q_out").at(NJ + g + 1))
                    signal("rot_ready").by(mm(bank[4 + g][:, 0:NT], c("rot"), qr_raw[:, g, :]))
                uk = sw("uk", j=NJ, n=CL)
                for h in range(H):
                    o0 = NOPE * (h % 2)
                    pe.wait_ge(*signal("q_out").at(min(NJ, h // 2 + 1) if h < 4 else NJ))
                    if h >= 4:
                        pe.wait_ge(*signal("qlat_out").at(h - 3))
                    signal("qlat_ready").by(mm(bank[h % 4][:, 0:NT], uk[o0:o0 + NOPE, h // 2, :],
                                               qn[o0:o0 + NOPE, h // 2, :]))
                pe.wait_ge(*signal("qr_ready").at(2))
                sel = c("sel", 4)
                for h in range(H):
                    last = mm(bank[7][:, h * NS:h * NS + NS], sel[:, h % 4, :], qr[:, h // 4, SEQ:NT])
                signal("qs_ready").by(last)
                prompt_attention()
                sample_attention()

                uv = sw("uv")
                pe.wait_ge(*signal("olat_out").at(6))
                pe.wait_ge(*signal("sample_out").at(NS))
                for j in range(NJ):
                    for o0 in (0, 1):
                        h = 2 * j + o0
                        last = mm(bank[j][HD * o0:HD * o0 + HD, 0:NT], uv[:, h * HD:h * HD + HD], olat[:, h, :])
                    signal("omla_ready").by(last)

            def prompt_attention():
                units = [(0, 0, 4), (0, 4, 4)] + [(1, h, 2) for h in range(0, H, 2)]

                def scores(u):
                    qt, h0, nh = units[u]
                    if u >= 2:
                        pe.wait_ge(*signal("score_out").at(u - 1))
                    for i in range(nh):
                        h, n = h0 + i, (qt + 1) * P
                        out = bank[u % 2][:, i * n:i * n + n]
                        mm(out, qlat[:, h, qt * P:qt * P + P], ckv[:, 0:n], True, False)
                        last = mm(out, qr[:, h // 4, qt * P:qt * P + P], kr_group[:, h % 4, 0:n], False, True)
                    signal("score_ready").by(last)

                pe.wait_ge(*signal("qlat_out").at(H))
                scores(0)
                scores(1)
                for u, (qt, h0, nh) in enumerate(units):
                    if u + 2 < len(units):
                        scores(u + 2)
                    pe.wait_ge(*signal("prob_ready").at(u + 1))
                    if u >= 2:
                        pe.wait_ge(*signal("prob_t_out").at(u - 1))
                    for i in range(4):
                        last = tp(bank[2 + u % 2][:, i * P:i * P + P], prob[:, u % 2, i * P:i * P + P])
                    signal("prob_t_ready").by(last)
                    pe.wait_ge(*signal("prob_t_out").at(u + 1))
                    if u >= 2:
                        pe.wait_ge(*signal("olat_out").at(u - 1))
                    rhs = prob_t[:, u % 3, :]
                    if qt == 0:
                        last = mm(bank[4 + u % 2][:, 0:512], ckv_tok[:, 0, :], rhs)
                    else:
                        two = rhs.rearrange("p (h k q) -> p h k q", h=2, k=2)
                        for k in range(2):
                            last = mm(bank[4 + u % 2][:, 0:256], ckv_tok[:, k, :], two[:, :, k, :], k == 0, k == 1)
                    signal("olat_ready").by(last)

            def sample_attention():

                def turn(m):
                    b, n = m // 4, m % 4
                    if n == 0:
                        pe.wait_ge(*signal(f"past_loaded{b % 3}").at(2 * (b // 3) + 2))
                    if m >= 3:
                        pe.wait_ge(*ckv_t_out(m - 3))
                    if n == 0:
                        if b:
                            pe.wait_ge(*signal("kr_t_out").at(b))
                            bank7_read(3 * b)
                        for i in range(4):
                            last = tp(bank[7][:, i * P:i * P + P], past_kr[b % 3][:, i * P:i * P + P])
                        signal("kr_turned").by(last)
                    for i in range(4):
                        j = 4 * n + i
                        last = tp(bank[m % 3][:, i * P:i * P + P], past_ckv[b % 3][:, j * CL:j * CL + CL])
                    signal("turned").by(last)

                def ckv_t_out(m):
                    return signal("ckv_t_act" if m % 2 else "ckv_t_dve").at(m // 2 + 1)

                def bank7_read(s):
                    if 0 < s <= 8:
                        pe.wait_ge(*signal("wa_out").at(s))
                    elif 8 < s <= SV_STEP:
                        pe.wait_ge(*signal("kk_norm_out").at(min(s, 12) - 8))
                    elif s > SV_STEP:
                        pe.wait_ge(*signal("sv_tok_ready").at(1))

                def prepare_rwkv(s):
                    if s > SV_STEP or 12 <= s < SV_STEP:
                        return
                    bank7_read(s)
                    out = bank[7][:, 0:NT]
                    if s < 8:
                        i, j = s // NJ, s % NJ
                        pe.wait_ge(*signal("lora_ready").at(2))
                        signal("wa_ready").by(mm(out, sw("wa_up")[64 * i:64 * i + 64, j * P:j * P + P],
                                                 lora[64 * i:64 * i + 64, :]))
                    elif s < 12:
                        pe.wait_ge(*signal("kk_squared").at(1))
                        signal("kk_norm").by(mm(out, c("blk"), w2[:, s - 8, :]))
                    else:
                        wait_apart(pe, signal("sv_ready").at(1))
                        for j in range(NJ):
                            last = tp(bank[7][0:6 * NS, j * P:j * P + P], sv[:, j, :, :].rearrange("p n b -> p (n b)"))
                        signal("sv_turned").by(last)

                def scores(m):
                    b, n = m // 4, m % 4
                    pe.wait_ge(*ckv_t_out(m))
                    if n == 0:
                        pe.wait_ge(*signal("kr_t_out").at(b + 1))
                    if m >= 2:
                        pe.wait_ge(*signal("s_rows_out").at(m - 1))
                    out = bank[4 + m % 2]
                    mm(out[0:H, 0:512], qlat[:, :, SEQ + b], ckv_t[:, 4 * n:4 * n + 4, :], True, False)
                    for g in range(4):
                        last = mm(out[0:H, g * P:g * P + P], qr_group[:, g, :, b], kr_t[:, b % 2, n * P:n * P + P], False, g == 3)
                    signal("s_ready").by(last)

                def turn_probabilities(b):
                    wait_apart(pe, signal("s_exp_ready").at(b + 1))
                    if b:
                        wait_apart(pe, signal("pt_out").at(b))
                    for j in range(JS):
                        last = tp(bank[3][:, j * H:j * H + H], s_rows[b % 2][0:H, j * P:j * P + P], H)
                    signal("pt_ready").by(last)

                def values(b):
                    pe.wait_ge(*signal("pt_out").at(b + 1))
                    if b:
                        pe.wait_ge(*signal("sample_out").at(b))
                    mm(bank[6][0:H, P:2 * P], ckv[:, SEQ + b:SEQ + b + 1].broadcast_to([P, H]), ident)
                    for j in range(JS):
                        last = mm(bank[6][0:H, 0:P], s_pt[:, j, :], past_ckv[b % 3][:, j * CL:j * CL + CL],
                                  j == 0, j == JS - 1)
                    signal("pv_ready").by(last)

                def turn_outputs(b):
                    wait_apart(pe, signal("o_rows").at(b + 1))
                    if b:
                        wait_apart(pe, signal("sample_out").at(b))
                    signal("o_turned").by(tp(bank[6][:, 256:256 + H], s_o[0:H, b % 2, :], H))

                pe.wait_ge(*signal("qs_out").at(1))
                pe.wait_ge(*signal("prob_t_out").at(6))
                pe.wait_ge(*signal("olat_out").at(6))
                for b in range(NS):
                    out = bank[6][0:H, 272 + b:273 + b]
                    mm(out, qlat[:, :, SEQ + b], ckv[:, SEQ + b:SEQ + b + 1], True, False)
                    last = mm(out, qr_group[:, 0, :, b], kr[:, SEQ + b:SEQ + b + 1], False, True)
                signal("snew_ready").by(last)
                for m in range(4 * NS + 6):
                    if m < 4 * NS:
                        turn(m)
                    if 0 <= m - 2 < 4 * NS:
                        scores(m - 2)
                    if m < 4 * NS and m % 4:
                        if m % 4 == 1:
                            pe.wait_ge(*signal("kr_t_out").at(m // 4 + 1))
                        prepare_rwkv(3 * (m // 4) + m % 4 - 1)
                    if m >= 7:
                        stage, b = (turn_probabilities, values, turn_outputs, None)[(m - 7) % 4], (m - 7) // 4
                        if stage and b < NS:
                            stage(b)

            def rwkv():
                pe.wait_ge(*signal("omla_out").at(NJ))
                wait_apart(pe, signal("so_loaded").at(1))
                for j in range(NJ):
                    last = tp(bank[5][:, j * NS:j * NS + NS], so_tok[0:NS, j * P:j * P + P], NS)
                signal("so_turned").by(last)
                pe.wait_ge(*signal("so_out").at(1))
                for T in range(2):
                    solve(T)
                    for cc in range(2):
                        chunk(T, cc)
                    outputs(T)
                pe.wait_ge(*signal("rwkv_out").at(2))
                pe.wait_ge(*signal("z_out").at(4))
                for j in range(NJ):
                    last = mm(bank[j][:, 0:NT], c("blk"), oT[:, j, :])
                signal("gn_mean").by(last)
                pe.wait_ge(*signal("rkr_ready").at(1))
                for j in range(NJ):
                    last = mm(bank[4 + j][:, 0:NT], c("blk"), e1[:, j, :])
                signal("bonus_ready").by(last)
                pe.wait_ge(*signal("gn_squared").at(1))
                pe.wait_ge(*signal("centred").at(1))
                for j in range(NJ):
                    last = mm(bank[j][:, 0:NT], c("blk"), e2[:, j, :])
                signal("gn_var").by(last)
                pe.wait_ge(*signal("bonus_out").at(1))
                pe.wait_ge(*signal("gd_ready").at(1))
                for j in range(NJ):
                    last = mm(bank[4 + j][:, 0:NT], sw("g_up")[:, j * P:j * P + P], wstat)
                signal("gate_up").by(last)

            def head(n):
                return 2 * (n % NJ) + n // NJ

            def solve(T):
                pe.wait_ge(*signal("operands_ready").at(T + 1))
                if T:
                    pe.wait_ge(*signal("rwkv_out").at(T))
                    pe.wait_ge(*signal("z_out").at(2 * T))
                turned = [AR[T][:, :, 0, :], Bt[T], Kt[T], p[:, 8:12, T * P:T * P + P]]
                for n, src in enumerate(turned):
                    for j in range(NJ):
                        last = tp(bank[n][:, j * P:j * P + P], src[:, j, :])
                    signal("tok_turned").by(last)
                for n in range(4):
                    for i in range(2):
                        m = 2 * n + i
                        o0, j = HD * (m // NJ), m % NJ
                        last = mm(bank[4 + n][:, 256 * i:256 * i + 256], Bt[T][o0:o0 + HD, j, :],
                                  AR[T][o0:o0 + HD, j, :, :])
                    signal("pairs_ready").by(last)
                for n in range(4):
                    pe.wait_ge(*signal("tok_out").at(4 * T + n + 1))
                    for i in range(2):
                        m = 2 * n + i
                        o0, j = HD * (m // NJ), m % NJ
                        last = mm(bank[n][:, 256 * i:256 * i + 256], Kt[T][o0:o0 + HD, j, :],
                                  AR[T][o0:o0 + HD, j, :, :])
                    signal("pairs_ready").by(last)
                for g in range(2):
                    pe.wait_ge(*signal("mb_out").at(4 * T + g + 1))
                    for j in range(NJ):
                        last = mm(bank[4 + g][:, j * P:j * P + P], AR[T][HD * g:HD * g + HD, j, 0, :],
                                  Bt[T][HD * g:HD * g + HD, j, :])
                    signal("pairs_ready").by(last)
                pe.wait_ge(*signal("mk_out").at(4 * T + 4))
                for n in range(1, LEVELS):
                    for g in range(2):
                        k = 2 * (T * (LEVELS - 1) + n - 1) + g + 1
                        pe.wait_ge(*signal("level_ready").at(k))
                        pe.wait_ge(*signal("x_out").at(k + 2 * T))
                        for i in range(4):
                            m = 4 * g + i
                            last = mm(bank[g][:, i * P:i * P + P], Ml[:, m, :], X[:, m, :])
                        signal("y_ready").by(last)
                    for g in range(2):
                        k = 2 * (T * (LEVELS - 1) + n - 1) + g + 1
                        pe.wait_ge(*signal("y_out").at(k))
                        if n < LEVELS - 1:
                            for i in range(4):
                                m = 4 * g + i
                                mm(bank[2 + g][:, i * P:i * P + P], XT[:, m, :], Y[:, m, :])
                        for i in range(4):
                            m = 4 * g + i
                            last = mm(bank[4 + g][:, i * P:i * P + P], Y[:, m, :], XT[:, m, :])
                        signal("xy_ready").by(last)
                for m in range(H):
                    h = head(m)
                    last = mm(bank[6][:, h * HD:h * HD + HD], MR_k[:, m, 0:P], tok[:, 3, h * HD:h * HD + HD])
                signal("g_ready").by(last)
                pe.wait_ge(*signal("g_out").at(T + 1))
                pe.wait_ge(*signal("x_out").at(2 * (T + 1) * LEVELS))
                for m in range(H):
                    h = head(m)
                    last = mm(bank[7][:, h * HD:h * HD + HD], XT[:, m, :], G[:, h * HD:h * HD + HD])
                signal("y0_ready").by(last)
                for m in range(H):
                    h = head(m)
                    o0 = HD * (h % 2)
                    last = mm(bank[6][o0:o0 + HD, (h // 2) * P:(h // 2) * P + P], tok[:, 0, h * HD:h * HD + HD],
                              XT[:, m, :])
                signal("wt_ready").by(last)

            def chunk(T, cc):
                n, o0 = 2 * T + cc, CHUNK * cc
                if n:
                    pe.wait_ge(*signal("z_out").at(n))
                if cc == 0:
                    pe.wait_ge(*signal("wt_out").at(T + 1))
                if n == 0:
                    pe.wait_ge(*signal("z_cleared").at(1))
                for j in range(NJ):
                    last = mm(bank[0][o0:o0 + CHUNK, j * P:j * P + P], WT[:, j, o0:o0 + CHUNK],
                              Z[:, n % 3, j * P:j * P + P])
                signal("u_ready").by(last)
                pe.wait_ge(*signal("u_out").at(n + 1))
                for j in range(NJ):
                    cols = slice(j * P, j * P + P)
                    mm(bank[1][:, cols], tok[o0:o0 + CHUNK, 1, cols], U[o0:o0 + CHUNK, cols], True, False)
                    last = mm(bank[1][:, cols], tok[o0:o0 + CHUNK, 2, cols], tok[o0:o0 + CHUNK, 3, cols], False, True)
                signal("z_ready").by(last)

            def outputs(T):
                for j in range(NJ):
                    out = bank[2][:, j * P:j * P + P]
                    for cc in range(2):
                        nc.tensor.matmul(out[:, CHUNK * cc:CHUNK * cc + CHUNK], Z[:, (2 * T + cc) % 3, j * P:j * P + P],
                                         AR[T][:, j, 1, CHUNK * cc:CHUNK * cc + CHUNK], start=cc == 0, stop=False,
                                         skip_group_check=True)
                    for i in range(2):
                        h, m = 2 * j + i, NJ * i + j
                        part = out[HD * i:HD * i + HD, :]
                        nc.tensor.matmul(part, U[:, h * HD:h * HD + HD], MR_b[:, m, P:2 * P], start=False,
                                         stop=False, skip_group_check=True)
                        last = nc.tensor.matmul(part, tok[:, 3, h * HD:h * HD + HD], MR_k[:, m, P:2 * P],
                                                start=False, stop=True, skip_group_check=True)
                signal("rwkv_ready").by(last)

            def mix_out():
                def half(n, half):
                    w = block_of(C_OUT + n // 2).rearrange("p (u k n) -> p u k n", u=2, k=KD)
                    for j in range(NJ):
                        k = j if half else NJ + j
                        if half:
                            pe.wait_ge(*signal("rwkv_mixed").at(j + 1))
                        last = mm(bank[4 + n % 4][:, 0:NT], w[:, n % 2, k, :], mixT[:, k, :], k == NJ, k == NJ - 1)
                    return last

                pe.wait_ge(*signal("gate_out").at(1))
                for n in range(4):
                    half(n, 0)
                for n in range(KD):
                    if n >= 4:
                        pe.wait_ge(*signal("mix_added").at(n - 3))
                        half(n, 0)
                    signal("mix_ready").by(half(n, 1))

            def cross():
                pe.wait_ge(*signal("squares_added").at(KD))
                pe.wait_ge(*signal("mix_added").at(KD))
                sum_squares(5)
                for n in range(KD):
                    if n >= 4:
                        pe.wait_ge(*signal("mq_out").at(n - 3))
                    if n == 6:
                        pe.wait_ge(*signal("squares_added").at(2 * KD))
                        sum_squares(memory=True)
                    project(C_Q, n, n % 4, hT, "mq_ready", h=5)
                pe.wait_ge(*signal("memg_ready").at(1))
                for n in range(KD):
                    pe.wait_ge(*signal("mq_out" if n < 4 else "kt_out").at(KD if n < 4 else n - 3))
                    project(C_MEMK, n, n % 4, memg, "kt_ready", NM)
                pe.wait_ge(*signal("kt_out").at(KD))
                for n in range(8):
                    b, T = n, n % 2
                    w = (block_of(C_MEMV + n // 2) if T == 0 else w)
                    wv = w.rearrange("p (k n) -> p k n", k=KD)
                    if n >= 2:
                        pe.wait_ge(*signal("v_out").at(n - 1))
                    for k in range(KD):
                        last = mm(bank[4 + T][:, 0:256], memg[:, k, T * P:T * P + P], wv[:, k, :], k == 0, k == KD - 1)
                    signal("v_ready").by(last)
                    pe.wait_ge(*signal(f"mem_k_loaded{b % 2}").at(b // 2 + 1))
                    if b >= 4 and b % 2 == 0:
                        pe.wait_ge(*signal("ms_rows").at(b // 2 - 1))
                    kt_b = mem_k[:, b % 2, :].rearrange("p (k m) -> p k m", k=KD)
                    for h in range(MH):
                        out = bank[6 + b // 2 % 2][32 * h:32 * h + 32, (b % 2) * NM:(b % 2) * NM + NM]
                        for dt in range(2):
                            k = 2 * h + dt
                            last = mm(out, q[:, k, SEQ + b:SEQ + b + 1].broadcast_to([P, 32]), kt_b[:, k, :],
                                      dt == 0, dt == 1)
                    signal("mem_k_used").by(last)
                pe.wait_ge(*signal("v_out").at(8))

                units = [(qt, hp) for hp in range(2) for qt in range(2)]

                def scores(u):
                    qt, hp = units[u]
                    if u >= 2:
                        pe.wait_ge(*signal("m_exp_ready").at(u - 1))
                    for i in range(2):
                        for dt in range(2):
                            k = 2 * (2 * hp + i) + dt
                            last = mm(bank[4 + u % 2][:, i * NM:i * NM + NM], q[:, k, qt * P:qt * P + P], KT[:, k, :],
                                      dt == 0, dt == 1)
                    signal("m_score_ready").by(last)

                scores(0)
                scores(1)
                pe.wait_ge(*signal("ms_rows").at(4))
                for u in range(4):
                    if u + 2 < 4:
                        scores(u + 2)
                    pe.wait_ge(*signal("m_prob_ready").at(u + 1))
                    if u >= 2:
                        pe.wait_ge(*signal("m_prob_t_out").at(u - 1))
                    for i in range(4):
                        last = tp(bank[6 + u % 2][:, i * P:i * P + P], m_prob[:, u, i * P:i * P + P])
                    signal("m_prob_t_ready").by(last)
                for k in range(KD):
                    pe.wait_ge(*signal("m_prob_t_out").at(2 * (k // 4) + 2))
                    if k >= 2:
                        pe.wait_ge(*signal("mo_out").at(k - 1))
                    for mt in range(2):
                        last = mm(bank[k % 2][:, 0:SEQ], V[:, mt, k * P:k * P + P], m_prob_t[:, k // 2, mt, :],
                                  mt == 0, mt == 1)
                    signal("mo_ready").by(last)
                pe.wait_ge(*signal("ms_prob_ready").at(1))
                pe.wait_ge(*signal("m_exp_ready").at(4))
                for n in range(4):
                    for i in range(4):
                        b, mt = 2 * n + i // 2, i % 2
                        last = tp(bank[2 + n][:, i * P:i * P + P], m_rows[:, b, mt * P:mt * P + P])
                    signal("m_pt_ready").by(last)
                pe.wait_ge(*signal("m_prob_t_out").at(4))
                for b in range(NS):
                    pe.wait_ge(*signal(f"mem_v_loaded{b % 2}").at(b // 2 + 1))
                    pe.wait_ge(*signal("m_pt_out").at(b // 2 + 1))
                    if b >= 4 and b % 2 == 0:
                        pe.wait_ge(*signal("ms_outputs").at(b // 2 - 1))
                    v_b = mem_v[:, b % 2, :].rearrange("p (m n) -> p m n", m=2)
                    for h in range(MH):
                        out = bank[6 + b // 2 % 2][32 * h:32 * h + 32, (b % 2) * MD:(b % 2) * MD + MD]
                        for mt in range(2):
                            last = mm(out, m_pt[:, b, mt, h:h + 1].broadcast_to([P, 32]),
                                      v_b[:, mt, h * MD:h * MD + MD], mt == 0, mt == 1)
                    signal("mem_v_used").by(last)
                for n in range(4):
                    pe.wait_ge(*signal("ms_outputs").at(n + 1))
                    for i in range(4):
                        b, dt = 2 * n + i // 2, i % 2
                        last = tp(bank[2 + n][:, i * P:i * P + P], m_rows[:, b, dt * P:dt * P + P])
                    signal("mo_turned").by(last)
                pe.wait_ge(*signal("mo_out").at(KD + 4))
                for n in range(KD):
                    if n >= 4:
                        pe.wait_ge(*signal("cross_added").at(n - 3))
                    project(C_O, n, n % 4, o, "cross_ready")

            where["phase"] = "before"
            pe.wait_ge(*signal("inputs_loaded").at(3))
            pe.wait_ge(*signal("ones_ready").at(1))
            keep_register(pe)
            for name in 'gu_used0 gu_used1 down_used0 down_used1 cross_ready'.split():
                signal(name).grant(pe)
            where["phase"] = "layer"
            with pe.Fori(0, DEPTH) as layer:
                where["layer"] = layer
                for u in range(2):
                    pe.wait_ge(*signal(f"part_added{u}").at(0))
                sum_squares()
                ffn(0)
                for u in range(2):
                    pe.wait_ge(*signal(f"part_added{u}").at(KD // 2))
                sum_squares()
                mixing()
                rwkv()
                mix_out()
                cross()
                pe.wait_ge(*signal("squares_added").at(3 * KD))
                sum_squares()
                ffn(1)
            use_register(pe)
            where["phase"] = "after"
            for u in range(2):
                pe.wait_ge(*signal(f"part_added{u}").at(0))
            sum_squares()

        @block.scalar
        def _(act):
            chain = Chain(act, signal("act_step"))

            def run(out, in_, func=ACT.Copy, done=None, **more):
                chain(nc.scalar.activation(out, in_, func, **more), signal(done) if done else None)

            def root(ap):
                k = signal("root_ready").count[where["phase"]] + 1
                act.wait_ge(*signal("inverse_ready").at(k))
                run(ap, ap, ACT.Sqrt, "root_ready")

            def root_of_norm(width=NT):
                run(spare[:, 0:1], spare[:, 0:1], ACT.Sqrt)
                root(rstd[:, 0:width])

            def ffn(f):
                with act.Fori(0, KF // 2) as i:
                    for u in range(2):
                        at = f * (KF // 2) + i
                        act.wait_ge(*signal(f"gate_ready{u}").at(at + 1))
                        act.wait_ge(*signal(f"hidden_ready{u}").at(at))
                        signal(f"silu_ready{u}").by(
                            nc.scalar.activation(silu[:, u, :], bank[u][:, 0:NT], ACT.Silu), KF // 2)

            def mixing():
                dest = [cq[:, 0, :], cq[:, 1, :], ckv, kr_raw]
                for n in range(18):
                    act.wait_ge(*signal("proj_ready").at(n + 1))
                    if n >= 6:
                        act.wait_ge(*signal("shifted").at(n - 5))
                    run(dest[n] if n < 4 else ptmp[:, n % 2, 1:NT + 1], bank[n % 4][:, 0:NT], done="proj_out")
                    if n == 3:
                        run(sq[:, 0:QT, :].rearrange("p a b -> p (a b)"), cq.rearrange("p a b -> p (a b)"),
                            ACT.Square, "mla_sq_ready")
                        run(sq[:, QT, :], ckv, ACT.Square, "mla_sq_ready")
                    if n == 5:
                        root(rstd[:])
                        root(rstd[:])
                for j in range(NJ + 2):
                    act.wait_ge(*signal("q_ready").at(j + 1))
                    run(qn[:, j, :] if j < NJ else qr_raw[:, j - NJ, :], bank[j][:, 0:NT], done="q_out")
                for h in range(H):
                    act.wait_ge(*signal("qlat_ready").at(h + 1))
                    run(qlat[:, h, :], bank[h % 4][:, 0:NT], done="qlat_out")
                units = [(0, 0, 4), (0, 4, 4)] + [(1, h, 2) for h in range(0, H, 2)]

                def exponentials(u):
                    act.wait_ge(*signal("score_max_ready").at(u + 1))
                    nh = units[u][2]
                    n = 512 // nh
                    for i in range(nh):
                        row = prob[:, u % 2, i * n:i * n + n]
                        run(row, row, ACT.Exp, "exp_ready" if i == nh - 1 else None, scale=MLA_SCALE,
                            bias=stat[:, 2 * (u % 2), i:i + 1], accum_out=stat[:, 2 * (u % 2) + 1, i:i + 1])

                exponentials(0)
                for u, (qt, h0, nh) in enumerate(units):
                    if u + 1 < len(units):
                        exponentials(u + 1)
                    act.wait_ge(*signal("prob_t_ready").at(u + 1))
                    run(prob_t[:, u % 3, :], bank[2 + u % 2][:, 0:512], done="prob_t_out")
                    act.wait_ge(*signal("olat_ready").at(u + 1))
                    n = nh * P
                    run(olat[:, h0:h0 + nh, qt * P:qt * P + P],
                        bank[4 + u % 2][:, 0:n].rearrange("p (h q) -> p h q", h=nh), done="olat_out")
                run(lora[0:64, :], p[0:64, 12, :], ACT.Tanh, "lora_ready")
                run(lora[64:P, :], p[64:P, 12, :], ACT.Copy, "lora_ready")

                def prepare_rwkv(s):
                    if s < 8:
                        act.wait_ge(*signal("wa_ready").at(s + 1))
                        run((w1 if s < NJ else iclr)[:, s % NJ, :], bank[7][:, 0:NT], done="wa_out")
                    if s == 1:
                        act.wait_ge(*signal("kk_raw").at(1))
                        run(w2.rearrange("p a b -> p (a b)"), kk.rearrange("p a b -> p (a b)"), ACT.Square,
                            "kk_squared")
                    if s == 8:
                        for j in range(NJ):
                            run(w1[:, j, :], w1[:, j, :], ACT.Sigmoid, bias=v("w0", j),
                                done="decay_ready" if j == NJ - 1 else None)
                        for j in range(NJ):
                            run(iclr[:, j, :], iclr[:, j, :], ACT.Sigmoid, bias=v("a0", j),
                                done="iclr_ready" if j == NJ - 1 else None)
                    if s == 10:
                        act.wait_ge(*signal("logw_ready").at(1))
                        run(sv[:, :, 1, :], logw[:, :, SEQ:NT], ACT.Exp, "sv_decay")
                    if s == 11:
                        root(w2.rearrange("p a b -> p (a b)"))
                    if s == SV_STEP:
                        act.wait_ge(*signal("sv_turned").at(1))
                        run(sv_tok[0:6 * NS, :], bank[7][0:6 * NS, 0:512], done="sv_tok_ready")

                for m in range(4 * NS + 6):
                    if m < 4 * NS and m % 4 == 0:
                        act.wait_ge(*signal("kr_turned").at(m // 4 + 1))
                        if m >= 8:
                            act.wait_ge(*signal("s_ready").at(m - 4))
                        run(kr_t[:, m // 4 % 2, :], bank[7][:, 0:512], done="kr_t_out")
                    if m < 4 * NS and m % 2:
                        act.wait_ge(*signal("turned").at(m + 1))
                        if m >= 4:
                            act.wait_ge(*signal("s_ready").at(m - 3))
                        n = m % 4
                        run(ckv_t[:, 4 * n:4 * n + 4, :].rearrange("p a b -> p (a b)"), bank[m % 3][:, 0:512],
                            done="ckv_t_act")
                    if 0 <= m - 2 < 4 * NS:
                        b, n = (m - 2) // 4, (m - 2) % 4
                        act.wait_ge(*signal("s_ready").at(m - 1))
                        if n == 0 and b >= 2:
                            act.wait_ge(*signal("pt_ready").at(b - 1))
                        run(s_rows[b % 2][0:H, n * 512:n * 512 + 512], bank[4 + m % 2][0:H, 0:512], done="s_rows_out")
                        if n == 3:
                            act.wait_ge(*signal("s_bias_ready").at(b + 1))
                            bias = s_stat[0:H, 0, b:b + 1]
                            run(s_stat[0:H, 1, b:b + 1], s_max[0:H, b, 4:5], ACT.Exp, scale=MLA_SCALE, bias=bias)
                            run(s_rows[b % 2][0:H, :], s_rows[b % 2][0:H, :], ACT.Exp, "s_exp_ready", scale=MLA_SCALE,
                                bias=bias, accum_out=s_stat[0:H, 2, b:b + 1])
                    if m < 4 * NS and m % 4:
                        prepare_rwkv(3 * (m // 4) + m % 4 - 1)
                    if m >= 7 and (m - 7) % 4 == 0:
                        b = (m - 7) // 4
                        act.wait_ge(*signal("pt_ready").at(b + 1))
                        if b:
                            act.wait_ge(*signal("pv_ready").at(b))
                        run(s_pt.rearrange("p a b -> p (a b)"), bank[3][:, 0:P], done="pt_out")
                for j in range(NJ):
                    act.wait_ge(*signal("omla_ready").at(j + 1))
                    run(mixT[:, NJ + j, :], bank[j][:, 0:NT], done="omla_out")

            def rwkv():
                act.wait_ge(*signal("sample_out").at(NS))
                act.wait_ge(*signal("stored").at(3))

                def decays(T):
                    act.wait_ge(*signal("decays").at(T + 1))
                    run(dex[T], dex[T], ACT.Exp)
                    run(din[T], cum[:, :, T * P:T * P + P], ACT.Exp)
                    run(dinv[T], cum[:, :, T * P:T * P + P], ACT.Exp, "decays_ready", scale=-1.0)

                decays(0)
                for T in range(2):
                    for n in range(4):
                        act.wait_ge(*signal("tok_turned").at(4 * T + n + 1))
                        run(tok[:, n, :], bank[n][:, 0:512], done="tok_out", scale=-1.0 if n == 1 else 1.0)
                    for n in range(1, LEVELS):
                        for g in range(2):
                            k = 2 * (T * (LEVELS - 1) + n - 1) + g + 1
                            act.wait_ge(*signal("y_ready").at(k))
                            if n > 1:
                                act.wait_ge(*signal("xy_ready").at(k - 2))
                            run(Y[:, 4 * g:4 * g + 4, :].rearrange("p a b -> p (a b)"), bank[g][:, 0:512], done="y_out")
                        if T == 0 and n == 2:
                            decays(1)
                    act.wait_ge(*signal("g_ready").at(T + 1))
                    run(G, bank[6][:, 0:512], done="g_out")
                    act.wait_ge(*signal("y0_ready").at(T + 1))
                    run(Y0, bank[7][:, 0:512], done="y0_out")
                    act.wait_ge(*signal("wt_ready").at(T + 1))
                    run(WT.rearrange("p a b -> p (a b)"), bank[6][:, 0:512], done="wt_out")
                    act.wait_ge(*signal("rwkv_ready").at(T + 1))
                    run(oT[:, :, T * P:T * P + P], bank[2][:, 0:512].rearrange("p (j t) -> p j t", j=NJ),
                        done="rwkv_out")
                act.wait_ge(*signal("z_out").at(4))
                run(wstat, p[:, 13, :], ACT.Sigmoid, "gd_ready")
                act.wait_ge(*signal("centred").at(1))
                act.wait_ge(*signal("bonus_ready").at(1))
                run(e2.rearrange("p a b -> p (a b)"), oT_flat, ACT.Square, "gn_squared")
                act.wait_ge(*signal("gate_up").at(1))
                for j in range(NJ):
                    run(gate[:, j, :], bank[4 + j][:, 0:NT], done="gate_out" if j == NJ - 1 else None)
                run(spare[:], spare[:], ACT.Sqrt)
                root(e2.rearrange("p a b -> p (a b)"))

            oT_flat = oT.rearrange("p a b -> p (a b)")

            def cross():
                root_of_norm()
                for n in range(KD):
                    if n == 6:
                        root(rstd[:, 0:NM])
                    act.wait_ge(*signal("mq_ready").at(n + 1))
                    run(q[:, n, :], bank[n % 4][:, 0:NT], done="mq_out")
                for n in range(KD):
                    act.wait_ge(*signal("kt_ready").at(n + 1))
                    run(KT[:, n, :], bank[n % 4][:, 0:NM], done="kt_out")

                def rows(n):
                    return m_rows[:, 2 * n:2 * n + 2, :].rearrange("p b m -> p (b m)")

                for n in range(4):
                    act.wait_ge(*signal("mem_k_used").at(2 * n + 2))
                    run(rows(n), bank[6 + n % 2][:, 0:512], done="ms_rows")

                def exponentials(u):
                    act.wait_ge(*signal("m_max_ready").at(u + 1))
                    for i in range(2):
                        cols = slice(i * NM, i * NM + NM)
                        run(m_prob[:, u, cols], bank[4 + u % 2][:, cols], ACT.Exp, "m_exp_ready" if i else None,
                            scale=MEM_SCALE, bias=m_st[:, 2 + u, i:i + 1], accum_out=m_st[:, 6, 2 * u + i:2 * u + i + 1])

                exponentials(0)
                for u in range(4):
                    if u + 1 < 4:
                        exponentials(u + 1)
                    qt, hp = u % 2, u // 2
                    act.wait_ge(*signal("m_prob_t_ready").at(u + 1))
                    run(m_prob_t[:, 2 * hp:2 * hp + 2, :, qt * P:qt * P + P].rearrange("p h k q -> p (h k) q"),
                        bank[6 + u % 2][:, 0:512].rearrange("p (a q) -> p a q", a=4), done="m_prob_t_out")
                act.wait_ge(*signal("ms_less_max").at(1))
                run(m_rows.rearrange("p b m -> p (b m)"), m_rows.rearrange("p b m -> p (b m)"), ACT.Exp,
                    "ms_exp_ready", scale=MEM_SCALE)
                for k in range(KD):
                    act.wait_ge(*signal("mo_ready").at(k + 1))
                    run(o[:, k, 0:SEQ], bank[k % 2][:, 0:SEQ], done="mo_out")
                for n in range(4):
                    act.wait_ge(*signal("m_pt_ready").at(n + 1))
                    run(m_pt[:, 2 * n:2 * n + 2, :, :].rearrange("p b m h -> p (b m) h"),
                        bank[2 + n][:, 0:512].rearrange("p (a h x) -> p a h x", a=4, h=MH)[:, :, :, 0], done="m_pt_out")
                for n in range(4):
                    act.wait_ge(*signal("mem_v_used").at(2 * n + 2))
                    run(rows(n), bank[6 + n % 2][:, 0:512], done="ms_outputs")
                for n in range(4):
                    act.wait_ge(*signal("mo_turned").at(n + 1))
                    for b in range(2):
                        run(o[:, :, SEQ + 2 * n + b].rearrange("p (h t) -> p t h", t=2),
                            bank[2 + n][:, 256 * b:256 * b + 256].rearrange("p (t h x) -> p t h x", t=2, h=MH)[:, :, :, 0],
                            done="mo_out" if b else None)

            where["phase"] = "before"
            act.wait_ge(*signal("inputs_loaded").at(3))
            act.wait_ge(*signal("ones_ready").at(1))
            run(spare[:], ones[:, 0:1])
            for name in 'silu_ready0 silu_ready1'.split():
                signal(name).grant(act)
            where["phase"] = "layer"
            with act.Fori(0, DEPTH) as layer:
                where["layer"] = layer
                root_of_norm()
                ffn(0)
                root_of_norm()
                mixing()
                rwkv()
                cross()
                root_of_norm()
                ffn(1)
            where["phase"] = "after"
            root_of_norm()

        @block.vector
        def _(dve):
            chain = Chain(dve, signal("dve_step"))

            def out_of(done):
                return signal(done) if done else None

            def tt(out, a, b, op, done=None):
                chain(nc.vector.tensor_tensor(out, a, b, op), out_of(done))

            def ts(out, a, s1, op0, s2=None, op1=None, done=None):
                if op1 is None:
                    chain(nc.vector.tensor_scalar(out, a, s1, None, op0), out_of(done))
                else:
                    chain(nc.vector.tensor_scalar(out, a, s1, s2, op0, op1), out_of(done))

            def stt(out, a, s, b, op0, op1, done=None):
                chain(nc.vector.scalar_tensor_tensor(out=out, in0=a, scalar=s, in1=b, op0=op0, op1=op1), out_of(done))

            def copy(out, a, done=None):
                chain(nc.vector.tensor_copy(out, a), out_of(done))

            def largest(out, a, done=None):
                chain(nc.vector.tensor_reduce(out, a, AX.X, ALU.max), out_of(done))

            def total(out, a, done=None):
                chain(nc.vector.tensor_reduce(out, a, AX.X, ALU.add), out_of(done))

            def clear(out, done=None):
                chain(nc.vector.memset(out, 0.0), out_of(done))

            def over(ap, *shape):
                return ap.rearrange("p (o n) -> p o n", o=1).broadcast_to(list(shape))

            def last_dim(ap, *shape):
                return ap.rearrange("p (n o) -> p n o", o=1).broadcast_to(list(shape))

            def flat(ap):
                return ap.rearrange("p a b -> p (a b)")

            def root_of_inverse(ap):
                k = signal("inverse_ready").count[where["phase"]] + 1
                chain(nc.vector.reciprocal(ap, ap), signal("inverse_ready"))
                dve.wait_ge(*signal("root_ready").at(k))

            def inverse_rms(out, sums, n, eps):
                ts(out, sums, 1.0 / n, ALU.mult, eps, ALU.add)
                root_of_inverse(out)

            def norm(n, gain, src, dst, done, width=NT, into=6, halves=True):
                dve.wait_ge(*signal("sumsq_ready").at(n))
                ts(rstd[:, 0:width], bank[into][:, 0:width], 1.0 / D, ALU.mult, RMS_EPS, ALU.add)
                root_of_inverse(rstd[:, 0:width])
                for k in range(KD):
                    stt(dst[:, k, 0:width], src[:, k, 0:width], gain(k), rstd[:, 0:width], ALU.mult, ALU.mult,
                        done if k == KD - 1 or k == KD // 2 - 1 and halves else None)

            def add_square(src, into, part):
                n = src.shape[-1]
                tt(sq[:, part, 0:n], src, src, ALU.mult)
                tt(into[:, 0:n], into[:, 0:n], sq[:, part, 0:n], ALU.add, "squares_added")

            def ffn(f):
                wait_apart(dve, signal("h_ready").at(6 * f + 2))
                with dve.Fori(0, KF // 2) as i:
                    for u in range(2):
                        at = f * (KF // 2) + i
                        dve.wait_ge(*signal(f"silu_ready{u}").at(at + 1))
                        dve.wait_ge(*signal(f"gu_used{u}").at(at + 1))
                        signal(f"hidden_ready{u}").by(
                            nc.vector.tensor_tensor(hidden[:, 2 * i + u, :], silu[:, u, :], bank[2 + u][:, 0:NT],
                                                    ALU.mult), KF // 2)
                clear(squares)
                wait_apart(dve, signal("h_ready").at(6 * f + 2))
                with dve.Fori(0, KD // 2) as i:
                    for u in range(2):
                        at = f * (KD // 2) + i
                        dve.wait_ge(*signal(f"down_used{u}").at(at + 1))
                        signal(f"ffn_added{u}").by(
                            nc.vector.scalar_tensor_tensor(out=xT[:, 2 * i + u, :], in0=bank[4 + u][:, 0:NT],
                                                           scalar=0.5, in1=xT[:, 2 * i + u, :], op0=ALU.mult,
                                                           op1=ALU.add), KD // 2)
                        dve.wait_ge(*signal(f"ffn_added{u}").at(at + 1))
                        signal(f"part_ready{u}").by(
                            nc.vector.tensor_tensor(sq[:, u, :], xT[:, 2 * i + u, :], xT[:, 2 * i + u, :],
                                                    ALU.mult), KD // 2)
                        dve.wait_ge(*signal(f"part_ready{u}").at(at + 1))
                        signal(f"part_added{u}").by(
                            nc.vector.tensor_tensor(squares, squares, sq[:, u, :], ALU.add), KD // 2)
                        dve.wait_ge(*signal(f"part_added{u}").at(at + 1))
                for u in range(2):
                    dve.wait_ge(*signal(f"ffn_added{u}").at((f + 1) * (KD // 2)))

            def mixing():
                for u in range(2):
                    clear(ptmp[:, u, 0:1])
                clear(kr_group.rearrange("p a b -> p (a b)"))
                clear(qr_group.rearrange("p a b c -> p (a b c)"))
                dve.wait_ge(*signal("mla_sum_ready").at(1))
                inverse_rms(rstd[:], bank[4][:, 0:NT], QT * P, RMS_EPS)
                for k in range(QT):
                    stt(cq[:, k, :], cq[:, k, :], v("q_norm", k), rstd[:], ALU.mult, ALU.mult,
                        "cq_ready" if k else None)
                dve.wait_ge(*signal("mla_sum_ready").at(2))
                inverse_rms(rstd[:], bank[5][:, 0:NT], CL, RMS_EPS)
                stt(ckv, ckv, v("kv_norm"), rstd[:], ALU.mult, ALU.mult, "ckv_ready")
                dve.wait_ge(*signal("rot_ready").at(1))
                tt(kr, kr_raw, c("cos"), ALU.mult)
                tt(diff, bank[6][:, 0:NT], c("sin"), ALU.mult)
                tt(kr, kr, diff, ALU.add, "kr_ready")
                for g in range(4):
                    copy(kr_group[32 * g:32 * g + 32, g, :], kr[32 * g:32 * g + 32, 0:SEQ])
                dve.wait_ge(*signal("small_loaded").at(2))
                for n, j in enumerate([12, 13] + list(range(12))):
                    dve.wait_ge(*signal("proj_out").at(5 + n))
                    src = ptmp[:, n % 2, :]
                    tt(diff[:, 0:SEQ], src[:, 0:SEQ], src[:, 1:SEQ + 1], ALU.subtract)
                    tt(diff[:, SEQ:NT], shift0[:, j, :], src[:, SEQ + 1:NT + 1], ALU.subtract)
                    stt(p[:, j, :], diff, v("mu", j), src[:, 1:NT + 1], ALU.mult, ALU.add)
                    copy(shift_out[:, j, :], src[:, SEQ:NT + 1], "shifted")
                dve.wait_ge(*signal("ckv_turned").at(1))
                copy(ckv_tok.rearrange("p a b -> p (a b)"), bank[6][:, 0:256])
                for g in range(2):
                    dve.wait_ge(*signal("rot_ready").at(g + 2))
                    tt(qr[:, g, :], qr_raw[:, g, :], c("cos"), ALU.mult)
                    tt(diff, bank[4 + g][:, 0:NT], c("sin"), ALU.mult)
                    tt(qr[:, g, :], qr[:, g, :], diff, ALU.add, "qr_ready")
                dve.wait_ge(*signal("qs_ready").at(1))
                for g in range(4):
                    rows = slice(32 * g, 32 * g + 32)
                    copy(qr_group[rows, g, :, :], bank[7][rows, 0:64].rearrange("p (h b) -> p h b", h=H),
                         "qs_out" if g == 3 else None)

                units = [(0, 0, 4), (0, 4, 4)] + [(1, h, 2) for h in range(0, H, 2)]

                def row_maxima(u):
                    qt, _, nh = units[u]
                    n = (qt + 1) * P
                    pr = prob[:, u % 2, :].rearrange("p (h k) -> p h k", h=nh)
                    ps = bank[u % 2][:, 0:512].rearrange("p (h k) -> p h k", h=nh)
                    dve.wait_ge(*signal("score_ready").at(u + 1))
                    if u >= 2:
                        dve.wait_ge(*signal("prob_t_ready").at(u - 1))
                    if qt:
                        copy(pr[:, :, 0:P], ps[:, :, 0:P])
                    tt(pr[:, :, n - P:n], ps[:, :, n - P:n], over(c("causal"), P, nh, P), ALU.add, "score_out")
                    largest(stat[:, 2 * (u % 2), 0:nh], pr)
                    ts(stat[:, 2 * (u % 2), 0:nh], stat[:, 2 * (u % 2), 0:nh], -MLA_SCALE, ALU.mult,
                       done="score_max_ready")

                row_maxima(0)
                for u in range(len(units)):
                    if u + 1 < len(units):
                        row_maxima(u + 1)
                    qt, _, nh = units[u]
                    n = (qt + 1) * P
                    pr = prob[:, u % 2, :].rearrange("p (h k) -> p h k", h=nh)
                    dve.wait_ge(*signal("exp_ready").at(u + 1))
                    total_of = stat[:, 2 * (u % 2) + 1, 0:nh]
                    chain(nc.vector.reciprocal(total_of, total_of))
                    tt(pr, pr, last_dim(total_of, P, nh, n), ALU.mult, "prob_ready")

                dve.wait_ge(*signal("snew_ready").at(1))
                copy(s_max[0:H, :, 4], bank[6][0:H, 272:280])
                for j in range(NJ):
                    ts(kk[:, j, :], kc[:, j, :], v("k_k", j), ALU.mult, done="kk_raw" if j == NJ - 1 else None)
                for m in range(4 * NS + 6):
                    if m < 4 * NS and m % 2 == 0:
                        dve.wait_ge(*signal("turned").at(m + 1))
                        if m >= 4:
                            dve.wait_ge(*signal("s_ready").at(m - 3))
                        n = m % 4
                        copy(ckv_t[:, 4 * n:4 * n + 4, :].rearrange("p a b -> p (a b)"), bank[m % 3][:, 0:512],
                             "ckv_t_dve")
                    if 0 <= m - 2 < 4 * NS:
                        b, n = (m - 2) // 4, (m - 2) % 4
                        dve.wait_ge(*signal("s_rows_out").at(m - 1))
                        largest(s_max[0:H, b, n:n + 1], s_rows[b % 2][0:H, n * 512:n * 512 + 512])
                        if n == 3:
                            largest(s_stat[0:H, 0, b:b + 1], s_max[0:H, b, :])
                            ts(s_stat[0:H, 0, b:b + 1], s_stat[0:H, 0, b:b + 1], -MLA_SCALE, ALU.mult,
                               done="s_bias_ready")
                    if m < 4 * NS and m % 4:
                        prepare_rwkv(3 * (m // 4) + m % 4 - 1)
                    if 4 * NS - 7 <= m < 4 * NS + 2:
                        step_samples(m - (4 * NS - 7))
                    if m < 6:
                        continue
                    b = (m - 6) // 4
                    if (m - 6) % 4 == 0:
                        dve.wait_ge(*signal("s_exp_ready").at(b + 1))
                        tt(s_stat[0:H, 2, b:b + 1], s_stat[0:H, 2, b:b + 1], s_stat[0:H, 1, b:b + 1], ALU.add)
                        chain(nc.vector.reciprocal(s_stat[0:H, 2, b:b + 1], s_stat[0:H, 2, b:b + 1]))
                    if (m - 6) % 4 == 2:
                        dve.wait_ge(*signal("pv_ready").at(b + 1))
                        if b >= 2:
                            dve.wait_ge(*signal("o_turned").at(b - 1))
                        ts(s_o[0:H, b % 2, :], bank[6][0:H, P:2 * P], s_stat[0:H, 1, b:b + 1], ALU.mult)
                        tt(s_o[0:H, b % 2, :], s_o[0:H, b % 2, :], bank[6][0:H, 0:P], ALU.add)
                        ts(s_o[0:H, b % 2, :], s_o[0:H, b % 2, :], s_stat[0:H, 2, b:b + 1], ALU.mult, done="o_rows")
                    if (m - 6) % 4 == 3:
                        dve.wait_ge(*signal("o_turned").at(b + 1))
                        copy(olat[:, :, SEQ + b], bank[6][:, 256:256 + H], "sample_out")

            rr, kc, vv = p[:, 0:NJ, :], p[:, NJ:2 * NJ, :], p[:, 2 * NJ:3 * NJ, :]

            def prepare_rwkv(s):
                if s == 9:
                    dve.wait_ge(*signal("decay_ready").at(1))
                    ts(flat(logw), flat(w1), -DECAY_C, ALU.mult, done="logw_ready")
                if s in (10, 11):
                    for j in range(2 * s - 20, 2 * s - 18):
                        chain(nc.vector.tensor_tensor_scan(cum[:, j, :], c("keep"), logw[:, j, 0:SEQ], 0.0,
                                                           ALU.mult, ALU.add))
                if 8 <= s < 12:
                    dve.wait_ge(*signal("kk_norm").at(s - 7))
                    ts(w2[:, s - 8, :], bank[7][:, 0:NT], 1e-24, ALU.max, done="kk_norm_out")
                if s == 11:
                    chain(nc.vector.reciprocal(flat(w2), flat(w2)), signal("inverse_ready"))
                if s == 12:
                    dve.wait_ge(*signal("root_ready").at(signal("inverse_ready").count["layer"]))
                    tt(flat(kk), flat(kk), flat(w2), ALU.mult)
                    dve.wait_ge(*signal("iclr_ready").at(1))
                    for j in range(NJ):
                        ts(w1[:, j, :], iclr[:, j, :], -1.0, ALU.add, v("k_a", j), ALU.mult)
                if s == 13:
                    stt(flat(kc), flat(w1), 1.0, flat(kc), ALU.add, ALU.mult)
                    tt(flat(iclr), flat(iclr), flat(kk), ALU.mult)
                if s == 14:
                    for n, src in ((2, kc), (3, kk), (4, iclr), (5, vv)):
                        copy(sv[:, :, n, :], src[:, :, SEQ:NT])
                    dve.wait_ge(*signal("sv_decay").at(1))
                    copy(sv[:, :, 0, :], rr[:, :, SEQ:NT], "sv_ready")

            def step_samples(s):
                full = [P, 32, HD]

                def by_key(n):
                    return over(svb[:, n, :], *full)

                if s == 0:
                    dve.wait_ge(*signal("svb_loaded").at(7))
                    dve.wait_ge(*signal("state_loaded").at(1))
                    tt(St, S, by_key(3), ALU.mult)
                if s == 1:
                    total(skk, St)
                if s == 2:
                    tt(S, S, by_key(1), ALU.mult)
                if s == 3:
                    tt(St, last_dim(skk, *full), by_key(4), ALU.mult)
                if s == 4:
                    tt(S, S, St, ALU.subtract)
                if s == 5:
                    tt(St, last_dim(svv, *full), by_key(2), ALU.mult)
                if s == 6:
                    tt(S, S, St, ALU.add, "state_ready")
                if s == 7:
                    tt(St, S, by_key(0), ALU.mult)
                if s == 8:
                    total(so, St, "so_ready")

            def rwkv():
                dve.wait_ge(*signal("omla_out").at(NJ))
                dve.wait_ge(*signal("stored").at(3))
                dve.wait_ge(*signal("so_turned").at(1))
                copy(oT[:, :, SEQ:NT], bank[5][:, 0:NJ * NS].rearrange("p (a b) -> p a b", a=NJ), "so_out")
                clear(Z[:, 0, :], "z_cleared")

                def operands(T, part):
                    cols = slice(T * P, T * P + P)
                    if part == 0:
                        tt(dex[T], cum[:, :, cols], logw[:, :, cols], ALU.subtract, "decays")
                    if part == 1:
                        dve.wait_ge(*signal("decays_ready").at(T + 1))
                        tt(AR[T][:, :, 0, :], kk[:, :, cols], dex[T], ALU.mult)
                    if part == 2:
                        tt(AR[T][:, :, 1, :], rr[:, :, cols], din[T], ALU.mult)
                    if part == 3:
                        tt(Bt[T], iclr[:, :, cols], dinv[T], ALU.mult)
                    if part == 4:
                        tt(Kt[T], kc[:, :, cols], dinv[T], ALU.mult, "operands_ready")

                for part in range(5):
                    operands(0, part)
                for T in range(2):
                    if T:
                        dve.wait_ge(*signal("rwkv_ready").at(T))
                    for i in range(4):
                        dve.wait_ge(*signal("pairs_ready").at(10 * T + i + 1))
                        tt(MR_b[:, 2 * i:2 * i + 2, :], bank[4 + i][:, 0:512].rearrange("p (h n) -> p h n", h=2),
                           over(c("mb"), P, 2, 2 * P), ALU.mult, "mb_out")
                    for i in range(4):
                        dve.wait_ge(*signal("pairs_ready").at(10 * T + i + 5))
                        tt(MR_k[:, 2 * i:2 * i + 2, :], bank[i][:, 0:512].rearrange("p (h n) -> p h n", h=2),
                           over(c("mk"), P, 2, 2 * P), ALU.mult, "mk_out")
                    four = [P, 4, P]
                    for g in range(2):
                        hs = slice(4 * g, 4 * g + 4)
                        dve.wait_ge(*signal("pairs_ready").at(10 * T + g + 9))
                        tt(X[:, hs, :], bank[4 + g][:, 0:512].rearrange("p (h n) -> p h n", h=4),
                           over(c("neg0"), *four), ALU.mult)
                        tt(X[:, hs, :], X[:, hs, :], over(ident, *four), ALU.add)
                        tt(XT[:, hs, :], MR_b[:, hs, 0:P], over(c("lvl")[:, 0:P], *four), ALU.mult)
                        tt(XT[:, hs, :], XT[:, hs, :], over(ident, *four), ALU.add, "x_out")
                    for n in range(1, LEVELS):
                        for g in range(2):
                            hs = slice(4 * g, 4 * g + 4)
                            dve.wait_ge(*signal("xy_ready").at(2 * (T * (LEVELS - 1) + n - 1) + g + 1))
                            if n < LEVELS - 1:
                                tt(flat(X[:, hs, :]), flat(X[:, hs, :]), bank[2 + g][:, 0:512], ALU.subtract)
                            tt(flat(XT[:, hs, :]), flat(XT[:, hs, :]), bank[4 + g][:, 0:512], ALU.subtract, "x_out")
                        if T == 0:
                            if n == 1:
                                dve.wait_ge(*signal("stored").at(4))
                            operands(1, n - 1)
                    dve.wait_ge(*signal("y0_out").at(T + 1))
                    for cc in range(2):
                        n, o0 = 2 * T + cc, CHUNK * cc
                        tt(dcm, over(c("blk"), P, NJ, P),
                           din[T][:, :, o0 + CHUNK - 1:o0 + CHUNK].broadcast_to([P, NJ, P]), ALU.mult)
                        dve.wait_ge(*signal("u_ready").at(n + 1))
                        tt(U[o0:o0 + CHUNK, :], bank[0][o0:o0 + CHUNK, 0:512], Y0[o0:o0 + CHUNK, :], ALU.add, "u_out")
                        dve.wait_ge(*signal("z_ready").at(n + 1))
                        tt(Z[:, (n + 1) % 3, :], Z[:, n % 3, :], bank[1][:, 0:512], ALU.add)
                        tt(Z[:, (n + 1) % 3, :], Z[:, (n + 1) % 3, :], flat(dcm), ALU.mult, "z_out")
                dve.wait_ge(*signal("rwkv_out").at(2))
                tt(flat(e1), flat(rr), flat(kc), ALU.mult)
                for j in range(NJ):
                    ts(e1[:, j, :], e1[:, j, :], v("r_k", j), ALU.mult, done="rkr_ready" if j == NJ - 1 else None)
                dve.wait_ge(*signal("gn_mean").at(1))
                for j in range(NJ):
                    stt(oT[:, j, :], bank[j][:, 0:NT], -1.0 / HD, oT[:, j, :], ALU.mult, ALU.add,
                        "centred" if j == NJ - 1 else None)
                dve.wait_ge(*signal("bonus_ready").at(1))
                for j in range(NJ):
                    tt(bonus[:, j, :], bank[4 + j][:, 0:NT], vv[:, j, :], ALU.mult,
                       "bonus_out" if j == NJ - 1 else None)
                dve.wait_ge(*signal("gn_var").at(1))
                for j in range(NJ):
                    ts(e2[:, j, :], bank[j][:, 0:NT], 1.0 / HD, ALU.mult, GN_EPS, ALU.add)
                root_of_inverse(flat(e2))
                dve.wait_ge(*signal("gate_out").at(1))
                for j in range(NJ):
                    stt(oT[:, j, :], oT[:, j, :], v("gn_w", j), e2[:, j, :], ALU.mult, ALU.mult)
                    stt(oT[:, j, :], oT[:, j, :], v("gn_b", j), bonus[:, j, :], ALU.add, ALU.add)
                    tt(oT[:, j, :], oT[:, j, :], gate[:, j, :], ALU.mult, "rwkv_mixed")
                clear(squares)
                for n in range(KD):
                    dve.wait_ge(*signal("mix_ready").at(n + 1))
                    tt(xT[:, n, :], xT[:, n, :], bank[4 + n % 4][:, 0:NT], ALU.add, "mix_added")
                    add_square(xT[:, n, :], squares, n % 2)

            def cross():
                dve.wait_ge(*signal("stored").at(5))
                norm(3, lambda k: v("cross", k), xT, hT, "h_ready", into=5)
                clear(mem_squares)
                dve.wait_ge(*signal("mem_loaded").at(1))
                for k in range(KD):
                    add_square(memg[:, k, :], mem_squares, k % 2)
                dve.wait_ge(*signal("stored").at(5))
                norm(4, lambda k: v("mem", k), memg, memg, "memg_ready", NM, halves=False)
                for n in range(8):
                    dve.wait_ge(*signal("v_ready").at(n + 1))
                    copy(V[:, n % 2, (n // 2) * 256:(n // 2) * 256 + 256], bank[4 + n % 2][:, 0:256], "v_out")

                def row_maxima(u):
                    ps = bank[4 + u % 2][:, 0:512].rearrange("p (h k) -> p h k", h=2)
                    dve.wait_ge(*signal("m_score_ready").at(u + 1))
                    largest(m_st[:, 2 + u, 0:2], ps)
                    ts(m_st[:, 2 + u, 0:2], m_st[:, 2 + u, 0:2], -MEM_SCALE, ALU.mult, done="m_max_ready")

                row_maxima(0)
                for u in range(4):
                    if u + 1 < 4:
                        row_maxima(u + 1)
                    pr = m_prob[:, u, :].rearrange("p (h k) -> p h k", h=2)
                    dve.wait_ge(*signal("m_exp_ready").at(u + 1))
                    total_of = m_st[:, 6, 2 * u:2 * u + 2]
                    chain(nc.vector.reciprocal(total_of, total_of))
                    tt(pr, pr, last_dim(total_of, P, 2, NM), ALU.mult, "m_prob_ready")

                dve.wait_ge(*signal("ms_rows").at(4))
                largest(m_st[:, 0, :], m_rows)
                tt(m_rows, m_rows, last_dim(m_st[:, 0, :], P, NS, NM), ALU.subtract, "ms_less_max")
                dve.wait_ge(*signal("ms_exp_ready").at(1))
                total(m_st[:, 1, :], m_rows)
                chain(nc.vector.reciprocal(m_st[:, 1, :], m_st[:, 1, :]))
                tt(m_rows, m_rows, last_dim(m_st[:, 1, :], P, NS, NM), ALU.mult, "ms_prob_ready")
                clear(squares)
                for n in range(KD):
                    dve.wait_ge(*signal("cross_ready").at(n + 1))
                    tt(xT[:, n, :], xT[:, n, :], bank[n % 4][:, 0:NT], ALU.add, "cross_added")
                    add_square(xT[:, n, :], squares, n % 2)

            where["phase"] = "before"
            chain(nc.vector.memset(ones[:], 1.0), signal("ones_ready"))
            dve.wait_ge(*signal("index_loaded").at(2))
            ts(rows_idx[:], rows_idx[:], PER, ALU.mult)
            tt(rows_idx[:], rows_idx[:], part_idx[:], ALU.add, "index_ready")
            dve.wait_ge(*signal("inputs_loaded").at(3))
            keep_register(dve)
            clear(squares)
            for k in range(KD):
                add_square(xT[:, k, :], squares, k % 2)
            for name in 'part_added0 part_added1 hidden_ready0 hidden_ready1 ffn_added0 ffn_added1 mix_added cross_added'.split():
                signal(name).grant(dve)
            where["phase"] = "layer"
            with dve.Fori(0, DEPTH) as layer:
                where["layer"] = layer
                copy(vec[:], vectors[:, bass.ds(layer * NV, NV)])
                norm(1, lambda k: v("ffn1", k), xT, hT, "h_ready")
                ffn(0)
                norm(2, lambda k: v("mix", k), xT, hT, "h_ready")
                mixing()
                ts(rows_idx[:], rows_idx[:], t["cache_ckv"].shape[1] * PER, ALU.add, done="index_ready")
                rwkv()
                cross()
                norm(5, lambda k: v("ffn2", k), xT, hT, "h_ready")
                dve.wait_ge(*signal("stored").at(7))
                ffn(1)
            use_register(dve)
            where["phase"] = "after"
            norm(1, lambda k: vectors[:, DEPTH * NV + k:DEPTH * NV + k + 1], xT, hT, "final_ready",
                 halves=False)

    return ({name: (s.count["before"], s.count["layer"]) for name, s in signals.items()}
            | {name: m.place for name, m in milestones.items()})


def lay_out_constants():
    con = np.zeros((P, NC_), np.float32)

    def put(name, a):
        at, n = CON[name]
        con[:, at:at + n] = a.reshape(P, n)

    i = np.arange(P)
    row, col = i[:, None], i[None, :]
    put("ident", np.eye(P))
    put("blk", (row // HD == col // HD).astype(np.float32))
    rot = np.where((row == col + 16) & (col % 32 < 16), -1.0, 0.0) + np.where((row == col - 16) & (col % 32 >= 16), 1.0, 0.0)
    put("rot", rot)
    put("sel", np.stack([(row == 32 * g + col % 32) for g in range(4)], 1).astype(np.float32))
    pos = np.concatenate([np.arange(SEQ), np.full(NS, PAST)]).astype(np.float32)
    inv = np.float32(10000.0) ** (-np.arange(16, dtype=np.float32) / np.float32(16))
    ang = pos[None, :] * inv[i % 16][:, None]
    put("cos", np.cos(ang))
    put("sin", np.sin(ang))
    put("causal", np.where(col <= row, 0.0, NEG))
    same = row // CHUNK == col // CHUNK
    strict, incl = same & (row < col), same & (row <= col)
    put("mk", np.stack([strict, incl], 1).astype(np.float32))
    put("mb", np.stack([strict * 1.0, incl * -1.0], 1))

    def level(s, t, n):
        return (s // (2 << n) == t // (2 << n)) & (s // (1 << n) % 2 == 0) & (t // (1 << n) % 2 == 1)

    lvl = [level(row, col, n) * (-1.0 if n == 0 else 1.0) for n in range(LEVELS)]
    put("lvl", np.stack(lvl, 1))
    put("neg0", level(col, row, 0) * -1.0)
    put("keep", np.broadcast_to(np.arange(SEQ) % CHUNK != 0, (P, SEQ)).astype(np.float32))
    return con


def kernel(**inputs):
    import concourse.bacc as bacc
    from concourse.bass_utils import run_bass_kernel_spmd

    a = {k: np.asarray(v) for k, v in inputs.items()}
    L = DEPTH

    def cols(w, n):
        _, k, m = w.shape
        return w.reshape(L, k // P, P, m // n, n).transpose(0, 3, 2, 1, 4)

    def rows(v):
        return v.reshape(L, -1, P).transpose(0, 2, 1)

    arrays = {"constants": lay_out_constants()}
    for f in ("ffn1", "ffn2"):
        arrays[f"{f}_gu"] = np.stack([cols(a[f"{f}_w_gate"], P), cols(a[f"{f}_w_up"], P)], 3)
        arrays[f"{f}_down"] = cols(a[f"{f}_w_down"], P)
    w_in = a["w_in"]
    q0 = RW * P
    w_in = np.concatenate([w_in[:, :, q0:q0 + QT * P + CL]] + [w_in[:, :, q0 + QT * P + CL:]] * 4
                          + [w_in[:, :, q0 - 2 * P:q0], w_in[:, :, :q0 - 2 * P]], 2)

    def pairs(w):
        t = cols(w, P)
        return t.reshape(L, t.shape[1] // 2, 2, P, KD, P).transpose(0, 1, 3, 2, 4, 5).reshape(L, -1, P, 2 * D)

    arrays["blocks"] = np.concatenate([pairs(w_in), pairs(a["w_out"]), pairs(a["mem_w_q"]),
                                       pairs(a["mem_w_k"]), cols(a["mem_w_v"], 2 * P).reshape(L, -1, P, 2 * D),
                                       pairs(a["mem_w_o"])], 1)
    uq = a["mla_w_uq"].reshape(L, QT, P, H, NOPE + ROPE).transpose(0, 2, 1, 3, 4)
    uk = a["mla_w_uk"].transpose(0, 2, 3, 1).reshape(L, NJ, P, CL).transpose(0, 2, 1, 3)
    arrays["small"] = np.concatenate(
        [x.reshape(L, P, -1) for x in (uq[..., :NOPE], uq[..., NOPE:], uk, a["mla_w_uv"],
                                       np.concatenate([a["rwkv_w_up"], a["rwkv_a_up"]], 1), a["rwkv_g_up"])], 2)
    vec = np.concatenate([rows(v) for v in (
        a["norm_ffn1"], a["norm_mix"], a["norm_cross"], a["norm_ffn2"], a["norm_mem"], a["shift_mu"], a["rwkv_w0"],
        a["rwkv_a0"], a["rwkv_k_k"], a["rwkv_k_a"], a["rwkv_r_k"].reshape(L, -1), a["rwkv_gn_w"], a["rwkv_gn_b"],
        a["mla_q_norm"], a["mla_kv_norm"])], 2)
    arrays["vectors"] = np.concatenate([vec[0], vec[1], a["norm_final"].reshape(KD, P).T], 1)
    x = np.concatenate([a["x_prompt"][0], a["x_sample"][:, 0]], 0)
    arrays["x"] = x.T.reshape(KD, P, NT).transpose(1, 0, 2)
    arrays["mem"] = a["mem_prompt"][0].T.reshape(KD, P, NM).transpose(1, 0, 2)
    arrays["shift0"] = a["state_shift"].reshape(L, NS, RW, P).transpose(0, 3, 2, 1)
    arrays["cache_ckv"] = a["cache_ckv"]
    arrays["cache_krope"] = a["cache_krope"]
    arrays["state_wkv"] = a["state_wkv"]
    arrays["mem_k"] = a["cache_mem_k"].reshape(L, NS, NM, KD, P).transpose(0, 1, 4, 3, 2)
    arrays["mem_v"] = a["cache_mem_v"].reshape(L, NS, 2, P, D).transpose(0, 1, 3, 2, 4)
    arrays["pages"] = np.repeat(a["page_table"].T, PER, axis=0)
    arrays["page_part"] = np.repeat((np.arange(P, dtype=np.int32) % PER)[:, None], NS, axis=1)
    arrays = {k: np.ascontiguousarray(v) for k, v in arrays.items()}
    outs = {"y": (P, KD, NT), "o_ckv": (L, P, NT), "o_krope": (L, ROPE, NT), "o_wkv": (L, P, NJ, P),
            "o_shift": (L, P, RW, NS + 1), "o_mem_k": (L, P, KD, NM), "o_mem_v": (L, P, 2, D),
            "o_wkv_s": (L, P, 32 * HD)}

    totals = {}
    for _ in range(2):
        nc = bacc.Bacc("TRN2", target_bir_lowering=False, num_devices=1)
        t = {k: nc.dram_tensor(f"in_{k}", v.shape, mybir.dt.from_np(v.dtype), kind="ExternalInput").ap()
             for k, v in arrays.items()}
        t.update({k: nc.dram_tensor(f"out_{k}", s, F32, kind="ExternalOutput").ap() for k, s in outs.items()})
        totals = build(nc, t, totals)
    r = run_bass_kernel_spmd(nc, [{f"in_{k}": x for k, x in arrays.items()}], core_ids=[0]).results[0]
    got = {k: r[f"out_{k}"] for k in outs}

    y = got["y"].transpose(2, 1, 0).reshape(NT, D)
    ckv, kr = got["o_ckv"].transpose(0, 2, 1), got["o_krope"].transpose(0, 2, 1)
    wkv = np.stack([got["o_wkv"][:, HD * (h % 2):HD * (h % 2) + HD, h // 2, HD * (h % 2):HD * (h % 2) + HD]
                    for h in range(H)], 1).transpose(0, 1, 3, 2)[:, None]
    shift = got["o_shift"].transpose(0, 3, 2, 1).reshape(L, NS + 1, RW * P)
    mem_k = got["o_mem_k"].transpose(0, 3, 2, 1).reshape(L, 1, NM, MH, MD)
    mem_v = got["o_mem_v"].transpose(0, 2, 1, 3).reshape(L, 1, NM, MH, MD)
    out = (y[None, :SEQ], y[SEQ:, None], ckv[:, None, :SEQ], kr[:, None, :SEQ], wkv, shift[:, None, 0],
           mem_k, mem_v, ckv[:, SEQ:, None], kr[:, SEQ:, None], got["o_wkv_s"].reshape(L, NS, H, HD, HD),
           shift[:, 1:])
    return tuple(np.ascontiguousarray(o) for o in out)
```
